# Optimizing a Trainium2 kernel written in Bass

```python
import jax, jax.numpy as jnp
from jax import lax
import numpy as np

D_MODEL = 1024
BATCH = 1
SEQ = 1024
DEPTH = 2
DEC_BATCH = 8
DEC_SEQ = 1
PAST_LEN = 4096
PAGE_SIZE = 128

N_EVEN = (DEPTH + 1) // 2
N_ODD = DEPTH // 2
N_MOD = 6
EPS = 1e-6
NEG = -1e30
CONV_CH = D_MODEL // 2
CONV_W = 3
HG_WIDTH = D_MODEL // 2
HG_DK = 128
HG_HEADS = HG_WIDTH // HG_DK
HG_CHUNK = 64
EVEN_SPLITS = (CONV_CH, 2 * CONV_CH, 3 * CONV_CH, 3 * CONV_CH + HG_WIDTH,
               3 * CONV_CH + 2 * HG_WIDTH, 3 * CONV_CH + 3 * HG_WIDTH)
EVEN_IN = 3 * CONV_CH + 4 * HG_WIDTH
EVEN_OUT = CONV_CH + HG_WIDTH
MLA_HEADS = 8
NOPE = 128
ROPE_D = 64
V_D = 128
Q_LORA = 384
KV_LORA = 256
ROPE_THETA = 10000.0
MLA_SCALE = (NOPE + ROPE_D) ** -0.5
Q_BLOCK = 128
D_FF = ((8 * D_MODEL // 3 + 255) // 256) * 256

kernel_name = 'hybrid_conv_hgrn2_mla_adaln_decode_step'

F32 = jnp.float32

def rmsnorm(x, g):
    xf = x.astype(F32)
    y = xf * lax.rsqrt(jnp.mean(xf * xf, axis=-1, keepdims=True) + EPS)
    return (y * g.astype(F32)).astype(x.dtype)

def adaln_mod(c, w, b):
    m = jax.nn.silu(c) @ w + b
    return [t[:, None, :] for t in jnp.split(m, N_MOD, axis=-1)]

def modulate(x, g, shift, scale):
    return rmsnorm(x, g) * (1 + scale) + shift

def rope(x, pos):
    half = ROPE_D // 2
    inv = ROPE_THETA ** (-jnp.arange(half, dtype=F32) / half)
    ang = pos.astype(F32)[:, None] * inv[None, :]
    cos = jnp.cos(ang)[None, :, None, :]
    sin = jnp.sin(ang)[None, :, None, :]
    x1 = x[..., :half].astype(F32)
    x2 = x[..., half:].astype(F32)
    return jnp.concatenate([x1 * cos - x2 * sin, x1 * sin + x2 * cos], axis=-1).astype(x.dtype)

def short_conv(u, buf, w):
    T = u.shape[1]
    p = jnp.concatenate([buf.astype(u.dtype), u], axis=1)
    y = w[0] * p[:, 0:T]
    for j in range(1, CONV_W):
        y = y + w[j] * p[:, j:j + T]
    return y, p[:, -(CONV_W - 1):]

def hgrn_gates(q_pre, f_pre, lb):
    N, T, _ = q_pre.shape
    fp = f_pre.astype(F32)
    sig = jax.nn.sigmoid(fp)
    logf = jnp.log(lb + (1 - lb) * sig)
    k = (1 - lb) * jax.nn.sigmoid(-fp)
    q = jax.nn.silu(q_pre.astype(F32)) * (HG_DK ** -0.5)
    shp = (N, T, HG_HEADS, HG_DK)
    return q.reshape(shp), k.reshape(shp), logf.reshape(shp)

def hgrn_chunked(q, k, v, logf):
    N, T, H, K = q.shape
    n = T // HG_CHUNK

    def chunks(a):
        return a.reshape(N, n, HG_CHUNK, H, a.shape[-1]).transpose(1, 0, 3, 2, 4)

    causal = jnp.tril(jnp.ones((HG_CHUNK, HG_CHUNK), bool))[:, :, None]

    def step(S, inp):
        qc, kc, vc, gc = inp
        G = jnp.cumsum(gc, axis=2)
        o = jnp.einsum('nhtk,nhkv->nhtv', qc * jnp.exp(G), S)
        decay = jnp.exp(jnp.where(causal, G[:, :, :, None] - G[:, :, None], NEG))
        A = jnp.einsum('nhtk,nhsk,nhtsk->nhts', qc, kc, decay)
        o = o + jnp.einsum('nhts,nhsv->nhtv', A, vc)
        GL = G[:, :, -1:]
        S = jnp.exp(GL[:, :, 0])[..., None] * S + jnp.einsum('nhsk,nhsv->nhkv', kc * jnp.exp(GL - G), vc)
        return S, o

    S0 = jnp.zeros((N, H, K, v.shape[-1]), F32)
    S, o = lax.scan(step, S0, (chunks(q), chunks(k), chunks(v), chunks(logf)))
    o = o.transpose(1, 0, 3, 2, 4).reshape(N, T, H, v.shape[-1])
    return o, S

def hgrn_recurrent(q, k, v, logf, S0):
    def step(S, inp):
        qt, kt, vt, gt = inp
        S = jnp.exp(gt)[..., None] * S + kt[..., None] * vt[..., None, :]
        return S, jnp.einsum('nhk,nhkv->nhv', qt, S)

    tm = lambda a: jnp.moveaxis(a, 1, 0)
    S, o = lax.scan(step, S0.astype(F32), (tm(q), tm(k), tm(v), tm(logf)))
    return jnp.moveaxis(o, 0, 1), S

def even_mixer(h, conv_buf, S0, w_in, conv_w, lb, gnorm, w_out):
    N, T, _ = h.shape
    z = h @ w_in
    bg, cg, xv, qp, fp, ip, gp = jnp.split(z, EVEN_SPLITS, axis=-1)
    conv_y, new_buf = short_conv(cg * xv, conv_buf, conv_w)
    a_out = bg * conv_y
    q, k, logf = hgrn_gates(qp, fp, lb)
    v = ip.astype(F32).reshape(N, T, HG_HEADS, HG_DK)
    if S0 is None:
        o, S = hgrn_chunked(q, k, v, logf)
    else:
        o, S = hgrn_recurrent(q, k, v, logf, S0)
    o = rmsnorm(o, gnorm) * jax.nn.silu(gp.astype(F32).reshape(N, T, HG_HEADS, HG_DK))
    b_out = o.reshape(N, T, HG_WIDTH).astype(h.dtype)
    y = jnp.concatenate([a_out, b_out], axis=-1) @ w_out
    return y, new_buf, S

def mla_project(h, pos, w_dqkv, q_norm, w_uq, kv_norm, w_uk):
    N, T, _ = h.shape
    d = h @ w_dqkv
    cq = rmsnorm(d[..., :Q_LORA], q_norm)
    ckv = rmsnorm(d[..., Q_LORA:Q_LORA + KV_LORA], kv_norm)
    kr = rope(d[..., Q_LORA + KV_LORA:][:, :, None], pos)[:, :, 0]
    q = (cq @ w_uq).reshape(N, T, MLA_HEADS, NOPE + ROPE_D)
    q_lat = jnp.einsum('nthd,chd->nthc', q[..., :NOPE], w_uk)
    q_rope = rope(q[..., NOPE:], pos)
    return q_lat, q_rope, ckv, kr

def latent_scores(q_lat, q_rope, ckv, kr):
    s = jnp.einsum('nthc,nsc->nhts', q_lat, ckv) + jnp.einsum('nthr,nsr->nhts', q_rope, kr)
    return s.astype(F32) * MLA_SCALE

def mla_out(ctx, w_uv, w_o):
    N, T = ctx.shape[:2]
    o = jnp.einsum('nthc,chv->nthv', ctx, w_uv)
    return o.reshape(N, T, MLA_HEADS * V_D) @ w_o

def mla_prompt_attend(q_lat, q_rope, ckv, kr):
    T = q_lat.shape[1]
    outs = []
    for i in range(T // Q_BLOCK):
        lo, hi = i * Q_BLOCK, (i + 1) * Q_BLOCK
        s = latent_scores(q_lat[:, lo:hi], q_rope[:, lo:hi], ckv[:, :hi], kr[:, :hi])
        mask = jnp.arange(hi)[None, :] <= jnp.arange(lo, hi)[:, None]
        p = jax.nn.softmax(jnp.where(mask, s, NEG), axis=-1).astype(ckv.dtype)
        outs.append(jnp.einsum('nhts,nsc->nthc', p, ckv[:, :hi]))
    return jnp.concatenate(outs, axis=1)

def mla_sample_attend(q_lat, q_rope, ckv_new, kr_new, ckv_past, kr_past):
    T = q_lat.shape[1]
    P = ckv_past.shape[1]
    s_past = latent_scores(q_lat, q_rope, ckv_past, kr_past)
    s_new = latent_scores(q_lat, q_rope, ckv_new, kr_new)
    s_new = jnp.where(jnp.tril(jnp.ones((T, T), bool)), s_new, NEG)
    p = jax.nn.softmax(jnp.concatenate([s_past, s_new], axis=-1), axis=-1).astype(ckv_new.dtype)
    return (jnp.einsum('nhts,nsc->nthc', p[..., :P], ckv_past)
            + jnp.einsum('nhts,nsc->nthc', p[..., P:], ckv_new))

def swiglu(h, w_gu, w_down):
    g, u = jnp.split(h @ w_gu, 2, axis=-1)
    return (jax.nn.silu(g) * u) @ w_down

def setup_inputs(seed: int = 0) -> dict:
    key = jax.random.key(seed)
    ks = iter(jax.random.split(key, 40))
    nrm = lambda shape, scale: jax.random.normal(next(ks), shape, F32) * scale
    D = D_MODEL
    n_pages = PAST_LEN // PAGE_SIZE
    n_used = DEC_BATCH * n_pages
    n_phys = n_used + (n_used + 3) // 4
    page_table = jax.random.permutation(next(ks), n_phys)[:n_used].reshape(DEC_BATCH, n_pages).astype(jnp.int32)
    return {
        'x_prompt': nrm((BATCH, SEQ, D), 1.0),
        'x_sample': nrm((DEC_BATCH, DEC_SEQ, D), 1.0),
        'c_prompt': nrm((BATCH, D), 1.0),
        'c_sample': nrm((DEC_BATCH, D), 1.0),
        'cache_conv': nrm((N_EVEN, DEC_BATCH, CONV_W - 1, CONV_CH), 1.0),
        'state_hgrn': nrm((N_EVEN, DEC_BATCH, HG_HEADS, HG_DK, HG_DK), 0.5),
        'cache_ckv': nrm((N_ODD, n_phys, PAGE_SIZE, KV_LORA), 1.0),
        'cache_krope': nrm((N_ODD, n_phys, PAGE_SIZE, ROPE_D), 1.0),
        'page_table': page_table,
        'w_ada': nrm((DEPTH, D, N_MOD * D), 0.5 * D ** -0.5),
        'b_ada': nrm((DEPTH, N_MOD * D), 0.01),
        'norm_mix': 1.0 + nrm((DEPTH, D), 0.02),
        'norm_ffn': 1.0 + nrm((DEPTH, D), 0.02),
        'w_in_even': nrm((N_EVEN, D, EVEN_IN), D ** -0.5),
        'conv_w': nrm((N_EVEN, CONV_W, CONV_CH), CONV_W ** -0.5),
        'hg_lb_logits': nrm((N_EVEN, HG_WIDTH), 0.5),
        'hg_gnorm': 1.0 + nrm((N_EVEN, HG_DK), 0.02),
        'w_out_even': nrm((N_EVEN, EVEN_OUT, D), EVEN_OUT ** -0.5),
        'w_dqkv': nrm((N_ODD, D, Q_LORA + KV_LORA + ROPE_D), D ** -0.5),
        'q_norm': 1.0 + nrm((N_ODD, Q_LORA), 0.02),
        'w_uq': nrm((N_ODD, Q_LORA, MLA_HEADS * (NOPE + ROPE_D)), Q_LORA ** -0.5),
        'kv_norm': 1.0 + nrm((N_ODD, KV_LORA), 0.02),
        'w_uk': nrm((N_ODD, KV_LORA, MLA_HEADS, NOPE), KV_LORA ** -0.5),
        'w_uv': nrm((N_ODD, KV_LORA, MLA_HEADS, V_D), KV_LORA ** -0.5),
        'w_o': nrm((N_ODD, MLA_HEADS * V_D, D), (MLA_HEADS * V_D) ** -0.5),
        'w_gu': nrm((DEPTH, D, 2 * D_FF), D ** -0.5),
        'w_down': nrm((DEPTH, D_FF, D), D_FF ** -0.5),
        'norm_final': 1.0 + nrm((D,), 0.02),
    }

def reference(x_prompt, x_sample, c_prompt, c_sample, cache_conv, state_hgrn, cache_ckv, cache_krope,
              page_table, w_ada, b_ada, norm_mix, norm_ffn, w_in_even, conv_w, hg_lb_logits, hg_gnorm,
              w_out_even, w_dqkv, q_norm, w_uq, kv_norm, w_uk, w_uv, w_o, w_gu, w_down, norm_final):
    Bp, Tp, _ = x_prompt.shape
    Bs, Ts, _ = x_sample.shape
    past_len = page_table.shape[1] * PAGE_SIZE
    pos_p = jnp.arange(Tp)
    pos_s = past_len + jnp.arange(Ts)
    lb_sm = jax.nn.softmax(hg_lb_logits.astype(F32), axis=0)
    lb_all = jnp.concatenate([jnp.zeros_like(lb_sm[:1]), jnp.cumsum(lb_sm, axis=0)[:-1]], axis=0)

    xp, xs = x_prompt, x_sample
    conv_p, hg_p, ckv_p, kr_p = [], [], [], []
    conv_s, hg_s, ckv_s, kr_s = [], [], [], []
    for l in range(DEPTH):
        j = l // 2
        mp = adaln_mod(c_prompt, w_ada[l], b_ada[l])
        ms = adaln_mod(c_sample, w_ada[l], b_ada[l])
        hp = modulate(xp, norm_mix[l], mp[0], mp[1])
        hs = modulate(xs, norm_mix[l], ms[0], ms[1])
        if l % 2 == 0:
            zero_buf = jnp.zeros((Bp, CONV_W - 1, CONV_CH), hp.dtype)
            yp, bp_, Sp = even_mixer(hp, zero_buf, None, w_in_even[j], conv_w[j], lb_all[j],
                                     hg_gnorm[j], w_out_even[j])
            ys, bs_, Ss = even_mixer(hs, cache_conv[j], state_hgrn[j], w_in_even[j], conv_w[j],
                                     lb_all[j], hg_gnorm[j], w_out_even[j])
            conv_p.append(bp_)
            hg_p.append(Sp)
            conv_s.append(bs_)
            hg_s.append(Ss)
        else:
            qlp, qrp, ckvp, krp = mla_project(hp, pos_p, w_dqkv[j], q_norm[j], w_uq[j], kv_norm[j], w_uk[j])
            yp = mla_out(mla_prompt_attend(qlp, qrp, ckvp, krp), w_uv[j], w_o[j])
            qls, qrs, ckvs, krs = mla_project(hs, pos_s, w_dqkv[j], q_norm[j], w_uq[j], kv_norm[j], w_uk[j])
            ckv_past = cache_ckv[j, page_table].reshape(Bs, past_len, KV_LORA)
            kr_past = cache_krope[j, page_table].reshape(Bs, past_len, ROPE_D)
            ys = mla_out(mla_sample_attend(qls, qrs, ckvs, krs, ckv_past, kr_past), w_uv[j], w_o[j])
            ckv_p.append(ckvp)
            kr_p.append(krp)
            ckv_s.append(ckvs)
            kr_s.append(krs)
        xp = xp + mp[2] * yp
        xs = xs + ms[2] * ys
        hp = modulate(xp, norm_ffn[l], mp[3], mp[4])
        hs = modulate(xs, norm_ffn[l], ms[3], ms[4])
        xp = xp + mp[5] * swiglu(hp, w_gu[l], w_down[l])
        xs = xs + ms[5] * swiglu(hs, w_gu[l], w_down[l])

    y_prompt = rmsnorm(xp, norm_final)
    y_sample = rmsnorm(xs, norm_final)
    return (y_prompt, y_sample, jnp.stack(conv_p), jnp.stack(hg_p), jnp.stack(ckv_p), jnp.stack(kr_p),
            jnp.stack(conv_s), jnp.stack(hg_s), jnp.stack(ckv_s), jnp.stack(kr_s))


_drawn_inputs = setup_inputs


def setup_inputs(seed=0):
    import zlib

    import numpy as np

    out = dict(_drawn_inputs(seed))
    spreads = {}
    factors = {'cache_ckv': 7.556,
     'cache_krope': 8.0,
     'b_ada': 2.752,
     'norm_ffn': 7.129,
     'hg_gnorm': 8.0,
     'q_norm': 8.0,
     'kv_norm': 8.29,
     'norm_final': 9.668}
    for name, (base, spread) in spreads.items():
        noise = np.random.default_rng([zlib.crc32(name.encode()), seed]).standard_normal(out[name].shape)
        drawn = base * np.exp(spread * noise) if base else spread * noise
        out[name] = __import__('jax').numpy.asarray(drawn.astype(out[name].dtype))
    for name, factor in factors.items():
        out[name] = (out[name] * factor).astype(out[name].dtype)
    return out
```

```python
from contextlib import ExitStack

import concourse.bass as bass
import numpy as np
from concourse import mybir

F = mybir.dt.float32
R = mybir.dt.float32r
I32 = mybir.dt.int32
ACT = mybir.ActivationFunctionType
ALU = mybir.AluOpType
AX = mybir.AxisListType
RMAX = bass.bass_isa.ReduceOp.max

P = 128
D = 1024
KT = D // P
T = 1024
NS = 8
N = T + NS
NC = 3
CW = N // NC
LASTP = CW - NS
TB = T // P
EPS = 1e-6
NEG = -1e30
HEADS = 4
CH = 64
NCH = T // CH
BL = 8
NBL = T // BL
CB = CH // BL
FF = 2816
FT = FF // P
FFN_CHUNKS = [(0, 8), (8, 7), (15, 7)]
MH = 8
ROPE = 64
HR = ROPE // 2
CT = 2
QT = 3
ORDER_HEAD = 85
ORDER_SEQ = 18
ORDER_PAIR = 51
MLA_SCALE = (P + ROPE) ** -0.5
PAGES = 32
PG = 4
PW = CT * P + ROPE

PIECES = [(d, h * NBL // 2, NBL // 2) for d in range(4) for h in range(2)] + [(d, 0, NBL) for d in range(4, BL)]

G_IN = 0
G_OUT = G_IN + 7 * HEADS
G_FFN0 = G_OUT + KT
FFN_SLOTS = 2 * FT + KT * len(FFN_CHUNKS)
G_LAT = G_FFN0 + FFN_SLOTS
G_PAIR = G_LAT + 6
PAIR_SLOTS = 6 + KT
PAIRS = MH // 2
G_FFN1 = G_PAIR + PAIRS * PAIR_SLOTS
G_END = G_FFN1 + FFN_SLOTS
Z_ORDER = [4, 3, 5, 1, 2, 0, 6]
SLOT_F, SLOT_Q, SLOT_V, SLOT_CG, SLOT_XV, SLOT_BG, SLOT_G = range(7)
READY0 = (0, 0, 2)

NORMS = [KT, KT, KT, QT, CT, KT, KT]
SQ_BASE = [NC * sum(NORMS[:i]) for i in range(len(NORMS) + 1)]
HI_MIX, HI_OUT, HI_FFN0, HI_LAT, HI_CQ, HI_CKV, HI_FFN1 = (NC * n for n in (0, KT, 2 * KT, 3 * KT, 4 * KT, 4 * KT + QT, 4 * KT + QT + CT))


def row_tiles(g):
    if g >= G_FFN1:
        return row_tiles(g - G_FFN1 + G_FFN0) if g < G_END else KT
    if g >= G_PAIR:
        u = (g - G_PAIR) % PAIR_SLOTS
        return QT if u < 3 else CT if u < 5 else 2 * CT if u == 5 else 2
    if G_FFN0 <= g < G_LAT:
        g -= G_FFN0
        for _, n in FFN_CHUNKS:
            if g < 2 * n:
                return KT
            g -= 2 * n
            if g < KT:
                return n
            g -= KT
    return KT


class InOrder:

    def __init__(self, eng, sem):
        self.eng, self.sem, self.base, self.n = eng, sem, 0, 0

    def put(self, ins):
        ins.then_inc(self.sem, 1)
        self.n += 1

    def wait(self):
        self.eng.wait_ge(self.sem, self.base + self.n if not isinstance(self.base, int) else self.base + self.n)

    def __call__(self, ins):
        self.put(ins)
        self.wait()

    def enter(self, i, per):
        self.start, self.per = self.base + self.n, per
        self.base, self.n = i * per + self.start, 0

    def leave(self, turns):
        assert self.n == self.per, (self.n, self.per)
        self.base, self.n = self.start + turns * self.per, 0


def cols(c):
    return slice(c * CW, (c + 1) * CW)


def one(ap):
    return ap.rearrange("p o n -> p (o n)")


def trunk(nc, x_prompt, x_sample, c_prompt, c_sample, cache_conv, state_hgrn, cache_ckv, cache_krope,
          page_table, w_ada, b_ada, norm_mix, norm_ffn, w_in_even, conv_w, hg_gnorm, w_out_even, w_dqkv,
          q_norm, w_uq, kv_norm, w_uk, w_uv, w_o, w_gu, w_down, norm_final, rope_cos, rope_sin,
          y_prompt, y_sample, conv_prompt, hgrn_prompt, ckv_prompt, krope_prompt,
          conv_sample, hgrn_sample, ckv_sample, krope_sample):
    ctx = ExitStack()
    with ctx:
        def sb(name, shape, dt=F):
            return ctx.enter_context(nc.sbuf_tensor(name, shape, dt))

        def sem(name):
            return ctx.enter_context(nc.semaphore(name))

        xT = sb("xT", [P, KT, N])
        hh = sb("hh", [P, KT, N], R)
        hl = sb("hl", [P, KT, N], R)
        wst = [sb(f"wst{b}", [P, KT, P]) for b in range(2)]
        whi = [sb(f"whi{b}", [P, KT, P], R) for b in range(2)]
        wlo = [sb(f"wlo{b}", [P, KT, P], R) for b in range(2)]
        ident = sb("ident", [P, P])
        ones = sb("ones", [P, P])
        vec0 = sb("vec0", [P, P])
        vec1 = sb("vec1", [P, 98])
        cconv = sb("cconv", [P, NS, 2, HEADS])
        cout = sb("cout", [P, 1 + NS, 2, HEADS])
        mod = sb("mod", [P, 2, 48, 1 + NS])
        amp = sb("amp", [P, 4, KT, 1 + NS])
        siluc = sb("siluc", [P, KT, 1 + NS])
        sq = [sb(f"sq{b}", [P, CW]) for b in range(2)]
        rt = sb("rt", [P, CW])
        rs = sb("rs", [P, CW])
        gtmp = sb("gtmp", [P, NS])
        causal = sb("causal", [P, P])
        masks = sb("masks", [P, NS])
        ARENA = 75712
        sb("arena", [P, ARENA // 4])
        at0 = nc.sbuf_base - ARENA
        used = {}

        def lay(stage, name, shape, dt=F):
            at = used.get(stage, 0)
            used[stage] = at + int(np.prod(shape[1:])) * 4 + 31 & ~31
            assert used[stage] <= ARENA, (name, used[stage], ARENA)
            return nc.alloc_sbuf_tensor_at(name, shape, dt, offset=at0 + at)

        b_adaT = vec0[:, 0:96].rearrange("p (l i) -> p l i", l=2)
        gT = vec0[:, 96:128].rearrange("p (s l k) -> p s l k", s=2, l=2)
        finT = vec1[:, 0:8]
        convT = vec1[:, 8:20].rearrange("p (w j) -> p w j", w=3)
        gnT = vec1[:, 20:21]
        qnT = vec1[:, 21:24]
        kvnT = vec1[:, 24:26]
        cT = vec1[:, 26:98].rearrange("p (n k) -> p n k", k=KT)

        xtok = lay("set", "xtok", [P, TB, D])
        adaw = [lay("set", f"adaw{b}", [P, KT, 512]) for b in range(2)]
        xstok = lay("set", "xstok", [NS, D])
        rows0 = lay("set", "rows0", [P, P])
        rows1 = lay("set", "rows1", [98, P])
        rows2 = lay("set", "rows2", [64, P])
        hf = lay("mix", "hf", [P, N])
        hk = lay("mix", "hk", [P, N])
        hq = lay("mix", "hq", [P, N])
        hv = lay("mix", "hv", [P, N])
        ug = lay("mix", "ug", [P, N + 2])
        qb = lay("mix", "qb", [P, T])
        k1 = lay("mix", "k1", [P, T])
        ki = [lay("mix", f"ki{b}", [P, T]) for b in range(2)]
        mq = lay("mix", "mq", [P, T])
        ed = [lay("mix", f"ed{b}", [P, 512]) for b in range(2)]
        am = mq[:].rearrange("p (c t) -> p c t", t=P)
        dtmp = lay("mix", "dtmp", [P, 512])
        oacc = lay("mix", "oacc", [P, N])
        vtok = lay("mix", "vtok", [P, TB, P])
        ktok = lay("mix", "ktok", [P, TB, P])
        st = lay("mix", "st", [P, NCH + 1, P])
        s0 = lay("mix", "s0", [P, NS, P])
        fb = lay("mix", "fb", [P, NBL])
        cp = lay("mix", "cp", [P, NBL])
        ftot = lay("mix", "ftot", [P, NCH])
        ahi = lay("ffn", "ahi", [P, 8, N], R)
        alo = lay("ffn", "alo", [P, 8, N], R)
        sil = [lay("ffn", f"sil{c}", [P, CW]) for c in range(NC)]
        atmp = [lay("ffn", f"atmp{c}", [P, CW]) for c in range(NC)]
        NH = 4
        used["norm"] = ARENA - NH * CW * 4 & ~31
        htmp = [lay("norm", f"htmp{b}", [P, CW]) for b in range(NH)]
        kr = lay("keep", "kr", [P, N])
        rc = lay("keep", "rc", [P, N])
        rsn = lay("keep", "rsn", [P, N])
        os32 = lay("keep", "os32", [P, MH, NS])
        ktn = lay("keep", "ktn", [P, 3, P])
        knew = lay("keep", "knew", [P, CT * P])
        cqs = lay("keep", "cqs", [P, QT, NS])
        used["dec"] = used["keep"]
        sw = [lay("keep", f"sw{c}", [P, CW]) for c in range(NC)]
        used["lat"] = used["pair"] = used["keep"]
        craw = lay("lat", "craw", [P, QT + CT, N])
        ckv32 = lay("lat", "ckv32", [P, CT, N])
        lt = [lay("lat", f"lt{b}", [P, CW]) for b in range(2)]
        ctok = [lay("lat", f"ctok{b}", [P, PW]) for b in range(2)]
        wuvw = lay("dec", "wuvw", [P, CT, MH * P])
        kts = [lay("dec", f"kts{b}", [P, 3, P]) for b in range(2)]
        wukt = lay("dec", "wukt", [P, CT * P])
        qns = lay("dec", "qns", [P, MH, NS])
        qlat = lay("dec", "qlat", [P, CT, NS, MH])
        qrs = lay("dec", "qrs", [ROPE, NS, MH])
        qsw = lay("dec", "qsw", [ROPE, MH, NS])
        mx = lay("dec", "mx", [P, MH])
        mxa = lay("dec", "mxa", [P, MH])
        den = lay("dec", "den", [P, MH])
        rden = lay("dec", "rden", [P, MH])
        ctxs = lay("dec", "ctxs", [P, CT, MH, NS])
        pse = lay("dec", "pse", [P, PAGES + 1, MH])
        pex = lay("dec", "pex", [P, PAGES + 1, MH])
        ptab = lay("dec", "ptab", [1, NS * PAGES], I32)
        used["page"] = used["dec"]
        wuqw = lay("dec", "wuqw", [P, QT, MH * (P + ROPE)])
        wukw = lay("dec", "wukw", [P, CT, MH * P])
        pages = lay("page", "pages", [P, PAGES, PW])
        qn = lay("pair", "qn", [P, 2, N])
        qr = lay("pair", "qr", [P, N])
        kn = lay("pair", "kn", [P, 2, N])
        vv = lay("pair", "vv", [P, TB, 2 * P])
        pp = [lay("pair", f"pp{b}", [P, T]) for b in range(2)]
        pt = [lay("pair", f"pt{b}", [P, TB, P]) for b in range(2)]
        amx = [lay("pair", f"amx{b}", [P, 4]) for b in range(2)]
        O0 = 5
        ytok = [lay("fin", f"ytok{b}", [P, D]) for b in range(2)]

        x_rest = nc.dram_tensor("x_rest", [P, KT, N], F).ap()
        crow = lay("fin", "crow", [72, P])
        low = [ctx.enter_context(nc.psum_tensor(f"bank{i}", [P, 512], F)) for i in range(NC)]
        w34 = ctx.enter_context(nc.psum_tensor("bank34", [P, 1024], F))
        w56 = ctx.enter_context(nc.psum_tensor("bank56", [P, 1024], F))
        b7 = ctx.enter_context(nc.psum_tensor("bank7", [P, 512], F))
        bank = [t[:] for t in low] + [w[:, 512 * j:512 * j + 512] for w in (w34, w56) for j in range(2)] + [b7[:]]
        sbank = [w34, w56]

        vecs_loaded, x_loaded, ident_ready, ones_ready = map(sem, ("vecs_loaded", "x_loaded", "ident_ready", "ones_ready"))
        vec_bank, vec_ready, xt_bank, xt_act, xt_dve = map(sem, ("vec_bank", "vec_ready", "xt_bank", "xt_act", "xt_dve"))
        siluc_ready, ada_used, ada_bank, mod_ready, amp_ready = map(
            sem, ("siluc_ready", "ada_used", "ada_bank", "mod_ready", "amp_ready"))
        ada_loaded = [sem(f"ada_loaded{b}") for b in range(2)]
        w_loaded = [sem(f"w_loaded{b}") for b in range(2)]
        w_hi, w_split = sem("w_hi"), sem("w_split")
        bank_ready = [sem(f"bank_ready{c}") for c in range(NC)]
        bank_free = [sem(f"bank_free{c}") for c in range(NC)]
        sq_ready, sq_used, ss_ready, rt_ready, rs_ready, ht_ready = map(
            sem, ("sq_ready", "sq_used", "ss_ready", "rt_ready", "rs_ready", "ht_ready"))
        hi_ready, lo_ready = sem("hi_ready"), sem("lo_ready")
        dve_order, x_order, pool_order = sem("dve_order"), sem("x_order"), sem("pool_order")
        sp_turn, pool_turn = sem("sp_turn"), sem("pool_turn")
        x_saved, x_back = sem("x_saved"), sem("x_back")
        qsig_ready, gsig_ready = sem("qsig_ready"), sem("gsig_ready")
        ki_ready, ki_used, qe_ready, e_ready = map(sem, ("ki_ready", "ki_used", "qe_ready", "e_ready"))
        a_ready, a_taken, wk_half, wk_ready, wk_free = map(sem, ("a_ready", "a_taken", "wk_half", "wk_ready", "wk_free"))
        bc_ready = [sem(f"bc_ready{b}") for b in range(2)]
        bc_free = [sem(f"bc_free{b}") for b in range(2)]
        st_ready, o_ready, o_taken, dv_ready, s_new = map(sem, ("st_ready", "o_ready", "o_taken", "dv_ready", "s_new"))
        oacc_ready, hsq_ready, hrt_ready, hrs_ready, y_ready = map(
            sem, ("oacc_ready", "hsq_ready", "hrt_ready", "hrs_ready", "y_ready"))
        s0_loaded, st_saved, so_saved = sem("s0_loaded"), sem("st_saved"), sem("so_saved")
        sil_ready, act_ready, ahi_ready, alo_ready = map(sem, ("sil_ready", "act_ready", "ahi_ready", "alo_ready"))
        rope_loaded, sw_ready, kr_ready, kr2_ready, ckv_ready = map(
            sem, ("rope_loaded", "sw_ready", "kr_ready", "kr2_ready", "ckv_ready"))
        tk_ready, tk_taken = sem("tk_ready"), sem("tk_taken")
        tk_saved = [sem(f"tk_saved{b}") for b in range(2)]
        wuq_loaded, wuk_loaded, wuv_loaded, ptab_loaded = map(sem, ("wuq_loaded", "wuk_loaded", "wuv_loaded", "ptab_loaded"))
        qs_ready, qs_sw, qs_taken, wt_ready, wt_taken, ql_ready, ql_taken = map(
            sem, ("qs_ready", "qs_sw", "qs_taken", "wt_ready", "wt_taken", "ql_ready", "ql_taken"))
        page_loaded = [sem(f"page_loaded{q}") for q in range(PAGES // PG)]
        page_used, kt_used = sem("page_used"), sem("kt_used")
        kt_bank = [sem(f"kt_bank{b}") for b in range(2)]
        kt_out = [sem(f"kt_out{b}") for b in range(2)]
        ds_ready, ds_taken, mx_ready, mxa_ready, pse_ready, pex_ready = map(
            sem, ("ds_ready", "ds_taken", "mx_ready", "mxa_ready", "pse_ready", "pex_ready"))
        den_ready, den_sum, ctx_ready, ctx_taken, os_ready, os_taken = map(
            sem, ("den_ready", "den_sum", "ctx_ready", "ctx_taken", "os_ready", "os_taken"))
        masks_ready, knew_ready, sw_used, p_used = map(sem, ("masks_ready", "knew_ready", "sw_used", "p_used"))
        vx_ready, vx_taken, sc_ready, nb_ready, p_ready, pn_ready = map(
            sem, ("vx_ready", "vx_taken", "sc_ready", "nb_ready", "p_ready", "pn_ready"))
        pt_bank = [sem(f"pt_bank{b}") for b in range(2)]
        pt_out = [sem(f"pt_out{b}") for b in range(2)]
        ao_ready, oh_ready, ol_ready = sem("ao_ready"), sem("oh_ready"), sem("ol_ready")
        f_ready = sem("f_ready")
        yt_bank = [sem(f"yt_bank{b}") for b in range(2)]
        yt_out = [sem(f"yt_out{b}") for b in range(2)]
        yt_saved = [sem(f"yt_saved{b}") for b in range(2)]
        conv_bank, conv_out = sem("conv_bank"), sem("conv_out")
        saved = sem("saved")

        block = ctx.enter_context(nc.Block())

        @block.sync
        def _(sp):
            saves = [0]

            def load(g, b, dst, src):
                sp.wait_ge(w_split, g + 1)
                sp.sem_inc(sp_turn, 1)
                sp.dma_start(dst, src).then_inc(w_loaded[b], 32)

            def setup():
                for dst, src in ((rows0[0:96, :], b_ada.rearrange("l (i p) -> (l i) p", p=P)),
                                 (rows0[96:112, :], norm_mix.rearrange("l (i p) -> (l i) p", p=P)),
                                 (rows0[112:128, :], norm_ffn.rearrange("l (i p) -> (l i) p", p=P)),
                                 (rows1[0:8, :], norm_final.rearrange("(i p) -> i p", p=P)),
                                 (rows1[8:20, :], conv_w.rearrange("o w (j p) -> (o w j) p", p=P)),
                                 (rows1[20:21, :], hg_gnorm),
                                 (rows1[21:24, :], q_norm.rearrange("o (i p) -> (o i) p", p=P)),
                                 (rows1[24:26, :], kv_norm.rearrange("o (i p) -> (o i) p", p=P)),
                                 (rows1[26:34, :], c_prompt.rearrange("o (i p) -> (o i) p", p=P)),
                                 (rows1[34:98, :], c_sample.rearrange("n (i p) -> (n i) p", p=P)),
                                 (rows2[:], cache_conv.rearrange("o n w (j p) -> (o n w j) p", p=P))):
                    sp.dma_start(dst, src).then_inc(vecs_loaded, 16)
                for i in range(TB):
                    sp.dma_start(xtok[:, i, :], x_prompt[0, i * P:(i + 1) * P, :]).then_inc(x_loaded, 16)
                sp.dma_start(xstok[:], x_sample.rearrange("n o d -> (n o) d")).then_inc(x_loaded, 16)
                for l in range(2):
                    wada = w_ada[l].rearrange("(k p) (w m) -> p k w m", p=P, m=512)
                    with nc.sync.Fori(0, 6) as i:
                        for b in range(2):
                            sp.wait_ge(ada_used, 2 * i + 12 * l + b + 1)
                            sp.dma_start(adaw[b][:], wada[:, :, bass.ds(2 * i + b, 1), :].rearrange("p k o m -> p k (o m)")
                                         ).then_inc(ada_loaded[b], 16)

            def mixer():
                sp.wait_ge(xt_act, 8)
                sp.wait_ge(xt_dve, 9)
                sp.dma_start(x_rest, xT[:]).then_inc(x_saved, 16)
                win = w_in_even[0].rearrange("(k p) (z j m) -> p k z j m", p=P, z=7, m=P)
                with nc.sync.Fori(0, HEADS // 2) as i:
                    for e in range(2):
                        h = 2 * i + e
                        for u in range(7):
                            load(14 * i + 7 * e + u + G_IN, (7 * e + u) % 2, wst[(7 * e + u) % 2][:],
                                 win[:, :, Z_ORDER[u], bass.ds(h, 1), :].rearrange("p k o m -> p k (o m)"))
                            if u == 4:
                                sp.wait_ge(so_saved, 16 * h + 16)
                                sp.dma_start(s0[:], state_hgrn[0].rearrange("n h k v -> k n h v")
                                             [:, :, bass.ds(h, 1), :].rearrange("k n o v -> k n (o v)")).then_inc(s0_loaded, 16)

            def out_proj():
                wout = w_out_even[0].rearrange("(k p) (j m) -> p k j m", p=P, m=P)
                for b in range(2):
                    load(G_OUT + b, b, wst[b][:], wout[:, :, b, :])
                sp.wait_ge(lo_ready, HI_FFN0)
                sp.dma_start(xT[:], x_rest).then_inc(x_back, 16)
                with nc.sync.Fori(1, KT // 2) as i:
                    for b in range(2):
                        load(2 * i + G_OUT + b, b, wst[b][:], wout[:, :, bass.ds(2 * i + b, 1), :].rearrange("p k o m -> p k (o m)"))

            def ffn(l, g0):
                wgu = w_gu[l].rearrange("(k p) (z f m) -> p k z f m", p=P, z=2, m=P)
                wdn = w_down[l].rearrange("(f p) (j m) -> p f j m", p=P, m=P)
                g = g0
                for f0, n in FFN_CHUNKS:
                    with nc.sync.Fori(0, n) as i:
                        for b in range(2):
                            load(2 * i + g + b, b, wst[b][:], wgu[:, :, b, bass.ds(i + f0, 1), :].rearrange("p k o m -> p k (o m)"))
                    g += 2 * n
                    with nc.sync.Fori(0, KT // 2) as i:
                        for b in range(2):
                            load(2 * i + g + b, b, wst[b][:, 0:n, :],
                                 wdn[:, f0:f0 + n, bass.ds(2 * i + b, 1), :].rearrange("p k o m -> p k (o m)"))
                    g += KT

            def latents():
                sp.wait_ge(bank_ready[NC - 1], G_LAT + READY0[NC - 1])
                sp.dma_start(rc[:], rope_cos).then_inc(rope_loaded, 16)
                sp.dma_start(rsn[:], rope_sin).then_inc(rope_loaded, 16)
                wd = w_dqkv[0].rearrange("(k p) m -> p k m", p=P)
                for u in range(6):
                    w = ROPE if u == 5 else P
                    load(G_LAT + u, u % 2, wst[u % 2][:, :, 0:w], wd[:, :, u * P:u * P + w])

            def tokens_out():
                for i in range(TB + 1):
                    b = i % 2
                    rows = P if i < TB else NS
                    sp.wait_ge(tk_taken, i + 1)
                    dst_c = ckv_prompt[0, 0, i * P:(i + 1) * P, :] if i < TB else ckv_sample[0, :, 0, :]
                    dst_r = krope_prompt[0, 0, i * P:(i + 1) * P, :] if i < TB else krope_sample[0, :, 0, :]
                    sp.dma_start(dst_c, ctok[b][0:rows, 0:CT * P]).then_inc(tk_saved[b], 16)
                    sp.dma_start(dst_r, ctok[b][0:rows, CT * P:PW]).then_inc(tk_saved[b], 16)

            def decode():
                sp.dma_start(ptab[:], page_table.rearrange("(o n) j -> o (n j)", o=1)).then_inc(ptab_loaded, 16)
                sp.wait_ge(knew_ready, 1)
                sp.wait_ge(lo_ready, HI_FFN1)
                sp.wait_ge(tk_saved[0], 32 * 5 + 32)
                sp.wait_ge(tk_saved[1], 32 * 4 + 32)
                sp.dma_start(wuqw[:], w_uq[0].rearrange("(k p) m -> p k m", p=P)).then_inc(wuq_loaded, 16)
                sp.dma_start(wukw[:], w_uk[0].rearrange("(k p) h m -> p k (h m)", p=P)).then_inc(wuk_loaded, 16)
                sp.dma_start(wuvw[:], w_uv[0].rearrange("(k p) h m -> p k (h m)", p=P)).then_inc(wuv_loaded, 16)
                sp.wait_ge(ptab_loaded, 16)
                sp.wait_ge(wt_ready, MH)
                with nc.sync.Fori(0, NS) as n:
                    for j in range(PAGES):
                        if j % PG == 0:
                            sp.wait_ge(page_used, (PAGES // PG) * n + j // PG + 1)
                        page = sp.value_load(ptab[0:1, bass.ds(n * PAGES + j, 1)], min_val=0, max_val=cache_ckv.shape[1] - 1)
                        sp.dma_start(pages[:, j, 0:CT * P], cache_ckv[0, bass.ds(page, 1)].rearrange("o p c -> p (o c)")
                                     ).then_inc(page_loaded[j // PG], 16)
                        sp.dma_start(pages[:, j, CT * P:PW], cache_krope[0, bass.ds(page, 1)].rearrange("o p c -> p (o c)")
                                     ).then_inc(page_loaded[j // PG], 16)

            def pairs():
                wq = w_uq[0].rearrange("(k p) (r e m) -> p k r e m", p=P, e=2, m=P + ROPE)
                wk = w_uk[0].rearrange("(k p) (r e) m -> p k r e m", p=P, e=2)
                wv = w_uv[0].rearrange("(k p) (r e) m -> p k r e m", p=P, e=2)
                wo = w_o[0].rearrange("(r k p) (j m) -> p r k j m", p=P, k=2, m=P)
                with nc.sync.Fori(0, PAIRS) as r:
                    g = PAIR_SLOTS * r + G_PAIR
                    for e in range(2):
                        load(g + e, e, wst[e][:, 0:QT, :], wq[:, :, bass.ds(r, 1), e, 0:P].rearrange("p k o m -> p k (o m)"))
                    sp.wait_ge(w_split, g + 2 + 1)
                    for e in range(2):
                        sp.dma_start(wst[0][:, 0:QT, e * ROPE:(e + 1) * ROPE],
                                     wq[:, :, bass.ds(r, 1), e, P:P + ROPE].rearrange("p k o m -> p k (o m)")).then_inc(w_loaded[0], 16)
                    for e in range(2):
                        load(g + 3 + e, (3 + e) % 2, wst[(3 + e) % 2][:, 0:CT, :],
                             wk[:, :, bass.ds(r, 1), e, :].rearrange("p k o m -> p k (o m)"))
                    load(g + 5, 1, wst[1][:, 0:2 * CT, :].rearrange("p (k e) m -> p k (e m)", k=CT),
                         wv[:, :, bass.ds(r, 1), :, :].rearrange("p k o e m -> p k (o e m)"))
                    with nc.sync.Fori(0, KT // 2) as i:
                        for b in range(2):
                            load(PAIR_SLOTS * r + 2 * i + G_PAIR + 6 + b, b, wst[b][:, 0:2, :],
                                 wo[:, bass.ds(r, 1), :, bass.ds(2 * i + b, 1), :].rearrange("p o k q m -> p (o k) (q m)"))

            def final():
                sp.wait_ge(conv_out, 1)
                for dst, r0, n in ((conv_prompt.rearrange("o b w (j p) -> (o b w j) p", p=P), 0, 8),
                                   (conv_sample.rearrange("o n w (j p) -> (o n w j) p", p=P), 8, 64)):
                    sp.dma_start(dst, crow[r0:r0 + n, :]).then_inc(saved, 16)
                for i in range(TB + 1):
                    b = i % 2
                    sp.wait_ge(yt_out[b], 2 * (i // 2) + 2)
                    dst = y_prompt[0, i * P:(i + 1) * P, :] if i < TB else y_sample.rearrange("n o d -> (n o) d")
                    sp.dma_start(dst, ytok[b][0:P if i < TB else NS, :]).then_inc(yt_saved[b], 16)
                sp.wait_ge(saved, 32)
                sp.wait_ge(yt_saved[0], 16 * 5 + 16)
                sp.wait_ge(yt_saved[1], 16 * 4 + 16)
                sp.wait_ge(tk_saved[0], 32 * 5 + 32)
                sp.wait_ge(tk_saved[1], 32 * 4 + 32)
                sp.wait_ge(st_saved, 16 * HEADS + 16)
                sp.wait_ge(so_saved, 16 * HEADS + 16)

            sp.sem_inc(st_saved, 16)
            sp.sem_inc(so_saved, 16)
            for b in range(2):
                sp.sem_inc(yt_saved[b], 16)
                sp.sem_inc(tk_saved[b], 32)
            phases = [setup, mixer, out_proj, lambda: ffn(0, G_FFN0), latents, tokens_out, decode, pairs,
                      lambda: ffn(1, G_FFN1), final]
            for phase in phases:
                phase()

        @block.gpsimd
        def _(pool):
            order = InOrder(pool, pool_order)

            def split_at(g0, i, u, nk, per):
                b = (g0 + u) % 2
                pool.wait_ge(w_loaded[b], 32 * ((g0 + u) // 2 + 1) + i * (16 * per))
                pool.wait_ge(bank_ready[NC - 1], i * per + g0 + u + 1)
                pool.sem_inc(pool_turn, 1)
                nc.gpsimd.tensor_copy(whi[b][:, 0:nk, :], wst[b][:, 0:nk, :]).then_inc(w_hi, 1)
                pool.wait_ge(w_hi, i * per + g0 + u + 1)
                nc.gpsimd.tensor_tensor(wlo[b][:, 0:nk, :], wst[b][:, 0:nk, :], whi[b][:, 0:nk, :].bitcast(F),
                                        ALU.subtract).then_inc(w_split, 1)

            def split(g):
                if g < G_END:
                    split_at(g, 0, 0, row_tiles(g), 0)

            def low_half(n, dst_k, c, src):
                pool.wait_ge(hi_ready, n + 1)
                nc.gpsimd.tensor_tensor(hl[:, dst_k, cols(c)], src, hh[:, dst_k, cols(c)].bitcast(F),
                                        ALU.subtract).then_inc(lo_ready, 1)

            def norm_lows(hi0):
                for c in range(NC):
                    for k in range(KT):
                        low_half(hi0 + KT * c + k, k, c, htmp[(KT * c + k) % NH][:])

            def setup():
                nc.gpsimd.memset(ones[:], 1.0).then_inc(ones_ready, 1)
                pool.wait_ge(ones_ready, 1)
                nc.gpsimd.affine_select(out=ident[:], in_=ones[:], compare_op=ALU.is_equal, fill=0.0, base=0,
                                        pattern=[[-1, P]], channel_multiplier=1).then_inc(ident_ready, 1)
                order(nc.gpsimd.memset(causal[:], 0.0))
                nc.gpsimd.affine_select(out=masks[:], in_=causal[:, 0:NS], compare_op=ALU.is_equal, fill=NEG, base=0,
                                        pattern=[[-1, NS]], channel_multiplier=1).then_inc(masks_ready, 1)
                pool.wait_ge(masks_ready, 1)
                nc.gpsimd.affine_select(out=causal[:], in_=causal[:], compare_op=ALU.is_ge, fill=NEG, base=0,
                                        pattern=[[-1, P]], channel_multiplier=1).then_inc(masks_ready, 1)
                split(0)
                split(1)
                norm_lows(HI_MIX)

            def mixer():
                with nc.gpsimd.Fori(0, HEADS // 2) as i:
                    for u in range(14):
                        split_at(G_IN + 2, i, u, KT, 14)

            def out_proj():
                for c in range(NC):
                    for k in range(KT):
                        low_half(HI_OUT + KT * c + k, k, c, xT[:, k, cols(c)])
                with nc.gpsimd.Fori(0, KT // 2) as i:
                    for u in range(2):
                        split_at(G_OUT + 2, i, u, KT, 2)

            def ffn(l, g0, hi0):
                norm_lows(hi0)
                g = g0
                for f0, n in FFN_CHUNKS:
                    def turn(i, splits):
                        splits(0)
                        for c in range(NC):
                            pool.wait_ge(ahi_ready, 3 * i + 3 * (FT * l + f0) + c + 1)
                            d = one(alo[:, bass.ds(i, 1), cols(c)])
                            nc.gpsimd.tensor_tensor(d, atmp[c][:], one(ahi[:, bass.ds(i, 1), cols(c)]).bitcast(F),
                                                    ALU.subtract).then_inc(alo_ready, 1)
                        splits(1)
                    with nc.gpsimd.Fori(0, n - 1) as i:
                        turn(i, lambda u: split_at(g + 2, i, u, KT, 2))
                    turn(n - 1, lambda u: split(g + 2 * n + u))
                    g += 2 * n
                    with nc.gpsimd.Fori(0, KT // 2 - 1) as i:
                        for u in range(2):
                            split_at(g + 2, i, u, n, 2)
                    g += KT
                    split(g)
                    split(g + 1)

            def latents():
                norm_lows(HI_LAT)
                for u in range(2, 6):
                    split(G_LAT + u)
                for c in range(NC):
                    for k in range(QT):
                        low_half(HI_CQ + QT * c + k, k, c, lt[(QT * c + k) % 2][:])
                for c in range(NC):
                    for k in range(CT):
                        low_half(HI_CKV + CT * c + k, QT + k, c, ckv32[:, k, cols(c)])

            def decode():
                with nc.gpsimd.Fori(0, NS) as n:
                    pool.wait_ge(mx_ready, n + 1)
                    pool.sem_inc(pool_turn, 1)
                    nc.gpsimd.partition_all_reduce(mxa[:], mx[:], P, RMAX).then_inc(mxa_ready, 1)
                split(G_PAIR)
                split(G_PAIR + 1)

            def pairs():
                def turn(r, last):
                    for u in range(2, PAIR_SLOTS):
                        split_at(G_PAIR, r, u, row_tiles(G_PAIR + u), PAIR_SLOTS)
                    for u in range(2):
                        if last:
                            split(G_FFN1 + u)
                        else:
                            split_at(G_PAIR, r, PAIR_SLOTS + u, QT, PAIR_SLOTS)
                with nc.gpsimd.Fori(0, PAIRS - 1) as r:
                    turn(r, False)
                turn(PAIRS - 1, True)

            pool.sem_inc(w_split, 2)
            pool.sem_inc(alo_ready, NC)
            phases = [setup, mixer, out_proj, lambda: ffn(0, G_FFN0, HI_FFN0), latents, lambda: None, decode, pairs,
                      lambda: ffn(1, G_FFN1, HI_FFN1), lambda: None]
            for phase in phases:
                phase()

        @block.scalar
        def _(act):
            def high(dst, src, ready=hi_ready):
                nc.scalar.copy(dst, src).then_inc(ready, 1)

            def norm(inst, src, ready, scale, highs):
                nk = NORMS[inst]
                for c in range(NC):
                    ready(c)
                    for k in range(nk):
                        m = nk * c + k
                        act.wait_ge(sq_used, SQ_BASE[inst] + m + 1)
                        nc.scalar.activation(sq[(SQ_BASE[inst] + m) % 2][:], src(k, c), ACT.Square).then_inc(sq_ready, 1)
                    act.wait_ge(ss_ready, NC * inst + c + 1)
                    if NC * inst + c > 0:
                        act.wait_ge(rs_ready, NC * inst + c)
                    nc.scalar.activation(rt[:], bank[7][:, 0:CW], ACT.Sqrt, bias=EPS, scale=scale).then_inc(rt_ready, 1)
                    if c > 0:
                        highs(c - 1)
                highs(NC - 1)

            def model_norm(inst, ht0, ready):
                def highs(c):
                    for k in range(KT):
                        act.wait_ge(ht_ready, ht0 + KT * c + k + 1)
                        high(hh[:, k, cols(c)], htmp[(KT * c + k) % NH][:])
                norm(inst, lambda k, c: xT[:, k, cols(c)], ready, 1.0 / D, highs)

            def updated(g):
                return lambda c: act.wait_ge(bank_free[c], g + 1)

            def setup():
                for k in range(KT):
                    act.wait_ge(xt_bank, 2 * k + 2)
                    nc.scalar.copy(xT[:, k, T // 2:T], bank[(2 * k + 1) % 6]).then_inc(xt_act, 1)
                act.wait_ge(vec_ready, 2)
                nc.scalar.activation(siluc[:].rearrange("p k n -> p n k"), cT, ACT.Silu).then_inc(siluc_ready, 1)
                act.wait_ge(xt_dve, 9)
                model_norm(0, 0, lambda c: None)

            def mixer():
                act.wait_ge(x_saved, 16)
                with nc.scalar.Fori(0, HEADS // 2) as i:
                    for e in range(2):
                        h = i * 2 + e
                        def filled(u, c):
                            act.wait_ge(bank_ready[c], 14 * i + G_IN + 7 * e + u + 1 + READY0[c])
                        act.wait_ge(o_taken, h + 1)
                        for c in range(NC):
                            filled(SLOT_F, c)
                            nc.scalar.activation(hf[:, cols(c)], bank[c][:, 0:CW], ACT.Sigmoid)
                            nc.scalar.activation(hk[:, cols(c)], bank[c][:, 0:CW], ACT.Sigmoid, scale=-1.0).then_inc(bank_free[c], 1)
                        for c in range(NC):
                            filled(SLOT_Q, c)
                            nc.scalar.activation(hq[:, cols(c)], bank[c][:, 0:CW], ACT.Sigmoid).then_inc(qsig_ready, 1)
                        for c in range(NC):
                            filled(SLOT_V, c)
                            nc.scalar.copy(hv[:, cols(c)], bank[c][:, 0:CW]).then_inc(bank_free[c], 1)

                        def tokens(task, dst):
                            act.wait_ge(wk_ready, 8 * h + task + 1)
                            nc.scalar.copy(dst, bank[5].rearrange("p (b k) -> p b k", b=4)).then_inc(wk_free, 1)

                        for c in range(NC):
                            filled(SLOT_CG, c)
                            nc.scalar.copy(ug[:, 2 + c * CW:2 + (c + 1) * CW], bank[c][:, 0:CW]).then_inc(bank_free[c], 1)
                            if c < 2:
                                tokens(c, vtok[:, 4 * c:4 * c + 4, :])
                        tokens(2, ktok[:, 0:4, :])
                        tokens(3, ktok[:, 4:8, :])
                        for c in range(NC):
                            filled(SLOT_G, c)
                            nc.scalar.activation(one(xT[:, bass.ds(h + HEADS, 1), cols(c)]), bank[c][:, 0:CW],
                                                 ACT.Sigmoid).then_inc(gsig_ready, 1)
                            if c == 0:
                                act.wait_ge(s_new, h + 1)
                                act.dma_start(hgrn_sample[0].rearrange("n h k v -> k n h v")[:, :, bass.ds(h, 1), :]
                                              .rearrange("k n o v -> k n (o v)"), s0[:]).then_inc(so_saved, 16)
                        act.wait_ge(st_ready, h + 1)
                        act.dma_start(hgrn_prompt[0, 0, bass.ds(h, 1)].rearrange("o k v -> k (o v)"),
                                      st[:, NCH, :]).then_inc(st_saved, 16)
                        act.wait_ge(oacc_ready, h + 1)
                        def square(c):
                            nc.scalar.activation(sq[c % 2][:], oacc[:, cols(c)], ACT.Square).then_inc(hsq_ready, 1)
                        def root(c):
                            act.wait_ge(bc_ready[(15 + c) % 2], 9 * h + (15 + c) // 2 + 1)
                            act.wait_ge(hrs_ready, NC * h + c + 1)
                            nc.scalar.activation(rt[:], bank[6 + (15 + c) % 2][:, 0:CW], ACT.Sqrt, bias=EPS,
                                                 scale=1.0 / P).then_inc(hrt_ready, 1)
                            act.wait_ge(hrt_ready, NC * h + c + 1)
                            act.sem_inc(bc_free[(15 + c) % 2], 1)
                        square(0)
                        square(1)
                        root(0)
                        square(2)
                        root(1)
                        root(2)

            def out_proj():
                act.wait_ge(bank_ready[NC - 1], G_OUT + READY0[NC - 1])
                act.wait_ge(y_ready, HEADS)
                for c in range(NC):
                    for k in range(KT):
                        high(hh[:, k, cols(c)], xT[:, k, cols(c)])

            def ffn(l, g0, inst, ht0):
                model_norm(inst, ht0, updated(g0))
                g = g0
                for f0, n in FFN_CHUNKS:
                    act.wait_ge(bank_ready[NC - 1], g + READY0[NC - 1])
                    with nc.scalar.Fori(0, n) as i:
                        m0 = i * 3 + 3 * (FT * l + f0)
                        for c in range(NC):
                            act.wait_ge(bank_ready[c], 2 * i + g + 1 + READY0[c])
                            act.wait_ge(act_ready, m0 + c + 1)
                            nc.scalar.activation(sil[c][:], bank[c][:, 0:CW], ACT.Silu).then_inc(bank_free[c], 1)
                        for c in range(NC):
                            act.wait_ge(act_ready, m0 + c + 1 + NC)
                            high(one(ahi[:, bass.ds(i, 1), cols(c)]), atmp[c][:], ahi_ready)
                    g += 2 * n + KT

            def swap_halves(dst, src, n, done):
                for j in range(n):
                    ins = nc.scalar.copy(dst[(j ^ 1) * HR:((j ^ 1) + 1) * HR], src[j * HR:(j + 1) * HR])
                ins.then_inc(done, 1)

            def latents():
                model_norm(2, 48, updated(G_LAT))
                for u in range(QT + CT):
                    for c in range(NC):
                        act.wait_ge(bank_ready[c], G_LAT + u + 1 + READY0[c])
                        nc.scalar.copy(craw[:, u, cols(c)], bank[c][:, 0:CW]).then_inc(bank_free[c], 1)
                for c in range(NC):
                    act.wait_ge(bank_ready[c], G_LAT + 5 + 1 + READY0[c])
                    swap_halves(sw[c][0:ROPE, :], bank[c][0:ROPE, 0:CW], 2, sw_ready)
                act.wait_ge(kr_ready, NC)
                nc.scalar.copy(kr[ROPE:P, :], kr[0:ROPE, :]).then_inc(kr2_ready, 1)

                def cq_highs(c):
                    for k in range(QT):
                        act.wait_ge(ht_ready, 72 + QT * c + k + 1)
                        high(hh[:, k, cols(c)], lt[(QT * c + k) % 2][:])

                def ckv_highs(c):
                    for k in range(CT):
                        act.wait_ge(ht_ready, 81 + CT * c + k + 1)
                        high(hh[:, QT + k, cols(c)], ckv32[:, k, cols(c)])
                norm(3, lambda k, c: craw[:, k, cols(c)], lambda c: act.wait_ge(bank_free[c], G_LAT + QT + CT + 1), 1.0 / (QT * P), cq_highs)
                norm(4, lambda k, c: craw[:, QT + k, cols(c)], lambda c: None, 1.0 / (CT * P), ckv_highs)

            def tokens_out():
                for i in range(TB + 1):
                    b, rows = i % 2, P if i < TB else NS
                    act.wait_ge(tk_ready, i + 1)
                    act.wait_ge(tk_saved[b], 32 * (i // 2) + 32)
                    nc.scalar.copy(ctok[b][0:rows, :], bank[3 + b][0:rows, 0:PW]).then_inc(tk_taken, 1)

            def decode():
                act.wait_ge(qs_ready, 1)
                swap_halves(qsw[:], bank[1][0:ROPE, 0:MH * NS].rearrange("p (h n) -> p h n", h=MH), 2, qs_sw)
                with nc.scalar.Fori(0, NS) as n:
                    for j in range(0, PAGES, 2):
                        act.wait_ge(kt_bank[0], n * (PAGES // 2) + j // 2 + 1)
                        act.wait_ge(kt_used, n * PAGES + j + 1)
                        nc.scalar.copy(kts[0][:, 0:CT, :], bank[3][:, 0:CT * P].rearrange("p (k m) -> p k m", k=CT))
                        nc.scalar.copy(kts[0][0:ROPE, CT, :], bank[3][0:ROPE, CT * P:3 * P]).then_inc(kt_out[0], 1)
                    act.wait_ge(pse_ready, n + 1 + 1)
                    nc.scalar.activation(pex[:], pse[:], ACT.Exp, scale=MLA_SCALE).then_inc(pex_ready, 1)

            def pairs():
                with nc.scalar.Fori(0, PAIRS) as r:
                    g = r * PAIR_SLOTS + G_PAIR
                    def out_of(u, c, dst, src=None):
                        act.wait_ge(bank_ready[c], g + u + 1 + READY0[c])
                        nc.scalar.copy(dst, bank[c][:, 0:CW]).then_inc(bank_free[c], 1)
                    act.wait_ge(bank_free[NC - 1], g + 1)
                    for e in range(2):
                        for c in range(NC):
                            out_of(e, c, qn[:, e, cols(c)])
                    for c in range(NC):
                        act.wait_ge(bank_ready[c], g + 2 + 1 + READY0[c])
                        act.wait_ge(sw_used, r * NC + c + 1)
                        swap_halves(sw[c][:], bank[c][:, 0:CW], 4, sw_ready)
                    for e in range(2):
                        for c in range(NC):
                            out_of(3 + e, c, kn[:, e, cols(c)])
                    u0 = r * (2 * TB)

                    def probs(u):
                        w = (u // 2 + 1) * P
                        act.wait_ge(nb_ready, u0 + u + 1)
                        act.wait_ge(p_used, u0 + u + 1)
                        nc.scalar.activation(pp[u % 2][:, 0:w], sbank[u % 2][:, 0:w], ACT.Exp, bias=amx[u % 2][:, 1:2],
                                             scale=MLA_SCALE, accum_out=amx[u % 2][:, 2:3]).then_inc(p_ready, 1)

                    def output(u):
                        e, q = u % 2, u // 2
                        act.wait_ge(ao_ready, u0 + u + 1 + 2)
                        high(hh[:, O0 + e, q * P:(q + 1) * P], bank[e][:, 0:P], oh_ready)

                    probs(0)
                    for u in range(2 * TB):
                        if u + 1 < 2 * TB:
                            probs(u + 1)
                        if u // 2 >= 4:
                            act.wait_ge(pt_bank[1], r * TB + (u - 8) + 1)
                            act.wait_ge(ao_ready, u0 + u + 1)
                            w = u // 2 + 1 - 4
                            nc.scalar.copy(pt[u % 2][:, 4:4 + w, :], bank[7][:, 0:w * P].rearrange("p (b q) -> p b q", b=w)
                                           ).then_inc(pt_out[1], 1)
                        if u > 0:
                            output(u - 1)
                    output(2 * TB - 1)
                    for e in range(2):
                        high(hh[:, O0 + e, T:N], one(os32[:, bass.ds(2 * r + e, 1), :]), oh_ready)

            def final():
                model_norm_no_split()
                act.wait_ge(conv_bank, 1)
                nc.scalar.copy(crow[:], bank[0][0:72, 0:P]).then_inc(conv_out, 1)
                for i in range(TB + 1):
                    b, rows = i % 2, P if i < TB else NS
                    act.wait_ge(yt_bank[1], i + 1)
                    act.wait_ge(yt_saved[b], 16 * (i // 2) + 16)
                    nc.scalar.copy(ytok[b][0:rows, 512:D], bank[4 + 2 * b][0:rows, :]).then_inc(yt_out[b], 1)

            def model_norm_no_split():
                norm(6, lambda k, c: xT[:, k, cols(c)], updated(G_END), 1.0 / D, lambda c: None)

            act.sem_inc(bank_free[0], 1)
            act.sem_inc(bank_free[1], 1)
            act.sem_inc(bank_free[2], 1)
            act.sem_inc(wk_free, 1)
            act.sem_inc(p_ready, 2)
            act.sem_inc(pt_out[1], 1)
            phases = [setup, mixer, out_proj, lambda: ffn(0, G_FFN0, 1, 24), latents, tokens_out, decode, pairs,
                      lambda: ffn(1, G_FFN1, 5, 87), final]
            for phase in phases:
                phase()

        @block.vector
        def _(dve):
            v = nc.vector
            order = InOrder(dve, dve_order)

            def inverse_root(ready, n, done):
                dve.wait_ge(ready, n)
                v.reciprocal(rs[:], rt[:]).then_inc(done, 1)

            def model_norm(inst, ht0, hi0, which):
                l, s = divmod(which, 2)
                a, shift = amp[:, which], mod[:, l, 24 * s:24 * s + KT]
                for c in range(NC):
                    inverse_root(rt_ready, NC * inst + c + 1, rs_ready)
                    dve.wait_ge(rs_ready, NC * inst + c + 1)
                    w = CW if c < NC - 1 else LASTP
                    for k in range(KT):
                        m = KT * c + k
                        h = htmp[m % NH]
                        if m >= NH:
                            dve.wait_ge(lo_ready, hi0 + m - NH + 1)
                        order(v.tensor_tensor(h[:], xT[:, k, cols(c)], rs[:], ALU.mult))
                        if c == NC - 1:
                            order(v.tensor_tensor(h[:, w:CW], h[:, w:CW], a[:, k, 1:1 + NS], ALU.mult))
                            order.put(v.tensor_tensor(h[:, w:CW], h[:, w:CW], shift[:, k, 1:1 + NS], ALU.add))
                        v.tensor_scalar(h[:, 0:w], h[:, 0:w], a[:, k, 0:1], shift[:, k, 0:1], ALU.mult, ALU.add
                                        ).then_inc(ht_ready, 1)

            def add_to_x(c, m, gate, src, turn, order=order):
                w = CW if c < NC - 1 else LASTP
                if c == NC - 1:
                    order(v.tensor_tensor(gtmp[:], src[:, w:CW], one(gate[:, bass.ds(m, 1), 1:1 + NS]), ALU.mult))
                xc = one(xT[:, bass.ds(m, 1), c * CW:c * CW + w])
                ins = v.scalar_tensor_tensor(xc, src[:, 0:w], one(gate[:, bass.ds(m, 1), 0:1]), xc, ALU.mult, ALU.add)
                if c == NC - 1:
                    order.put(ins)
                    xs = one(xT[:, bass.ds(m, 1), T:N])
                    ins = v.tensor_tensor(xs, xs, gtmp[:], ALU.add)
                    ins.then_inc(bank_free[c], 1)
                    dve.wait_ge(bank_free[c], turn + 1)
                else:
                    ins.then_inc(bank_free[c], 1)

            def setup():
                for n, dst, src in ((0, vec0[:], bank[6][:, 0:P]), (1, vec1[:], bank[6][:, P:P + 98]),
                                    (2, cconv[:], bank[6][:, 256:320].rearrange("p (n w j) -> p n w j", n=NS, w=2))):
                    dve.wait_ge(vec_bank, n + 1)
                    v.tensor_copy(dst, src).then_inc(vec_ready, 1)
                for k in range(KT):
                    dve.wait_ge(xt_bank, 2 * k + 1)
                    v.tensor_copy(xT[:, k, 0:T // 2], bank[(2 * k) % 6]).then_inc(xt_dve, 1)
                dve.wait_ge(xt_bank, 2 * KT + 1)
                v.tensor_copy(xT[:, :, T:N], bank[7][:, 0:KT * NS].rearrange("p (k n) -> p k n", k=KT)).then_inc(xt_dve, 1)
                for l in range(2):
                    dve.wait_ge(ada_bank, l + 1)
                    order(v.tensor_tensor(mod[:, l], bank[6 + l][:, 0:48 * 9].rearrange("p (i n) -> p i n", n=9),
                                          b_adaT[:, l, :].unsqueeze(2).to_broadcast([P, 48, 9]), ALU.add))
                    for s in range(2):
                        ins = v.scalar_tensor_tensor(amp[:, 2 * l + s], mod[:, l, 24 * s + KT:24 * s + 2 * KT], 1.0,
                                                     gT[:, s, l, :].unsqueeze(2).to_broadcast([P, KT, 9]), ALU.add, ALU.mult)
                        if s == 1:
                            ins.then_inc(amp_ready, 1)
                        else:
                            order.put(ins)
                dve.wait_ge(amp_ready, 2)
                model_norm(0, 0, HI_MIX, 0)

            def mixer():
                dve.wait_ge(x_saved, 16)
                order.put(v.memset(ug[:, 0:2], 0.0))
                order.put(v.tensor_copy(cout[:, 1:1 + NS, 0, :], cconv[:, :, 1, :]))
                with nc.vector.Fori(0, HEADS // 2) as i:
                    order.enter(i, 2 * ORDER_HEAD)
                    for e in range(2):
                        head(i, e)
                    order.leave(HEADS // 2)

            def blocks(t, first=0, n=NBL):
                return t[:, first * BL:(first + n) * BL].rearrange("p (b t) -> p b t", t=BL)

            def head(i, e):
                h = i * 2 + e
                n0 = order.n
                def filled(u, c):
                    dve.wait_ge(bank_ready[c], 14 * i + G_IN + 7 * e + u + 1 + READY0[c])
                def evacuated(u, c):
                    dve.wait_ge(bank_free[c], 14 * i + G_IN + 7 * e + u + 1 + 1)
                yc, yo = xT[:, bass.ds(h, 1), :], xT[:, bass.ds(h + HEADS, 1), :]

                order.put(v.memset(ki[0][:], 0.0))
                order(v.memset(ki[1][:], 0.0))
                for c in range(NC):
                    evacuated(SLOT_F, c)
                fv, kv, qv, vvw = (blocks(t) for t in (hf, hk, hq, hv))
                pf, kb = blocks(qb), blocks(k1)
                order(v.tensor_copy(pf[:, :, 0], fv[:, :, 0]))
                order(v.memset(kb[:, :, BL - 1], 1.0))
                for t in range(1, BL):
                    order.put(v.tensor_tensor(pf[:, :, t], pf[:, :, t - 1], fv[:, :, t], ALU.mult))
                    order(v.tensor_tensor(kb[:, :, BL - 1 - t], kb[:, :, BL - t], fv[:, :, BL - t], ALU.mult))
                order(v.tensor_copy(fb[:], pf[:, :, BL - 1]))
                fc, cc = fb[:].rearrange("p (c b) -> p c b", b=CB), cp[:].rearrange("p (c b) -> p c b", b=CB)
                order(v.memset(cc[:, :, 0], 1.0))
                for t in range(1, CB):
                    order(v.tensor_tensor(cc[:, :, t], cc[:, :, t - 1], fc[:, :, t - 1], ALU.mult))
                order(v.tensor_tensor(ftot[:], cc[:, :, CB - 1], fc[:, :, CB - 1], ALU.mult))
                order(v.tensor_tensor(k1[:], k1[:], hk[:, 0:T], ALU.mult))
                for c in range(NC):
                    dve.wait_ge(qsig_ready, NC * h + c + 1)
                    v.scalar_tensor_tensor(hq[:, cols(c)], bank[c][:, 0:CW], P ** -0.5, hq[:, cols(c)], ALU.mult, ALU.mult
                                           ).then_inc(bank_free[c], 1)
                for c in range(NC):
                    evacuated(SLOT_Q, c)
                order(v.tensor_tensor(qb[:], qb[:], hq[:, 0:T], ALU.mult))

                kiv = [t[:].rearrange("p (c s) -> p c s", c=NCH) for t in ki]
                k1v = k1[:].rearrange("p (c s) -> p c s", c=NCH)

                def keys(b):
                    if b > 2:
                        dve.wait_ge(ki_used, 7 * h + b - 2)
                    if b > 1:
                        w = (b - 1) * BL
                        order.put(v.tensor_tensor(kiv[b % 2][:, :, 0:w], kiv[(b - 1) % 2][:, :, 0:w],
                                              fc[:, :, b - 1].unsqueeze(2).to_broadcast([P, NCH, w]), ALU.mult))
                    v.tensor_copy(kiv[b % 2][:, :, (b - 1) * BL:b * BL], k1v[:, :, (b - 1) * BL:b * BL]).then_inc(ki_ready, 1)
                    dve.wait_ge(ki_ready, 8 * h + b)

                def product(n):
                    d, first, nb = PIECES[n]
                    if first == 0:
                        if d == 0:
                            order(v.tensor_copy(mq[:], hq[:, 0:T]))
                        else:
                            dve.wait_ge(e_ready, 12 * h + n)
                            m = blocks(mq)
                            order(v.tensor_tensor(m[:, :, d:BL], m[:, :, d:BL], fv[:, :, 1:BL - d + 1], ALU.mult))
                    w = BL - d
                    v.tensor_tensor(ed[n % 2][:, 0:nb * w].rearrange("p (b t) -> p b t", t=w), blocks(mq, first, nb)[:, :, d:BL],
                                    blocks(hk, first, nb)[:, :, 0:w], ALU.mult).then_inc(e_ready, 1)

                def weigh(n):
                    d, first, nb = PIECES[n]
                    w = BL - d
                    dve.wait_ge(bc_ready[n % 2], 9 * h + n // 2 + 1)
                    src = bank[6 + n % 2][:, 0:nb * w].rearrange("p (b t) -> p b t", t=w)
                    o = blocks(oacc, first, nb)[:, :, d:BL]
                    val = blocks(hv, first, nb)[:, :, 0:w]
                    if d == 0:
                        v.tensor_tensor(o, src, val, ALU.mult).then_inc(bc_free[n % 2], 1)
                        dve.wait_ge(bc_free[n % 2], 9 * h + n // 2 + 2)
                    else:
                        t = dtmp[:, 0:nb * w].rearrange("p (b t) -> p b t", t=w)
                        v.tensor_tensor(t, src, val, ALU.mult).then_inc(bc_free[n % 2], 1)
                        dve.wait_ge(bc_free[n % 2], 9 * h + n // 2 + 2)
                        order(v.tensor_tensor(o, o, t, ALU.add))

                def conv_input(c):
                    filled(SLOT_XV, c)
                    u = ug[:, 2 + c * CW:2 + (c + 1) * CW]
                    v.tensor_tensor(u, bank[c][:, 0:CW], u, ALU.mult).then_inc(bank_free[c], 1)

                def gated_conv(c):
                    filled(SLOT_BG, c)
                    y = one(yc[:, :, cols(c)])
                    v.tensor_tensor(y, bank[c][:, 0:CW], y, ALU.mult).then_inc(bank_free[c], 1)

                def out_gate(c):
                    dve.wait_ge(gsig_ready, NC * h + c + 1)
                    y = one(yo[:, :, cols(c)])
                    v.tensor_tensor(y, bank[c][:, 0:CW], y, ALU.mult).then_inc(bank_free[c], 1)

                def states(n):
                    dve.wait_ge(wk_ready, 8 * h + 4 + n + 1)
                    for q in range(4):
                        c = 4 * n + q
                        src = bank[5][:, q * P:(q + 1) * P]
                        if c == NCH - 1:
                            dve.wait_ge(st_saved, 16 * h + 16)
                        if c == 0:
                            ins = v.tensor_copy(st[:, 1, :], src)
                        else:
                            ins = v.scalar_tensor_tensor(st[:, c + 1, :], st[:, c, :], ftot[:, c:c + 1], src, ALU.mult, ALU.add)
                        if q == 3:
                            ins.then_inc(wk_free, 1)
                            dve.wait_ge(wk_free, 8 * h + 4 + n + 2)
                        else:
                            order(ins)

                def sample_states(n):
                    dve.wait_ge(bc_ready[n], 9 * h + 6 + 1)
                    t = k1[:, n * 512:(n + 1) * 512].rearrange("p (n v) -> p n v", n=4)
                    v.tensor_tensor(t, bank[6 + n].rearrange("p (n v) -> p n v", n=4),
                                    hk[:, T + 4 * n:T + 4 * n + 4].unsqueeze(2).to_broadcast([P, 4, P]), ALU.mult
                                    ).then_inc(bc_free[n], 1)
                    dve.wait_ge(bc_free[n], 9 * h + 6 + 2)
                    s = s0[:, 4 * n:4 * n + 4, :]
                    order(v.tensor_tensor(s, s, t, ALU.add))

                keys(1)
                keys(2)
                product(0)
                product(1)
                for c in range(NC):
                    evacuated(SLOT_V, c)
                for n in range(0, 12, 2):
                    keys(n // 2 + 3)
                    if n >= 6:
                        conv_input((n - 6) // 2)
                    weigh(n)
                    weigh(n + 1)
                    if n + 2 < 12:
                        product(n + 2)
                        product(n + 3)
                dve.wait_ge(e_ready, 12 * h + 12)
                order(v.memset(mq[:], 0.0))
                dve.wait_ge(a_ready, h + 1)
                for half in range(2):
                    rows = slice(CH * half, CH * half + CH)
                    v.tensor_copy(am[rows, :, CH * half + BL:CH * half + CH],
                                  w34[rows, 0:512].rearrange("p (c t) -> p c t", t=CH)[:, :, BL:CH]).then_inc(a_taken, 1)
                v.tensor_tensor(blocks(qb), blocks(qb), cp[:].unsqueeze(2).to_broadcast([P, NBL, BL]), ALU.mult).then_inc(qe_ready, 1)
                dg = ki[1][:].rearrange("p (n v) -> p n v", n=NS)
                v.tensor_tensor(dg, ident[:].unsqueeze(1).to_broadcast([P, NS, P]),
                                hv[:, T:N].unsqueeze(2).to_broadcast([P, NS, P]), ALU.mult).then_inc(dv_ready, 1)
                for c in range(NC):
                    evacuated(SLOT_XV, c)
                wc = [convT[:, w, bass.ds(h, 1)] for w in range(3)]
                y = one(yc[:, :, 0:T])
                order(v.tensor_scalar(y, ug[:, 2:2 + T], wc[2], None, ALU.mult))
                order(v.scalar_tensor_tensor(y, ug[:, 1:1 + T], wc[1], y, ALU.mult, ALU.add))
                order(v.scalar_tensor_tensor(y, ug[:, 0:T], wc[0], y, ALU.mult, ALU.add))
                y = one(yc[:, :, T:N])
                order(v.tensor_scalar(y, ug[:, 2 + T:2 + N], wc[2], None, ALU.mult))
                for w in range(2):
                    order(v.scalar_tensor_tensor(y, cconv[:, :, w, bass.ds(h, 1)].rearrange("p n o -> p (n o)"), wc[w], y,
                                                 ALU.mult, ALU.add))
                order.put(v.tensor_copy(cout[:, 0, :, bass.ds(h, 1)], ug[:, T:2 + T].unsqueeze(2)))
                order.put(v.tensor_copy(cout[:, 1:1 + NS, 1, bass.ds(h, 1)], ug[:, 2 + T:2 + N].unsqueeze(2)))
                gated_conv(0)
                dve.wait_ge(s0_loaded, 16 * h + 16)
                order(v.tensor_tensor(s0[:], s0[:], hf[:, T:N].unsqueeze(2).to_broadcast([P, NS, P]), ALU.mult))
                sample_states(0)
                sample_states(1)
                dve.sem_inc(s_new, 1)
                gated_conv(1)
                states(0)
                gated_conv(2)
                states(1)
                out_gate(0)
                states(2)
                dve.wait_ge(bc_ready[0], 9 * h + 7 + 1)
                v.tensor_copy(oacc[:, T:N], bank[6][:, 0:NS]).then_inc(bc_free[0], 1)
                out_gate(1)
                states(3)
                dve.sem_inc(st_ready, 1)
                out_gate(2)
                dve.wait_ge(o_ready, h + 1)
                dve.wait_ge(bc_free[0], 9 * h + 7 + 2)
                order.put(v.tensor_tensor(oacc[:, 0:512], w34[:, 0:512], oacc[:, 0:512], ALU.add))
                v.tensor_tensor(oacc[:, 512:T], w34[:, 512:T], oacc[:, 512:T], ALU.add).then_inc(o_taken, 1)
                dve.wait_ge(o_taken, h + 2)
                dve.sem_inc(oacc_ready, 1)
                for c in range(NC):
                    inverse_root(hrt_ready, NC * h + c + 1, hrs_ready)
                    dve.wait_ge(hrs_ready, NC * h + c + 2)
                    evacuated(SLOT_G, c)
                    order(v.scalar_tensor_tensor(oacc[:, cols(c)], oacc[:, cols(c)], gnT, rs[:], ALU.mult, ALU.mult))
                    y = one(yo[:, :, cols(c)])
                    ins = v.tensor_tensor(y, y, oacc[:, cols(c)], ALU.mult)
                    if c == NC - 1:
                        ins.then_inc(y_ready, 1)
                    else:
                        order.put(ins)
                assert order.n - n0 == ORDER_HEAD, order.n - n0

            def out_proj():
                dve.wait_ge(x_back, 16)
                dve.wait_ge(st_saved, 16 * HEADS + 16)
                dve.wait_ge(so_saved, 16 * HEADS + 16)
                residual_slots(G_OUT, 2 * KT, 0)

            def residual_slots(g, gate_at, l):
                with nc.vector.Fori(0, KT // 2) as i:
                    order.enter(i, 4)
                    for b in range(2):
                        for c in range(NC):
                            s = 2 * i + b + g
                            dve.wait_ge(bank_ready[c], s + 1 + READY0[c])
                            add_to_x(c, 2 * i + b, mod[:, l, gate_at:gate_at + KT, :], bank[c], s + 1)
                    order.leave(KT // 2)

            def ffn(l, g0, inst, ht0, hi0):
                model_norm(inst, ht0, hi0, 2 * l + 1)
                g = g0
                for f0, n in FFN_CHUNKS:
                    with nc.vector.Fori(0, n) as i:
                        m0 = i * 3 + 3 * (FT * l + f0)
                        for c in range(NC):
                            dve.wait_ge(bank_free[c], 2 * i + g + 1 + 1)
                            dve.wait_ge(bank_ready[c], 2 * i + g + 2 + READY0[c])
                            dve.wait_ge(alo_ready, m0 + c + 1)
                            v.tensor_tensor(atmp[c][:], sil[c][:], bank[c][:, 0:CW], ALU.mult).then_inc(act_ready, 1)
                            dve.wait_ge(act_ready, m0 + c + 1 + NC)
                            dve.sem_inc(bank_free[c], 1)
                    g += 2 * n
                    residual_slots(g, 5 * KT, l)
                    g += KT

            def rope(dst, c, src, rows, done, turn):
                s = sw[c][0:rows, :]
                order(v.tensor_tensor(s, s, rsn[0:rows, cols(c)], ALU.mult))
                v.tensor_tensor(dst, src, rc[0:rows, cols(c)], ALU.mult).then_inc(bank_free[c], 1)
                dve.wait_ge(bank_free[c], turn + 1)
                v.tensor_tensor(dst, dst, s, ALU.add).then_inc(done, 1)

            def latents():
                model_norm(2, 48, HI_LAT, 2)
                dve.wait_ge(rope_loaded, 32)
                for c in range(NC):
                    dve.wait_ge(sw_ready, c + 1)
                    rope(kr[0:ROPE, cols(c)], c, bank[c][0:ROPE, 0:CW], ROPE, kr_ready, G_LAT + 6)
                for inst, nk, k0, g, ht0, hi0 in ((3, QT, 0, qnT, 72, HI_CQ), (4, CT, QT, kvnT, 81, HI_CKV)):
                    for c in range(NC):
                        dve.wait_ge(ht_ready, ht0 + nk * c)
                        inverse_root(rt_ready, NC * inst + c + 1, rs_ready)
                        dve.wait_ge(rs_ready, NC * inst + c + 1)
                        for k in range(nk):
                            m = nk * c + k
                            if inst == 3:
                                dst = lt[m % 2][:]
                                if m >= 2:
                                    dve.wait_ge(lo_ready, hi0 + m - 1)
                            else:
                                dst = ckv32[:, k, cols(c)]
                            ins = v.scalar_tensor_tensor(dst, craw[:, k0 + k, cols(c)], g[:, k:k + 1], rs[:], ALU.mult, ALU.mult)
                            ins.then_inc(ht_ready, 1)
                            if inst == 3 and c == NC - 1:
                                dve.wait_ge(ht_ready, ht0 + m + 1)
                                order.put(v.tensor_copy(cqs[:, k, :], dst[:, LASTP:CW]))

            def tokens_out():
                order.put(v.memset(ktn[:], 0.0))
                order(v.memset(knew[:], 0.0))
                dve.wait_ge(ht_ready, 87)
                dve.wait_ge(kr_ready, NC)
                order.put(v.tensor_copy(ktn[:, 0:CT, 0:NS], ckv32[:, :, T:N]))
                order.put(v.tensor_copy(ktn[0:ROPE, CT, 0:NS], kr[0:ROPE, T:N]))
                dve.wait_ge(tk_taken, TB + 1)
                v.tensor_copy(knew[0:NS, :], ctok[0][0:NS, 0:CT * P]).then_inc(knew_ready, 1)

            def decode():
                order.wait()
                dve.wait_ge(qs_ready, 1)
                order.put(v.tensor_copy(qns[:], bank[0][:, 0:MH * NS].rearrange("p (h n) -> p h n", h=MH)))
                dve.wait_ge(qs_sw, 1)
                q = qrs[:].rearrange("p n h -> p h n")
                order(v.tensor_scalar(qsw[:], qsw[:], rsn[0:ROPE, T:T + 1], None, ALU.mult))
                v.scalar_tensor_tensor(q, bank[1][0:ROPE, 0:MH * NS].rearrange("p (h n) -> p h n", h=MH), rc[0:ROPE, T:T + 1],
                                       qsw[:], ALU.mult, ALU.add).then_inc(qs_taken, 1)
                for h in range(MH):
                    dve.wait_ge(wt_ready, h + 1)
                    if h > 0:
                        dve.wait_ge(ql_ready, h)
                    v.tensor_copy(wukt[:], bank[3 + h % 2][:, 0:CT * P]).then_inc(wt_taken, 1)
                dve.wait_ge(ql_ready, MH)
                for ct in range(CT):
                    ins = v.tensor_copy(qlat[:, ct].rearrange("p n h -> p h n"),
                                        bank[5 + ct][:, 0:MH * NS].rearrange("p (h n) -> p h n", h=MH))
                    ins.then_inc(ql_taken, 1)
                with nc.vector.Fori(0, NS) as n:
                    order.enter(n, ORDER_SEQ)
                    for j in range(1, PAGES, 2):
                        dve.wait_ge(kt_bank[1], n * (PAGES // 2) + j // 2 + 1)
                        dve.wait_ge(kt_used, n * PAGES + j + 1)
                        order.put(v.tensor_copy(kts[1][:, 0:CT, :], bank[4][:, 0:CT * P].rearrange("p (k m) -> p k m", k=CT)))
                        v.tensor_copy(kts[1][0:ROPE, CT, :], bank[4][0:ROPE, CT * P:3 * P]).then_inc(kt_out[1], 1)
                    dve.wait_ge(ds_ready, n + 1)
                    sc = bank[5][:, 0:(PAGES + 1) * MH].rearrange("p (j h) -> p j h", h=MH)
                    order(v.tensor_scalar(sc[:, PAGES, :], sc[:, PAGES, :], masks[:, bass.ds(n, 1)], None, ALU.add))
                    v.tensor_reduce(mx[:], bank[5][:, 0:(PAGES + 1) * MH].rearrange("p (j h) -> p h j", h=MH), axis=AX.X,
                                    op=ALU.max).then_inc(mx_ready, 1)
                    dve.wait_ge(mxa_ready, n + 1)
                    v.tensor_tensor(pse[:], sc, mxa[:].unsqueeze(1).to_broadcast([P, PAGES + 1, MH]), ALU.subtract
                                    ).then_inc(pse_ready, 1)
                    dve.wait_ge(pex_ready, n + 1)
                    v.tensor_reduce(den[:], pex[:].rearrange("p j h -> p h j"), axis=AX.X, op=ALU.add).then_inc(den_ready, 1)
                    dve.wait_ge(den_sum, n + 1)
                    order(v.reciprocal(rden[:], bank[2][:, 0:MH]))
                    for ct in range(CT):
                        dve.wait_ge(ctx_ready, 2 * n + ct + 1)
                        ins = v.tensor_tensor(ctxs[:, ct, :, bass.ds(n, 1)].rearrange("p h o -> p (h o)"), bank[7 - ct][:, 0:MH],
                                              rden[:], ALU.mult)
                        ins.then_inc(ctx_taken, 1)
                    order.leave(NS)
                dve.wait_ge(os_ready, 1)
                v.tensor_copy(os32[:], bank[1][:, 0:MH * NS].rearrange("p (h n) -> p h n", h=MH)).then_inc(os_taken, 1)

            def pairs():
                with nc.vector.Fori(0, PAIRS) as r:
                    order.enter(r, ORDER_PAIR)
                    g = r * PAIR_SLOTS + G_PAIR
                    for c in range(NC):
                        dve.wait_ge(sw_ready, r * NC + NC + c + 1)
                        rope(qr[:, cols(c)], c, bank[c][:, 0:CW], P, sw_used, g + 3)
                    for c in range(NC):
                        dve.wait_ge(bank_ready[c], g + 5 + 1 + READY0[c])
                        v.tensor_copy(vv[:, 2 * c:2 * c + 2, :], bank[c].rearrange("p (b m) -> p b m", b=2)).then_inc(bank_free[c], 1)
                    dve.wait_ge(vx_ready, r + 1)
                    v.tensor_copy(vv[:, 6:8, :], bank[7].rearrange("p (b m) -> p b m", b=2)).then_inc(vx_taken, 1)
                    u0 = r * (2 * TB)

                    def maxima(u):
                        q, s = u // 2, sbank[u % 2]
                        dve.wait_ge(sc_ready, u0 + u + 1)
                        diag = s[:, q * P:(q + 1) * P]
                        order(v.tensor_tensor(diag, diag, causal[:], ALU.add))
                        order(v.reduce_max(amx[u % 2][:, 0:1], s[:, 0:(q + 1) * P], axis=AX.X))
                        v.tensor_scalar(amx[u % 2][:, 1:2], amx[u % 2][:, 0:1], -MLA_SCALE, None, ALU.mult).then_inc(nb_ready, 1)

                    def low_output(u):
                        e, q = u % 2, u // 2
                        dve.wait_ge(oh_ready, r * (2 * TB + 2) + u + 1)
                        v.tensor_tensor(hl[:, O0 + e, q * P:(q + 1) * P], bank[e][:, 0:P],
                                        hh[:, O0 + e, q * P:(q + 1) * P].bitcast(F), ALU.subtract).then_inc(ol_ready, 1)

                    maxima(0)
                    for u in range(2 * TB):
                        q = u // 2
                        dve.wait_ge(p_ready, u0 + u + 1 + 2)
                        order(v.reciprocal(amx[u % 2][:, 3:4], amx[u % 2][:, 2:3]))
                        p = pp[u % 2][:, 0:(q + 1) * P]
                        v.tensor_scalar(p, p, amx[u % 2][:, 3:4], None, ALU.mult).then_inc(pn_ready, 1)
                        if u + 1 < 2 * TB:
                            maxima(u + 1)
                        dve.wait_ge(pt_bank[0], u0 + u + 1)
                        dve.wait_ge(ao_ready, u0 + u + 1)
                        w = min(q + 1, 4)
                        v.tensor_copy(pt[u % 2][:, 0:w, :], bank[2][:, 0:w * P].rearrange("p (b q) -> p b q", b=w)
                                      ).then_inc(pt_out[0], 1)
                        if u > 0:
                            low_output(u - 1)
                    low_output(2 * TB - 1)
                    for e in range(2):
                        dve.wait_ge(oh_ready, r * (2 * TB + 2) + 2 * TB + e + 1)
                        v.tensor_tensor(hl[:, O0 + e, T:N], one(os32[:, bass.ds(2 * r + e, 1), :]),
                                        hh[:, O0 + e, T:N].bitcast(F), ALU.subtract).then_inc(ol_ready, 1)
                    with nc.vector.Fori(0, KT // 2) as i:
                        inner = InOrder(dve, x_order)
                        inner.base = (r * (KT // 2) + i) * 4
                        for b in range(2):
                            for c in range(NC):
                                s = g + 2 * i + 6 + b
                                dve.wait_ge(bank_ready[c], s + 1 + READY0[c])
                                add_to_x(c, 2 * i + b, mod[:, 1, 2 * KT:3 * KT, :], bank[c], s + 1, inner)
                    order.leave(PAIRS)

            def final():
                for c in range(NC):
                    if c > 0:
                        dve.wait_ge(f_ready, KT * c)
                    inverse_root(rt_ready, NC * 6 + c + 1, rs_ready)
                    dve.wait_ge(rs_ready, NC * 6 + c + 1)
                    for k in range(KT):
                        x = xT[:, k, cols(c)]
                        v.scalar_tensor_tensor(x, x, finT[:, k:k + 1], rs[:], ALU.mult, ALU.mult).then_inc(f_ready, 1)
                for i in range(TB + 1):
                    b, rows = i % 2, P if i < TB else NS
                    dve.wait_ge(yt_bank[0], i + 1)
                    dve.wait_ge(yt_saved[b], 16 * (i // 2) + 16)
                    v.tensor_copy(ytok[b][0:rows, 0:512], bank[3 + 2 * b][0:rows, :]).then_inc(yt_out[b], 1)

            dve.sem_inc(act_ready, NC)
            dve.sem_inc(o_taken, 1)
            dve.sem_inc(hrs_ready, 1)
            dve.sem_inc(pse_ready, 1)
            dve.sem_inc(sw_used, NC)
            dve.sem_inc(ol_ready, 2)
            for b in range(2):
                dve.sem_inc(bc_free[b], 1)
            dve.sem_inc(pt_out[0], 1)
            phases = [setup, mixer, out_proj, lambda: ffn(0, G_FFN0, 1, 24, HI_FFN0), latents, tokens_out, decode, pairs,
                      lambda: ffn(1, G_FFN1, 5, 87, HI_FFN1), final]
            for phase in phases:
                phase()

        @block.tensor
        def _(pe):
            mm = nc.tensor.matmul

            def three(out, wh_, wl_, xh_, xl_, start, stop):
                mm(out, wh_, xh_, start=start, stop=False)
                mm(out, wh_, xl_, start=False, stop=False)
                return mm(out, wl_, xh_, start=False, stop=stop)

            def slot(g, b, nk, hi, lo, ready=None, after=None, rows=P):
                pe.wait_ge(w_split, g + 1 + 2)
                for c in range(NC):
                    if ready:
                        ready(c)
                    pe.wait_ge(bank_free[c], g + 1)
                    for k in range(nk):
                        last = three(bank[c][0:rows, 0:CW], whi[b][:, k, 0:rows], wlo[b][:, k, 0:rows], hi[:, k, cols(c)],
                                     lo[:, k, cols(c)], k == 0, k == nk - 1)
                    last.then_inc(bank_ready[c], 1)
                    if after:
                        after(c)

            def sums(inst):
                nk = NORMS[inst]
                for c in range(NC):
                    if NC * inst + c > 0:
                        pe.wait_ge(rt_ready, NC * inst + c)
                    for k in range(nk):
                        m = SQ_BASE[inst] + nk * c + k
                        pe.wait_ge(sq_ready, m + 1)
                        mm(bank[7][:, 0:CW], ones[:], sq[m % 2][:], start=k == 0, stop=k == nk - 1).then_inc(sq_used, 1)
                    pe.wait_ge(sq_used, SQ_BASE[inst] + nk * (c + 1) + 2)
                    pe.sem_inc(ss_ready, 1)

            def lows_ready(hi0, nk):
                return lambda c: pe.wait_ge(lo_ready, hi0 + nk * (c + 1))

            def setup():
                pe.wait_ge(ident_ready, 1)
                pe.wait_ge(vecs_loaded, 16 * 11)
                for dst, src, n in ((bank[6][:, 0:P], rows0, P), (bank[6][:, P:P + 98], rows1, 98), (bank[6][:, 256:320], rows2, 64)):
                    ins = nc.tensor.transpose(dst, src[:], ident[0:n, 0:n])
                ins.then_inc(vec_bank, 3)
                pe.wait_ge(x_loaded, 16 * (TB + 1))
                for k in range(KT):
                    for half in range(2):
                        n = 2 * k + half
                        if n >= 6:
                            pe.wait_ge(xt_act if half else xt_dve, (n - 6) // 2 + 1)
                        for q in range(4):
                            ins = nc.tensor.transpose(bank[n % 6][:, q * P:(q + 1) * P], xtok[:, 4 * half + q, k * P:(k + 1) * P], ident[:])
                        ins.then_inc(xt_bank, 1)
                for k in range(KT):
                    ins = nc.tensor.transpose(bank[7][:, k * NS:(k + 1) * NS], xstok[:, k * P:(k + 1) * P], ident[0:NS, 0:NS])
                ins.then_inc(xt_bank, 1)
                pe.wait_ge(siluc_ready, 1)
                pe.wait_ge(vec_ready, 3)
                pe.wait_ge(xt_dve, KT + 1)
                for l in range(2):
                    with nc.tensor.Fori(0, 6) as i:
                        for b in range(2):
                            pe.wait_ge(ada_loaded[b], 16 * i + 96 * l + 16)
                            for q in range(4):
                                for k in range(KT):
                                    ins = mm(bank[6 + l][:, bass.ds(i * 72 + (4 * b + q) * 9, 9)], adaw[b][:, k, q * P:(q + 1) * P],
                                             siluc[:, k, :], start=k == 0, stop=k == KT - 1)
                            ins.then_inc(ada_used, 1)
                    pe.wait_ge(ada_used, 12 * (l + 1) + 2)
                    pe.sem_inc(ada_bank, 1)
                pe.wait_ge(amp_ready, 2)
                sums(0)

            def mixer():
                with nc.tensor.Fori(0, HEADS // 2) as i:
                    for e in range(2):
                        head(i, e)

            def head(i, e):
                h = i * 2 + e

                def attend(b):
                    pe.wait_ge(ki_ready, 8 * h + b)
                    if b == 1:
                        pe.wait_ge(o_taken, h + 1)
                    for c in range(NCH):
                        ins = mm(w34[CH * (c % 2):CH * (c % 2) + CH, (c // 2) * CH + b * BL:(c // 2) * CH + (b + 1) * BL],
                                 ki[b % 2][:, c * CH:(c + 1) * CH], qb[:, c * CH + b * BL:c * CH + (b + 1) * BL],
                                 start=True, stop=True)
                    ins.then_inc(ki_used, 1)
                    if b == CB - 1:
                        pe.wait_ge(ki_used, 7 * h + 7)
                        pe.sem_inc(a_ready, 1)

                def transposes(task, src):
                    pe.wait_ge(wk_free, 8 * h + task + 1)
                    if task == 0:
                        for c in range(NC):
                            pe.wait_ge(bank_free[c], 14 * i + G_IN + 7 * e + SLOT_V + 1 + 1)
                    if task == 2:
                        pe.wait_ge(ki_ready, 8 * h + 8)
                    for q in range(4):
                        t = (4 * (task % 2) + q) * P
                        ins = nc.tensor.transpose(bank[5][:, q * P:(q + 1) * P], src[:, t:t + P], ident[:])
                    ins.then_inc(wk_ready, 1)

                def broadcast(n):
                    d, _, nb = PIECES[n]
                    w = nb * (BL - d)
                    pe.wait_ge(bc_free[n % 2], 9 * h + n // 2 + 1)
                    pe.wait_ge(e_ready, 12 * h + n + 1)
                    mm(bank[6 + n % 2][:, 0:w], ones[:], ed[n % 2][:, 0:w], start=True, stop=True).then_inc(bc_ready[n % 2], 1)

                def sample_values(n):
                    pe.wait_ge(bc_free[n], 9 * h + 6 + 1)
                    pe.wait_ge(dv_ready, h + 1)
                    mm(bank[6 + n][:], ones[:], ki[1][:, n * 512:(n + 1) * 512], start=True, stop=True).then_inc(bc_ready[n], 1)

                def outer(n):
                    pe.wait_ge(wk_free, 8 * h + 4 + n + 1)
                    for q in (0, 2, 1, 3):
                        c = 4 * n + q
                        rows = slice(CH * (c % 2), CH * (c % 2) + CH)
                        if q == 1:
                            ins.then_inc(wk_half, 1)
                            pe.wait_ge(wk_half, 4 * h + n + 1)
                        ins = mm(bank[5][:, q * P:(q + 1) * P], ktok[rows, c // 2, :], vtok[rows, c // 2, :], start=True, stop=True)
                    ins.then_inc(wk_ready, 1)

                def sample_outputs():
                    pe.wait_ge(bc_free[0], 9 * h + 7 + 1)
                    pe.wait_ge(s_new, h + 1)
                    for n in range(NS):
                        ins = mm(bank[6][:, n:n + 1], s0[:, n, :], hq[:, T + n:T + n + 1], start=True, stop=True)
                    ins.then_inc(bc_ready[0], 1)

                def outputs():
                    pe.wait_ge(a_taken, 2 * h + 2)
                    pe.wait_ge(qe_ready, h + 1)
                    pe.wait_ge(st_ready, h + 1)
                    for c in range(NCH):
                        if c % 2 == 0:
                            mm(w34[:, c * CH:(c + 2) * CH], vtok[:, c // 2, :], am[:, c // 2, :], start=True, stop=False)
                        if c > 0:
                            ins = mm(w34[:, c * CH:(c + 1) * CH], st[:, c, :], qb[:, c * CH:(c + 1) * CH],
                                     start=False, stop=c % 2 == 1)
                    ins.then_inc(o_ready, 1)

                def head_sums(c):
                    b, n = (15 + c) % 2, 9 * h + (15 + c) // 2
                    pe.wait_ge(bc_free[b], n + 1)
                    pe.wait_ge(hsq_ready, NC * h + c + 1)
                    mm(bank[6 + b][:, 0:CW], ones[:], sq[c % 2][:], start=True, stop=True).then_inc(bc_ready[b], 1)

                steps = {(SLOT_V, 1): [lambda: attend(1)], (SLOT_V, 2): [lambda: attend(2)],
                         (SLOT_CG, 0): [lambda: attend(3), lambda: transposes(0, hv), lambda: broadcast(0), lambda: broadcast(1)],
                         (SLOT_CG, 1): [lambda: attend(4), lambda: transposes(1, hv), lambda: broadcast(2), lambda: broadcast(3)],
                         (SLOT_CG, 2): [lambda: attend(5), lambda: broadcast(4), lambda: broadcast(5)],
                         (SLOT_XV, 0): [lambda: attend(6), lambda: broadcast(6), lambda: broadcast(7)],
                         (SLOT_XV, 1): [lambda: attend(7), lambda: broadcast(8), lambda: broadcast(9)],
                         (SLOT_XV, 2): [lambda: broadcast(10), lambda: broadcast(11)],
                         (SLOT_BG, 0): [lambda: transposes(2, ki[0]), lambda: sample_values(0), lambda: sample_values(1)],
                         (SLOT_BG, 1): [lambda: transposes(3, ki[0]), lambda: outer(0)],
                         (SLOT_BG, 2): [lambda: outer(1)],
                         (SLOT_G, 0): [lambda: outer(2), sample_outputs],
                         (SLOT_G, 1): [lambda: outer(3)],
                         (SLOT_G, 2): [outputs, lambda: head_sums(0), lambda: head_sums(1), lambda: head_sums(2)]}
                for u in range(7):
                    def after(c):
                        for step in steps.get((u, c), ()):
                            step()
                    slot(14 * i + G_IN + 7 * e + u, (7 * e + u) % 2, KT, hh, hl, lows_ready(HI_MIX, KT), after)

            def out_proj():
                slots(G_OUT, KT, KT, hh, hl, lows_ready(HI_OUT, KT))

            def slots(g, n, nk, hi, lo, ready=None):
                with nc.tensor.Fori(0, n // 2) as i:
                    for b in range(2):
                        slot(2 * i + g + b, b, nk, hi, lo, ready)

            def ffn(l, g0, hi0, inst):
                sums(inst)
                g = g0
                for f0, n in FFN_CHUNKS:
                    slots(g, 2 * n, KT, hh, hl, lows_ready(hi0, KT))
                    g += 2 * n
                    slots(g, KT, n, ahi, alo, lambda c: pe.wait_ge(alo_ready, NC * (FT * l + f0 + n - 1) + c + 1 + NC))
                    g += KT

            def latents():
                sums(2)
                for u in range(6):
                    slot(G_LAT + u, u % 2, KT, hh, hl, lows_ready(HI_LAT, KT), rows=P if u < 5 else ROPE)
                sums(3)
                sums(4)

            def tokens_out():
                pe.wait_ge(ht_ready, 87)
                pe.wait_ge(kr_ready, NC)
                for i in range(TB + 1):
                    b = i % 2
                    ts, rows = (slice(i * P, (i + 1) * P), P) if i < TB else (slice(T, N), NS)
                    if i >= 2:
                        pe.wait_ge(tk_taken, i - 1)
                    for ct in range(CT):
                        nc.tensor.transpose(bank[3 + b][0:rows, ct * P:(ct + 1) * P], ckv32[:, ct, ts], ident[:])
                    nc.tensor.transpose(bank[3 + b][0:rows, CT * P:PW], kr[0:ROPE, ts], ident[0:ROPE, 0:ROPE]).then_inc(tk_ready, 1)

            def decode():
                pe.wait_ge(wuq_loaded, 16)
                for c in range(NC):
                    pe.wait_ge(bank_free[c], G_PAIR + 1)
                for h in range(MH):
                    for part, w in ((0, P), (1, ROPE)):
                        for k in range(QT):
                            at = h * (P + ROPE) + part * P
                            ins = mm(bank[part][0:w, h * NS:(h + 1) * NS], wuqw[:, k, at:at + w], cqs[:, k, :],
                                     start=k == 0, stop=k == QT - 1)
                ins.then_inc(qs_ready, 1)
                pe.wait_ge(wuk_loaded, 16)
                pe.wait_ge(tk_taken, TB + 1)
                pe.wait_ge(qs_taken, 1)

                def latent_query(h):
                    pe.wait_ge(wt_taken, h + 1)
                    for ct in range(CT):
                        ins = mm(bank[5 + ct][:, h * NS:(h + 1) * NS], wukt[:, ct * P:(ct + 1) * P], qns[:, h, :], start=True, stop=True)
                    ins.then_inc(ql_ready, 1)
                for h in range(MH):
                    for ct in range(CT):
                        ins = nc.tensor.transpose(bank[3 + h % 2][:, ct * P:(ct + 1) * P], wukw[:, ct, h * P:(h + 1) * P], ident[:])
                    ins.then_inc(wt_ready, 1)
                    latent_query(h)
                pe.wait_ge(ql_taken, CT)
                pe.wait_ge(knew_ready, 1)
                with nc.tensor.Fori(0, NS) as n:
                    def turned(j):
                        b = j % 2
                        if j % PG == 0:
                            pe.wait_ge(page_loaded[j // PG], 32 * PG * n + 32 * PG)
                        pe.wait_ge(kt_out[b], n * (PAGES // 2) + j // 2 + 1)
                        for ct in range(CT):
                            nc.tensor.transpose(bank[3 + b][:, ct * P:(ct + 1) * P], pages[:, j, ct * P:(ct + 1) * P], ident[:])
                        nc.tensor.transpose(bank[3 + b][0:ROPE, CT * P:3 * P], pages[:, j, CT * P:PW], ident[:]).then_inc(kt_bank[b], 1)

                    def scored(j, keys):
                        out = bank[5][:, j * MH:(j + 1) * MH]
                        for ct in range(CT):
                            mm(out, keys[:, ct, :], qlat[:, ct, bass.ds(n, 1), :].rearrange("p o h -> p (o h)"), start=ct == 0, stop=False)
                        return mm(out, keys[0:ROPE, CT, :], qrs[:, bass.ds(n, 1), :].rearrange("p o h -> p (o h)"), start=False, stop=True)

                    turned(0)
                    pe.wait_ge(pse_ready, n + 1)
                    for j in range(PAGES):
                        if j + 1 < PAGES:
                            turned(j + 1)
                        pe.wait_ge(kt_out[j % 2], n * (PAGES // 2) + j // 2 + 1 + 1)
                        scored(j, kts[j % 2]).then_inc(kt_used, 1)
                    scored(PAGES, ktn).then_inc(ds_ready, 1)
                    pe.wait_ge(pex_ready, n + 1)
                    for ct in range(CT):
                        for j in range(PAGES + 1):
                            keys = pages[:, j, ct * P:(ct + 1) * P] if j < PAGES else knew[:, ct * P:(ct + 1) * P]
                            ins = mm(bank[7 - ct][:, 0:MH], keys, pex[:, j, :], start=j == 0, stop=j == PAGES)
                            if j == PAGES:
                                ins.then_inc(ctx_ready, 1)
                            elif ct == 1 and j % PG == PG - 1:
                                ins.then_inc(page_used, 1)
                    pe.wait_ge(den_ready, n + 1)
                    mm(bank[2][:, 0:MH], ones[:], den[:], start=True, stop=True).then_inc(den_sum, 1)
                pe.wait_ge(wuv_loaded, 16)
                pe.wait_ge(ctx_taken, CT * NS)
                for h in range(MH):
                    for ct in range(CT):
                        ins = mm(bank[1][:, h * NS:(h + 1) * NS], wuvw[:, ct, h * P:(h + 1) * P], ctxs[:, ct, h, :],
                                 start=ct == 0, stop=ct == CT - 1)
                ins.then_inc(os_ready, 1)

            def pairs():
                pe.wait_ge(os_taken, 1)
                pe.wait_ge(kr2_ready, 1)
                with nc.tensor.Fori(0, PAIRS) as r:
                    g = r * PAIR_SLOTS + G_PAIR
                    for u in range(3):
                        slot(g + u, u % 2, QT, hh, hl)
                    for e in range(2):
                        slot(g + 3 + e, (3 + e) % 2, CT, hh[:, QT:QT + CT, :], hl[:, QT:QT + CT, :])
                    pe.wait_ge(w_split, g + 5 + 1 + 2)
                    wv_h, wv_l = (w[1][:, 0:2 * CT, :].rearrange("p (k e) m -> p k (e m)", k=CT) for w in (whi, wlo))
                    for c in range(NC + 1):
                        if c < NC:
                            pe.wait_ge(bank_free[c], g + 5 + 1)
                            out = bank[c]
                        else:
                            pe.wait_ge(pt_out[1], r * TB + 1)
                            out = bank[7]
                        for q in range(2):
                            keys = slice((2 * c + q) * P, (2 * c + q + 1) * P)
                            for k in range(CT):
                                ins = three(out[:, q * 2 * P:(q + 1) * 2 * P], hh[:, QT + k, keys], hl[:, QT + k, keys],
                                            wv_h[:, k, :], wv_l[:, k, :], k == 0, k == CT - 1)
                        if c == NC:
                            ins.then_inc(vx_ready, 1)
                        elif c < NC - 1:
                            ins.then_inc(bank_ready[c], 1)
                    pe.wait_ge(vx_ready, r + 1)
                    pe.sem_inc(bank_ready[NC - 1], 1)
                    for c in range(NC):
                        pe.wait_ge(bank_free[c], g + 6 + 1)
                    pe.wait_ge(vx_taken, r + 1)
                    u0 = r * (2 * TB)

                    def scores(u):
                        e, q = u % 2, u // 2
                        pe.wait_ge(p_ready, u0 + u + 1)
                        for at in range(0, (q + 1) * P, 512):
                            keys = slice(at, min(at + 512, (q + 1) * P))
                            mm(sbank[e][:, keys], qn[:, e, q * P:(q + 1) * P], kn[:, e, keys], start=True, stop=False)
                            ins = mm(sbank[e][:, keys], qr[e * ROPE:(e + 1) * ROPE, q * P:(q + 1) * P],
                                     kr[e * ROPE:(e + 1) * ROPE, keys], start=False, stop=True)
                        ins.then_inc(sc_ready, 1)

                    def turned(u):
                        q = u // 2
                        pe.wait_ge(pn_ready, u0 + u + 1)
                        for part, bk in ((0, 2), (1, 7)):
                            if q < 4 * part:
                                continue
                            if part == 0:
                                pe.wait_ge(pt_out[0], u0 + u + 1)
                            else:
                                pe.wait_ge(pt_out[1], r * TB + (u - 8) + 1)
                            for k in range(4 * part, min(q + 1, 4 * part + 4)):
                                at = (k - 4 * part) * P
                                ins = nc.tensor.transpose(bank[bk][:, at:at + P], pp[u % 2][:, k * P:(k + 1) * P], ident[:])
                            ins.then_inc(pt_bank[part], 1)
                        pe.wait_ge(pt_bank[part if q >= 4 else 0], (r * TB + (u - 8) + 1) if q >= 4 else u0 + u + 1)
                        pe.sem_inc(p_used, 1)

                    def weighed(u):
                        e, q = u % 2, u // 2
                        pe.wait_ge(pt_out[0], u0 + u + 1 + 1)
                        if q >= 4:
                            pe.wait_ge(pt_out[1], r * TB + (u - 8) + 1 + 1)
                        pe.wait_ge(ol_ready, r * (2 * TB + 2) + u + 1)
                        for k in range(q + 1):
                            ins = mm(bank[e][:, 0:P], vv[:, k, e * P:(e + 1) * P], pt[e][:, k, :], start=k == 0, stop=k == q)
                        ins.then_inc(ao_ready, 1)

                    scores(0)
                    for u in range(2 * TB):
                        if u + 1 < 2 * TB:
                            scores(u + 1)
                        turned(u)
                        if u > 0:
                            weighed(u - 1)
                    weighed(2 * TB - 1)
                    with nc.tensor.Fori(0, KT // 2) as i:
                        for b in range(2):
                            slot(g + 2 * i + 6 + b, b, 2, hh[:, O0:O0 + 2, :], hl[:, O0:O0 + 2, :],
                                 lambda c: pe.wait_ge(ol_ready, r * (2 * TB + 2) + 2 * TB + 2 + 2))

            def final():
                sums(6)
                for c in range(NC):
                    pe.wait_ge(bank_free[c], G_END + 1)
                nc.tensor.transpose(bank[0][0:72, 0:P], cout[:].rearrange("p s w j -> p (s w j)"), ident[:]).then_inc(conv_bank, 1)
                pe.wait_ge(f_ready, NC * KT)
                for i in range(TB + 1):
                    b = i % 2
                    ts, rows = (slice(i * P, (i + 1) * P), P) if i < TB else (slice(T, N), NS)
                    if i >= 2:
                        pe.wait_ge(yt_out[b], 2 * (i // 2))
                    for half in range(2):
                        for q in range(4):
                            ins = nc.tensor.transpose(bank[3 + 2 * b + half][0:rows, q * P:(q + 1) * P], xT[:, 4 * half + q, ts], ident[:])
                        ins.then_inc(yt_bank[half], 1)

            pe.sem_inc(ada_used, 2)
            pe.sem_inc(sq_used, 2)
            pe.sem_inc(bank_ready[NC - 1], READY0[NC - 1])
            pe.sem_inc(page_used, PAGES // PG)
            pe.sem_inc(kt_used, 2)
            pe.sem_inc(p_used, 2)
            pe.sem_inc(ao_ready, 2)
            pe.sem_inc(kt_out[0], 1)
            pe.sem_inc(kt_out[1], 1)
            phases = [setup, mixer, out_proj, lambda: ffn(0, G_FFN0, HI_FFN0, 1), latents, tokens_out, decode, pairs,
                      lambda: ffn(1, G_FFN1, HI_FFN1, 5), final]
            for phase in phases:
                phase()


_INS = ['x_prompt', 'x_sample', 'c_prompt', 'c_sample', 'cache_conv', 'state_hgrn', 'cache_ckv', 'cache_krope',
        'page_table', 'w_ada', 'b_ada', 'norm_mix', 'norm_ffn', 'w_in_even', 'conv_w', 'hg_gnorm', 'w_out_even',
        'w_dqkv', 'q_norm', 'w_uq', 'kv_norm', 'w_uk', 'w_uv', 'w_o', 'w_gu', 'w_down', 'norm_final']
_OUTS = [(1, T, D), (NS, 1, D), (1, 1, 2, 512), (1, 1, HEADS, P, P), (1, 1, T, CT * P), (1, 1, T, ROPE),
         (1, NS, 2, 512), (1, NS, HEADS, P, P), (1, NS, 1, CT * P), (1, NS, 1, ROPE)]


def rope_tables():
    past = PAGES * P
    pos = np.concatenate([np.arange(T), np.full(NS, past)]).astype(np.float32)
    inv = (10000.0 ** (-np.arange(HR) / HR)).astype(np.float32)
    ang = (inv[:, None] * pos[None, :]).astype(np.float32)
    cos, sin = np.cos(ang), np.sin(ang)
    return (np.ascontiguousarray(np.tile(cos, (4, 1)), np.float32),
            np.ascontiguousarray(np.concatenate([-sin, sin, -sin, sin]), np.float32))


def kernel(**inputs):
    import concourse.bacc as _bacc
    from concourse.bass_utils import run_bass_kernel_spmd as _run

    nc = _bacc.Bacc("TRN2", target_bir_lowering=False, num_devices=1)
    arrays, args = {}, []
    given = {name: np.ascontiguousarray(inputs[name]) for name in _INS}
    given["rope_cos"], given["rope_sin"] = rope_tables()
    for name, a in given.items():
        arrays[f"in_{name}"] = a
        args.append(nc.dram_tensor(f"in_{name}", a.shape, mybir.dt.from_np(a.dtype), kind="ExternalInput").ap())
    for i, shape in enumerate(_OUTS):
        args.append(nc.dram_tensor(f"out_{i}", shape, F, kind="ExternalOutput").ap())
    trunk(nc, *args)
    r = _run(nc, [arrays], core_ids=[0])
    return tuple(r.results[0][f"out_{i}"] for i in range(len(_OUTS)))
```

```python
from contextlib import ExitStack

import concourse.bass as bass
import numpy as np
from concourse import mybir

F = mybir.dt.float32
R = mybir.dt.float32r
I32 = mybir.dt.int32
ACT = mybir.ActivationFunctionType
ALU = mybir.AluOpType
AX = mybir.AxisListType
RMAX = bass.bass_isa.ReduceOp.max

P = 128
D = 1024
KT = D // P
T = 1024
NS = 8
N = T + NS
NC = 3
CW = N // NC
LASTP = CW - NS
TB = T // P
EPS = 1e-6
CG = 4
GC = P // CG
NEG = -1e30
HEADS = 4
CH = 64
NCH = T // CH
BL = 8
NBL = T // BL
CB = CH // BL
FF = 2816
FT = FF // P
FFN_CHUNKS = [(0, 6), (6, 6), (12, 5), (17, 5)]
MH = 8
ROPE = 64
HR = ROPE // 2
CT = 2
QT = 3
ORDER_HEAD = 85
ORDER_SEQ = 2
ORDER_PAIR = 51
MLA_SCALE = (P + ROPE) ** -0.5
PAGES = 32
PG = 8
SP_ROPE = (1, 4, 7)
KB = 4
KT_BANKS = (3, 4, 0, 1)
SC_BANKS = (7, 2)
UN = PAGES // 2
QN = PAGES // CG
PW = CT * P + ROPE

PIECES = [(d, h * NBL // 2, NBL // 2) for d in range(4) for h in range(2)] + [(d, 0, NBL) for d in range(4, BL)]

AW = 256
ADA_SHIFT_SCALE = 2 * KT // 2
ADA_MIX = 3 * KT // 2
ADA_LAYER = 6 * KT // 2

G_IN = 0
G_OUT = G_IN + 7 * HEADS
G_FFN0 = G_OUT + KT
FFN_SLOTS = 2 * FT + KT * len(FFN_CHUNKS)
G_LAT = G_FFN0 + FFN_SLOTS
G_PAIR = G_LAT + 6
PAIR_SLOTS = 6 + KT
PAIRS = MH // 2
G_FFN1 = G_PAIR + PAIRS * PAIR_SLOTS
G_END = G_FFN1 + FFN_SLOTS
Z_ORDER = [4, 3, 5, 1, 2, 0, 6]
SLOT_F, SLOT_Q, SLOT_V, SLOT_CG, SLOT_XV, SLOT_BG, SLOT_G = range(7)
READY0 = (0, 0, 2)

NORMS = [KT, KT, KT, QT, CT, KT, KT]
SQ_BASE = [NC * sum(NORMS[:i]) for i in range(len(NORMS) + 1)]
HI_MIX, HI_OUT, HI_FFN0, HI_LAT, HI_CQ, HI_CKV, HI_FFN1 = (NC * n for n in (0, KT, 2 * KT, 3 * KT, 4 * KT, 4 * KT + QT, 4 * KT + QT + CT))


def row_tiles(g):
    if g >= G_FFN1:
        return row_tiles(g - G_FFN1 + G_FFN0) if g < G_END else KT
    if g >= G_PAIR:
        u = (g - G_PAIR) % PAIR_SLOTS
        return QT if u < 3 else CT if u < 5 else 2 * CT if u == 5 else 2
    if G_FFN0 <= g < G_LAT:
        g -= G_FFN0
        for _, n in FFN_CHUNKS:
            if g < 2 * n:
                return KT
            g -= 2 * n
            if g < KT:
                return n
            g -= KT
    return KT


class InOrder:

    def __init__(self, eng, sem):
        self.eng, self.sem, self.base, self.n = eng, sem, 0, 0

    def put(self, ins):
        ins.then_inc(self.sem, 1)
        self.n += 1

    def wait(self):
        self.eng.wait_ge(self.sem, self.base + self.n if not isinstance(self.base, int) else self.base + self.n)

    def __call__(self, ins):
        self.put(ins)
        self.wait()

    def enter(self, i, per):
        self.start, self.per = self.base + self.n, per
        self.base, self.n = i * per + self.start, 0

    def leave(self, turns):
        assert self.n == self.per, (self.n, self.per)
        self.base, self.n = self.start + turns * self.per, 0


def cols(c):
    return slice(c * CW, (c + 1) * CW)


def one(ap):
    return ap.rearrange("p o n -> p (o n)")


def trunk(nc, x_prompt, x_sample, c_prompt, c_sample, cache_conv, state_hgrn, cache_ckv, cache_krope,
          page_table, w_ada, b_ada, norm_mix, norm_ffn, w_in_even, conv_w, hg_gnorm, w_out_even, w_dqkv,
          q_norm, w_uq, kv_norm, w_uk, w_uv, w_o, w_gu, w_down, norm_final, rope_cos, rope_sin,
          y_prompt, y_sample, conv_prompt, hgrn_prompt, ckv_prompt, krope_prompt,
          conv_sample, hgrn_sample, ckv_sample, krope_sample):
    ctx = ExitStack()
    with ctx:
        def sb(name, shape, dt=F):
            return ctx.enter_context(nc.sbuf_tensor(name, shape, dt))

        def sem(name):
            return ctx.enter_context(nc.semaphore(name))

        xT = sb("xT", [P, KT, N])
        hh = sb("hh", [P, KT, N], R)
        hl = sb("hl", [P, KT, N], R)
        wst = [sb(f"wst{b}", [P, KT, P]) for b in range(2)]
        whi = [sb(f"whi{b}", [P, KT, P], R) for b in range(2)]
        wlo = [sb(f"wlo{b}", [P, KT, P], R) for b in range(2)]
        ident = sb("ident", [P, P])
        ones = sb("ones", [P, P])
        vec0 = sb("vec0", [P, P])
        vec1 = sb("vec1", [P, 98])
        cconv = sb("cconv", [P, NS, 2, HEADS])
        cout = sb("cout", [P, 1 + NS, 2, HEADS])
        mod = sb("mod", [P, 2, 48, 1 + NS])
        amp = sb("amp", [P, 4, KT, 1 + NS])
        siluc = sb("siluc", [P, KT, 1 + NS])
        sq = [sb(f"sq{b}", [P, CW]) for b in range(2)]
        rt = sb("rt", [P, CW])
        rs = sb("rs", [P, CW])
        gtmp = sb("gtmp", [P, NS])
        sel = sb("sel", [P, 1 + NS])
        causal = sb("causal", [P, P])
        masks = sb("masks", [P, NS])
        ARENA = 75648
        sb("arena", [P, ARENA // 4])
        at0 = nc.sbuf_base - ARENA
        used = {}

        def lay(stage, name, shape, dt=F):
            at = used.get(stage, 0)
            used[stage] = at + int(np.prod(shape[1:])) * 4 + 31 & ~31
            assert used[stage] <= ARENA, (name, used[stage], ARENA)
            return nc.alloc_sbuf_tensor_at(name, shape, dt, offset=at0 + at)

        b_adaT = vec0[:, 0:96].rearrange("p (l i) -> p l i", l=2)
        gT = vec0[:, 96:128].rearrange("p (s l k) -> p s l k", s=2, l=2)
        finT = vec1[:, 0:8]
        convT = vec1[:, 8:20].rearrange("p (w j) -> p w j", w=3)
        gnT = vec1[:, 20:21]
        qnT = vec1[:, 21:24]
        kvnT = vec1[:, 24:26]
        cT = vec1[:, 26:98].rearrange("p (n k) -> p n k", k=KT)

        xtok = lay("set", "xtok", [P, TB, D])
        xstok = lay("set", "xstok", [NS, D])
        rows0 = lay("set", "rows0", [P, P])
        rows1 = lay("set", "rows1", [98, P])
        rows2 = lay("set", "rows2", [64, P])
        hf = lay("mix", "hf", [P, N])
        hk = lay("mix", "hk", [P, N])
        hq = lay("mix", "hq", [P, N])
        hv = lay("mix", "hv", [P, N])
        ug = lay("mix", "ug", [P, N + 2])
        qb = lay("mix", "qb", [P, T])
        k1 = lay("mix", "k1", [P, T])
        ki = [lay("mix", f"ki{b}", [P, T]) for b in range(2)]
        mq = lay("mix", "mq", [P, T])
        ed = [lay("mix", f"ed{b}", [P, 512]) for b in range(2)]
        am = mq[:].rearrange("p (c t) -> p c t", t=P)
        dtmp = lay("mix", "dtmp", [P, 512])
        oacc = lay("mix", "oacc", [P, N])
        vtok = lay("mix", "vtok", [P, TB, P])
        ktok = lay("mix", "ktok", [P, TB, P])
        st = lay("mix", "st", [P, NCH + 1, P])
        s0 = lay("mix", "s0", [P, NS, P])
        fb = lay("mix", "fb", [P, NBL])
        cp = lay("mix", "cp", [P, NBL])
        ftot = lay("mix", "ftot", [P, NCH])
        most = max(n for _, n in FFN_CHUNKS)
        ahi = lay("ffn", "ahi", [P, most, N], R)
        alo = lay("ffn", "alo", [P, most, N], R)
        sil = [lay("ffn", f"sil{c}", [P, CW]) for c in range(NC)]
        NH = 3
        used["norm"] = used["ffn"]
        htmp = [lay("norm", f"htmp{b}", [P, CW]) for b in range(NH)]
        adaw = [lay("norm", f"adaw{b}", [P, KT, AW]) for b in range(2)]
        adar = lay("norm", "adar", [P, AW])
        atmp = [lay("ffn", f"atmp{c}", [P, CW]) for c in range(NC)]
        kr = lay("keep", "kr", [P, N])
        rc = lay("keep", "rc", [P, N])
        rsn = lay("keep", "rsn", [P, N])
        os32 = lay("keep", "os32", [P, MH, NS])
        ktn = lay("keep", "ktn", [P, 3, P])
        knew = lay("keep", "knew", [P, CT * P])
        cqs = lay("keep", "cqs", [P, QT, NS])
        used["dec"] = used["keep"]
        sw = [lay("keep", f"sw{c}", [P, CW]) for c in range(NC)]
        used["lat"] = used["pair"] = used["keep"]
        craw = lay("lat", "craw", [P, QT + CT, N])
        ckv32 = lay("lat", "ckv32", [P, CT, N])
        lt = [lay("lat", f"lt{b}", [P, CW]) for b in range(2)]
        ctok = [lay("lat", f"ctok{b}", [P, PW]) for b in range(2)]
        wuvw = lay("dec", "wuvw", [P, CT, MH * P])
        ktp = [w[:, 0:6, :].rearrange("p (k e) m -> p k (e m)", k=3) for w in wst]
        wukt = lay("dec", "wukt", [P, CT * P])
        qns = lay("dec", "qns", [P, MH, NS])
        qall = lay("dec", "qall", [P, 3, NS, MH])
        qcur = lay("dec", "qcur", [P, 3, MH])
        sct = [lay("dec", f"sct{b}", [P, 2 * P]) for b in range(2)]
        ctx8 = lay("dec", "ctx8", [P, CT * P])
        qsw = lay("dec", "qsw", [ROPE, MH, NS])
        mx = lay("dec", "mx", [P, MH])
        mxa = lay("dec", "mxa", [P, MH])
        den = lay("dec", "den", [P, MH])
        rden = lay("dec", "rden", [P, MH])
        ctxs = lay("dec", "ctxs", [P, CT, MH, NS])
        pse = lay("dec", "pse", [P, PAGES + 1, MH])
        pex = lay("dec", "pex", [P, PAGES + 1, MH])
        ptab = lay("dec", "ptab", [1, NS * PAGES], I32)
        used["page"] = used["dec"]
        wukw = lay("dec", "wukw", [P, CT, MH * P])
        used["wuq"] = ARENA - QT * MH * (P + ROPE) * 4
        assert used["wuq"] >= used["lat"]
        wuqw = lay("wuq", "wuqw", [P, QT, MH * (P + ROPE)])
        pages = lay("page", "pages", [P, PAGES, PW])
        qn = lay("pair", "qn", [P, 2, N])
        qr = lay("pair", "qr", [P, N])
        kn = lay("pair", "kn", [P, 2, N])
        vv = lay("pair", "vv", [P, TB, 2 * P])
        pp = [lay("pair", f"pp{b}", [P, T]) for b in range(2)]
        pt = [lay("pair", f"pt{b}", [P, TB, P]) for b in range(2)]
        amx = [lay("pair", f"amx{b}", [P, 4]) for b in range(2)]
        O0 = 5
        ytok = [lay("fin", f"ytok{b}", [P, D]) for b in range(2)]

        x_rest = nc.dram_tensor("x_rest", [P, KT, N], F).ap()
        crow = lay("fin", "crow", [72, P])
        low = [ctx.enter_context(nc.psum_tensor(f"bank{i}", [P, 512], F)) for i in range(NC)]
        w34 = ctx.enter_context(nc.psum_tensor("bank34", [P, 1024], F))
        w56 = ctx.enter_context(nc.psum_tensor("bank56", [P, 1024], F))
        b7 = ctx.enter_context(nc.psum_tensor("bank7", [P, 512], F))
        bank = [t[:] for t in low] + [w[:, 512 * j:512 * j + 512] for w in (w34, w56) for j in range(2)] + [b7[:]]
        sbank = [w34, w56]

        vecs_loaded, x_loaded, ident_ready, ones_ready = map(sem, ("vecs_loaded", "x_loaded", "ident_ready", "ones_ready"))
        vec_bank, vec_ready, xt_bank, xt_act, xt_dve = map(sem, ("vec_bank", "vec_ready", "xt_bank", "xt_act", "xt_dve"))
        sel_ready, ada_part = sem("sel_ready"), sem("ada_part")
        siluc_ready, ada_used, ada_copied, ada_back, ada_bank, mod_ready = map(
            sem, ("siluc_ready", "ada_used", "ada_copied", "ada_back", "ada_bank", "mod_ready"))
        ada_loaded = [sem(f"ada_loaded{b}") for b in range(2)]
        w_loaded = [sem(f"w_loaded{b}") for b in range(2)]
        w_hi, w_split = sem("w_hi"), sem("w_split")
        bank_ready = [sem(f"bank_ready{c}") for c in range(NC)]
        bank_free = [sem(f"bank_free{c}") for c in range(NC)]
        sq_ready, sq_used, ss_ready, rt_ready, rs_ready, ht_ready = map(
            sem, ("sq_ready", "sq_used", "ss_ready", "rt_ready", "rs_ready", "ht_ready"))
        hi_ready, lo_ready = sem("hi_ready"), sem("lo_ready")
        dve_order, x_order, pool_order = sem("dve_order"), sem("x_order"), sem("pool_order")
        sp_turn, pool_turn, pe_turn = sem("sp_turn"), sem("pool_turn"), sem("pe_turn")
        x_saved, x_back = sem("x_saved"), sem("x_back")
        qsig_ready, gsig_ready = sem("qsig_ready"), sem("gsig_ready")
        ki_ready, ki_used, qe_ready, e_ready = map(sem, ("ki_ready", "ki_used", "qe_ready", "e_ready"))
        a_ready, a_taken, wk_half, wk_ready, wk_free = map(sem, ("a_ready", "a_taken", "wk_half", "wk_ready", "wk_free"))
        bc_ready = [sem(f"bc_ready{b}") for b in range(2)]
        bc_free = [sem(f"bc_free{b}") for b in range(2)]
        st_ready, o_ready, o_taken, dv_ready, s_new = map(sem, ("st_ready", "o_ready", "o_taken", "dv_ready", "s_new"))
        oacc_ready, hsq_ready, hrt_ready, hrs_ready, y_ready = map(
            sem, ("oacc_ready", "hsq_ready", "hrt_ready", "hrs_ready", "y_ready"))
        s0_loaded, st_saved, so_saved = sem("s0_loaded"), sem("st_saved"), sem("so_saved")
        act_ready, ahi_ready, alo_ready = map(sem, ("act_ready", "ahi_ready", "alo_ready"))
        rope_loaded, sw_ready, kr_ready, kr2_ready = map(
            sem, ("rope_loaded", "sw_ready", "kr_ready", "kr2_ready"))
        tk_ready, tk_taken = sem("tk_ready"), sem("tk_taken")
        tk_saved = [sem(f"tk_saved{b}") for b in range(2)]
        wuq_loaded, wuk_loaded, wuv_loaded, ptab_loaded = map(sem, ("wuq_loaded", "wuk_loaded", "wuv_loaded", "ptab_loaded"))
        qs_ready, qs_sw, qs_taken, wt_ready, wt_taken, ql_ready, ql_taken = map(
            sem, ("qs_ready", "qs_sw", "qs_taken", "wt_ready", "wt_taken", "ql_ready", "ql_taken"))
        page_loaded = [sem(f"page_loaded{q}") for q in range(PAGES // PG)]
        prope_loaded = [sem(f"prope_loaded{q}") for q in range(PAGES // PG)]
        page_used, q_ready, sc_part, sc_bank, sc_out, sc_back, ctx_part, c8_ready, ct_bank = map(
            sem, ("page_used", "q_ready", "sc_part", "sc_bank", "sc_out", "sc_back", "ctx_part", "c8_ready", "ct_bank"))
        kt_bank = [sem(f"kt_bank{b}") for b in range(KB)]
        kt_out = [sem(f"kt_out{b}") for b in range(KB)]
        ds_ready, mx_ready, mxa_ready, pse_ready, pex_ready = map(
            sem, ("ds_ready", "mx_ready", "mxa_ready", "pse_ready", "pex_ready"))
        den_ready, den_sum, ctx_taken, os_ready, os_taken = map(
            sem, ("den_ready", "den_sum", "ctx_taken", "os_ready", "os_taken"))
        masks_ready, knew_ready, sw_used, p_used = map(sem, ("masks_ready", "knew_ready", "sw_used", "p_used"))
        vx_ready, vx_taken, sc_ready, nb_ready, p_ready, pn_ready = map(
            sem, ("vx_ready", "vx_taken", "sc_ready", "nb_ready", "p_ready", "pn_ready"))
        pt_bank = [sem(f"pt_bank{b}") for b in range(2)]
        pt_out = [sem(f"pt_out{b}") for b in range(2)]
        ao_ready, oh_ready, ol_ready = sem("ao_ready"), sem("oh_ready"), sem("ol_ready")
        f_ready = sem("f_ready")
        yt_bank = [sem(f"yt_bank{b}") for b in range(2)]
        yt_out = [sem(f"yt_out{b}") for b in range(2)]
        yt_saved = [sem(f"yt_saved{b}") for b in range(2)]
        conv_bank, conv_out = sem("conv_bank"), sem("conv_out")
        saved = sem("saved")

        block = ctx.enter_context(nc.Block())

        @block.sync
        def _(sp):
            def load(g, b, dst, src):
                sp.wait_ge(w_split, g + 1)
                sp.sem_inc(sp_turn, 1)
                sp.dma_start(dst, src).then_inc(w_loaded[b], 32)

            def load_ada(l, a, b):
                sp.wait_ge(ada_used, a + ADA_LAYER * l + 1)
                sp.dma_start(adaw[b][:], w_ada[l].rearrange("(k p) (w m) -> p k w m", p=P, m=AW)[:, :, bass.ds(a, 1), :]
                             .rearrange("p k o m -> p k (o m)")).then_inc(ada_loaded[b], 16)

            def setup():
                for dst, src in ((rows0[0:96, :], b_ada.rearrange("l (i p) -> (l i) p", p=P)),
                                 (rows0[96:112, :], norm_mix.rearrange("l (i p) -> (l i) p", p=P)),
                                 (rows0[112:128, :], norm_ffn.rearrange("l (i p) -> (l i) p", p=P)),
                                 (rows1[0:8, :], norm_final.rearrange("(i p) -> i p", p=P)),
                                 (rows1[8:20, :], conv_w.rearrange("o w (j p) -> (o w j) p", p=P)),
                                 (rows1[20:21, :], hg_gnorm),
                                 (rows1[21:24, :], q_norm.rearrange("o (i p) -> (o i) p", p=P)),
                                 (rows1[24:26, :], kv_norm.rearrange("o (i p) -> (o i) p", p=P)),
                                 (rows1[26:34, :], c_prompt.rearrange("o (i p) -> (o i) p", p=P)),
                                 (rows1[34:98, :], c_sample.rearrange("n (i p) -> (n i) p", p=P)),
                                 (rows2[:], cache_conv.rearrange("o n w (j p) -> (o n w j) p", p=P))):
                    sp.dma_start(dst, src).then_inc(vecs_loaded, 16)
                for i in range(TB):
                    sp.dma_start(xtok[:, i, :], x_prompt[0, i * P:(i + 1) * P, :]).then_inc(x_loaded, 16)
                sp.dma_start(xstok[:], x_sample.rearrange("n o d -> (n o) d")).then_inc(x_loaded, 16)
                with nc.sync.Fori(0, ADA_MIX // 2) as i:
                    for b in range(2):
                        load_ada(0, 2 * i + b, b)

            def mixer():
                sp.wait_ge(xt_act, 8)
                sp.wait_ge(xt_dve, 9)
                sp.dma_start(x_rest, xT[:]).then_inc(x_saved, 16)
                win = w_in_even[0].rearrange("(k p) (z j m) -> p k z j m", p=P, z=7, m=P)
                with nc.sync.Fori(0, HEADS // 2) as i:
                    for e in range(2):
                        h = 2 * i + e
                        for u in range(7):
                            load(14 * i + 7 * e + u + G_IN, (7 * e + u) % 2, wst[(7 * e + u) % 2][:],
                                 win[:, :, Z_ORDER[u], bass.ds(h, 1), :].rearrange("p k o m -> p k (o m)"))
                            if u == 4:
                                sp.wait_ge(so_saved, 16 * h + 16)
                                sp.dma_start(s0[:], state_hgrn[0].rearrange("n h k v -> k n h v")
                                             [:, :, bass.ds(h, 1), :].rearrange("k n o v -> k n (o v)")).then_inc(s0_loaded, 16)

            def out_proj():
                wout = w_out_even[0].rearrange("(k p) (j m) -> p k j m", p=P, m=P)
                for b in range(2):
                    load(G_OUT + b, b, wst[b][:], wout[:, :, b, :])
                sp.wait_ge(lo_ready, HI_FFN0)
                sp.dma_start(xT[:], x_rest).then_inc(x_back, 16)
                sp.wait_ge(st_saved, 16 * HEADS + 16)
                sp.wait_ge(so_saved, 16 * HEADS + 16)
                with nc.sync.Fori(1, KT // 2) as i:
                    for b in range(2):
                        load(2 * i + G_OUT + b, b, wst[b][:], wout[:, :, bass.ds(2 * i + b, 1), :].rearrange("p k o m -> p k (o m)"))
                        for e in range(2):
                            load_ada(0, 4 * i + ADA_MIX - 4 + 2 * b + e, e)

            def ffn(l, g0):
                wgu = w_gu[l].rearrange("(k p) (z f m) -> p k z f m", p=P, z=2, m=P)
                wdn = w_down[l].rearrange("(f p) (j m) -> p f j m", p=P, m=P)
                g = g0
                for f0, n in FFN_CHUNKS:
                    with nc.sync.Fori(0, n) as i:
                        for b in range(2):
                            load(2 * i + g + b, b, wst[b][:], wgu[:, :, b, bass.ds(i + f0, 1), :].rearrange("p k o m -> p k (o m)"))
                            if l == 0 and f0 < ADA_LAYER // 2:
                                load_ada(1, 2 * i + 2 * f0 + b, b)
                    g += 2 * n
                    with nc.sync.Fori(0, KT // 2) as i:
                        for b in range(2):
                            load(2 * i + g + b, b, wst[b][:, 0:n, :],
                                 wdn[:, f0:f0 + n, bass.ds(2 * i + b, 1), :].rearrange("p k o m -> p k (o m)"))
                    g += KT

            def latents():
                sp.wait_ge(bank_ready[NC - 1], G_LAT + READY0[NC - 1])
                sp.dma_start(rc[:], rope_cos).then_inc(rope_loaded, 16)
                sp.dma_start(rsn[:], rope_sin).then_inc(rope_loaded, 16)
                wd = w_dqkv[0].rearrange("(k p) m -> p k m", p=P)
                for u in range(6):
                    w = ROPE if u == 5 else P
                    load(G_LAT + u, u % 2, wst[u % 2][:, :, 0:w], wd[:, :, u * P:u * P + w])
                sp.wait_ge(lo_ready, HI_CQ)
                sp.dma_start(wuqw[:], w_uq[0].rearrange("(k p) m -> p k m", p=P)).then_inc(wuq_loaded, 16)

            def tokens_out():
                for i in range(TB + 1):
                    b = i % 2
                    rows = P if i < TB else NS
                    sp.wait_ge(tk_taken, i + 1)
                    dst_c = ckv_prompt[0, 0, i * P:(i + 1) * P, :] if i < TB else ckv_sample[0, :, 0, :]
                    dst_r = krope_prompt[0, 0, i * P:(i + 1) * P, :] if i < TB else krope_sample[0, :, 0, :]
                    sp.dma_start(dst_c, ctok[b][0:rows, 0:CT * P]).then_inc(tk_saved[b], 16)
                    sp.dma_start(dst_r, ctok[b][0:rows, CT * P:PW]).then_inc(tk_saved[b], 16)

            def decode():
                sp.dma_start(ptab[:], page_table.rearrange("(o n) j -> o (n j)", o=1)).then_inc(ptab_loaded, 16)
                sp.wait_ge(knew_ready, 1)
                sp.wait_ge(lo_ready, HI_FFN1)
                sp.wait_ge(tk_saved[0], 32 * 5 + 32)
                sp.wait_ge(tk_saved[1], 32 * 4 + 32)
                sp.dma_start(wukw[:], w_uk[0].rearrange("(k p) h m -> p k (h m)", p=P)).then_inc(wuk_loaded, 16)
                sp.dma_start(wuvw[:], w_uv[0].rearrange("(k p) h m -> p k (h m)", p=P)).then_inc(wuv_loaded, 16)
                sp.wait_ge(ptab_loaded, 16)
                sp.wait_ge(wt_ready, MH)
                with nc.sync.Fori(0, NS) as n:
                    at = [sp.value_load(ptab[0:1, bass.ds(n * PAGES + j, 1)], min_val=0, max_val=cache_ckv.shape[1] - 1)
                          for j in range(PAGES)]
                    for j, page in enumerate(at):
                        if j % PG == 0:
                            sp.wait_ge(page_used, (PAGES // PG) * n + j // PG + 1)
                        sp.dma_start(pages[:, j, 0:CT * P], cache_ckv[0, bass.ds(page, 1)].rearrange("o p c -> p (o c)")
                                     ).then_inc(page_loaded[j // PG], 16)
                        if j % PG in SP_ROPE:
                            sp.dma_start(pages[:, j, CT * P:PW], cache_krope[0, bass.ds(page, 1)].rearrange("o p c -> p (o c)")
                                         ).then_inc(page_loaded[j // PG], 16)

            def pairs():
                wq = w_uq[0].rearrange("(k p) (r e m) -> p k r e m", p=P, e=2, m=P + ROPE)
                wk = w_uk[0].rearrange("(k p) (r e) m -> p k r e m", p=P, e=2)
                wv = w_uv[0].rearrange("(k p) (r e) m -> p k r e m", p=P, e=2)
                wo = w_o[0].rearrange("(r k p) (j m) -> p r k j m", p=P, k=2, m=P)
                sp.wait_ge(ds_ready, NS)
                with nc.sync.Fori(0, PAIRS) as r:
                    g = PAIR_SLOTS * r + G_PAIR
                    for e in range(2):
                        load(g + e, e, wst[e][:, 0:QT, :], wq[:, :, bass.ds(r, 1), e, 0:P].rearrange("p k o m -> p k (o m)"))
                    sp.wait_ge(w_split, g + 2 + 1)
                    for e in range(2):
                        sp.dma_start(wst[0][:, 0:QT, e * ROPE:(e + 1) * ROPE],
                                     wq[:, :, bass.ds(r, 1), e, P:P + ROPE].rearrange("p k o m -> p k (o m)")).then_inc(w_loaded[0], 16)
                    for e in range(2):
                        load(g + 3 + e, (3 + e) % 2, wst[(3 + e) % 2][:, 0:CT, :],
                             wk[:, :, bass.ds(r, 1), e, :].rearrange("p k o m -> p k (o m)"))
                    load(g + 5, 1, wst[1][:, 0:2 * CT, :].rearrange("p (k e) m -> p k (e m)", k=CT),
                         wv[:, :, bass.ds(r, 1), :, :].rearrange("p k o e m -> p k (o e m)"))
                    with nc.sync.Fori(0, KT // 2) as i:
                        for b in range(2):
                            load(PAIR_SLOTS * r + 2 * i + G_PAIR + 6 + b, b, wst[b][:, 0:2, :],
                                 wo[:, bass.ds(r, 1), :, bass.ds(2 * i + b, 1), :].rearrange("p o k q m -> p (o k) (q m)"))

            def final():
                sp.wait_ge(conv_out, 1)
                for dst, r0, n in ((conv_prompt.rearrange("o b w (j p) -> (o b w j) p", p=P), 0, 8),
                                   (conv_sample.rearrange("o n w (j p) -> (o n w j) p", p=P), 8, 64)):
                    sp.dma_start(dst, crow[r0:r0 + n, :]).then_inc(saved, 16)
                for i in range(TB + 1):
                    b = i % 2
                    sp.wait_ge(yt_out[b], 2 * (i // 2) + 2)
                    dst = y_prompt[0, i * P:(i + 1) * P, :] if i < TB else y_sample.rearrange("n o d -> (n o) d")
                    sp.dma_start(dst, ytok[b][0:P if i < TB else NS, :]).then_inc(yt_saved[b], 16)
                sp.wait_ge(saved, 32)
                sp.wait_ge(yt_saved[0], 16 * 5 + 16)
                sp.wait_ge(yt_saved[1], 16 * 4 + 16)
                sp.wait_ge(tk_saved[0], 32 * 5 + 32)
                sp.wait_ge(tk_saved[1], 32 * 4 + 32)
                sp.wait_ge(st_saved, 16 * HEADS + 16)
                sp.wait_ge(so_saved, 16 * HEADS + 16)

            sp.sem_inc(st_saved, 16)
            sp.sem_inc(so_saved, 16)
            for b in range(2):
                sp.sem_inc(yt_saved[b], 16)
                sp.sem_inc(tk_saved[b], 32)
            phases = [setup, mixer, out_proj, lambda: ffn(0, G_FFN0), latents, tokens_out, decode, pairs,
                      lambda: ffn(1, G_FFN1), final]
            for phase in phases:
                phase()

        @block.gpsimd
        def _(pool):
            order = InOrder(pool, pool_order)

            def split_at(g0, i, u, nk, per):
                b = (g0 + u) % 2
                pool.wait_ge(w_loaded[b], 32 * ((g0 + u) // 2 + 1) + i * (16 * per))
                pool.wait_ge(bank_ready[NC - 1], i * per + g0 + u + 1)
                pool.sem_inc(pool_turn, 1)
                nc.gpsimd.tensor_copy(whi[b][:, 0:nk, :], wst[b][:, 0:nk, :]).then_inc(w_hi, 1)
                pool.wait_ge(w_hi, i * per + g0 + u + 1)
                nc.gpsimd.tensor_tensor(wlo[b][:, 0:nk, :], wst[b][:, 0:nk, :], whi[b][:, 0:nk, :].bitcast(F),
                                        ALU.subtract).then_inc(w_split, 1)

            def split(g):
                if g < G_END:
                    split_at(g, 0, 0, row_tiles(g), 0)

            def low_half(n, dst_k, c, src):
                pool.wait_ge(hi_ready, n + 1)
                nc.gpsimd.tensor_tensor(hl[:, dst_k, cols(c)], src, hh[:, dst_k, cols(c)].bitcast(F),
                                        ALU.subtract).then_inc(lo_ready, 1)

            def norm_lows(hi0):
                for c in range(NC):
                    for k in range(KT):
                        low_half(hi0 + KT * c + k, k, c, htmp[(KT * c + k) % NH][:])

            def setup():
                nc.gpsimd.memset(ones[:], 1.0).then_inc(ones_ready, 1)
                pool.wait_ge(ones_ready, 1)
                nc.gpsimd.affine_select(out=ident[:], in_=ones[:], compare_op=ALU.is_equal, fill=0.0, base=0,
                                        pattern=[[-1, P]], channel_multiplier=1).then_inc(ident_ready, 1)
                order(nc.gpsimd.memset(causal[:], 0.0))
                nc.gpsimd.affine_select(out=masks[:], in_=causal[:, 0:NS], compare_op=ALU.is_equal, fill=NEG, base=0,
                                        pattern=[[-1, NS]], channel_multiplier=1).then_inc(masks_ready, 1)
                pool.wait_ge(masks_ready, 1)
                nc.gpsimd.affine_select(out=causal[:], in_=causal[:], compare_op=ALU.is_ge, fill=NEG, base=0,
                                        pattern=[[-1, P]], channel_multiplier=1).then_inc(masks_ready, 1)
                split(0)
                split(1)
                norm_lows(HI_MIX)

            def mixer():
                with nc.gpsimd.Fori(0, HEADS // 2) as i:
                    for u in range(14):
                        split_at(G_IN + 2, i, u, KT, 14)

            def out_proj():
                for c in range(NC):
                    for k in range(KT):
                        low_half(HI_OUT + KT * c + k, k, c, xT[:, k, cols(c)])
                with nc.gpsimd.Fori(0, KT // 2) as i:
                    for u in range(2):
                        split_at(G_OUT + 2, i, u, KT, 2)

            def ffn(l, g0, hi0):
                norm_lows(hi0)
                g = g0
                for f0, n in FFN_CHUNKS:
                    def turn(i, splits):
                        splits(0)
                        for c in range(NC):
                            pool.wait_ge(ahi_ready, 3 * i + 3 * (FT * l + f0) + c + 1)
                            d = one(alo[:, bass.ds(i, 1), cols(c)])
                            nc.gpsimd.tensor_tensor(d, atmp[c][:], one(ahi[:, bass.ds(i, 1), cols(c)]).bitcast(F),
                                                    ALU.subtract).then_inc(alo_ready, 1)
                        splits(1)
                    with nc.gpsimd.Fori(0, n - 1) as i:
                        turn(i, lambda u: split_at(g + 2, i, u, KT, 2))
                    turn(n - 1, lambda u: split(g + 2 * n + u))
                    g += 2 * n
                    with nc.gpsimd.Fori(0, KT // 2 - 1) as i:
                        for u in range(2):
                            split_at(g + 2, i, u, n, 2)
                    g += KT
                    split(g)
                    split(g + 1)

            def latents():
                norm_lows(HI_LAT)
                for u in range(2, 6):
                    split(G_LAT + u)
                for c in range(NC):
                    for k in range(QT):
                        low_half(HI_CQ + QT * c + k, k, c, lt[(QT * c + k) % 2][:])
                for c in range(NC):
                    for k in range(CT):
                        low_half(HI_CKV + CT * c + k, QT + k, c, ckv32[:, k, cols(c)])

            def decode():
                pool.wait_ge(ptab_loaded, 16)
                pool.wait_ge(wt_ready, MH)
                with nc.gpsimd.Fori(0, NS) as n:
                    for j in range(PAGES):
                        if j % PG == 0:
                            pool.wait_ge(page_used, (PAGES // PG) * n + j // PG + 1)
                        if j % PG in SP_ROPE:
                            continue
                        page = pool.value_load(ptab[0:1, bass.ds(n * PAGES + j, 1)], min_val=0, max_val=cache_krope.shape[1] - 1)
                        pool.dma_start(pages[:, j, CT * P:PW], cache_krope[0, bass.ds(page, 1)].rearrange("o p c -> p (o c)")
                                       ).then_inc(prope_loaded[j // PG], 16)
                    pool.wait_ge(mx_ready, n + 1)
                    pool.sem_inc(pool_turn, 1)
                    nc.gpsimd.partition_all_reduce(mxa[:], mx[:], P, RMAX).then_inc(mxa_ready, 1)
                split(G_PAIR)
                split(G_PAIR + 1)

            def pairs():
                def turn(r, last):
                    for u in range(2, PAIR_SLOTS):
                        split_at(G_PAIR, r, u, row_tiles(G_PAIR + u), PAIR_SLOTS)
                    for u in range(2):
                        if last:
                            split(G_FFN1 + u)
                        else:
                            split_at(G_PAIR, r, PAIR_SLOTS + u, QT, PAIR_SLOTS)
                with nc.gpsimd.Fori(0, PAIRS - 1) as r:
                    turn(r, False)
                turn(PAIRS - 1, True)

            pool.sem_inc(w_split, 2)
            pool.sem_inc(alo_ready, NC)
            phases = [setup, mixer, out_proj, lambda: ffn(0, G_FFN0, HI_FFN0), latents, lambda: None, decode, pairs,
                      lambda: ffn(1, G_FFN1, HI_FFN1), lambda: None]
            for phase in phases:
                phase()

        @block.scalar
        def _(act):
            def high(dst, src, ready=hi_ready):
                nc.scalar.copy(dst, src).then_inc(ready, 1)

            def norm(inst, src, ready, scale, highs):
                nk = NORMS[inst]
                for c in range(NC):
                    ready(c)
                    for k in range(nk):
                        m = nk * c + k
                        act.wait_ge(sq_used, SQ_BASE[inst] + m + 1)
                        nc.scalar.activation(sq[(SQ_BASE[inst] + m) % 2][:], src(k, c), ACT.Square).then_inc(sq_ready, 1)
                    act.wait_ge(ss_ready, NC * inst + c + 1)
                    if NC * inst + c > 0:
                        act.wait_ge(rs_ready, NC * inst + c)
                    nc.scalar.activation(rt[:], bank[7][:, 0:CW], ACT.Sqrt, bias=EPS, scale=scale).then_inc(rt_ready, 1)
                    if c > 0:
                        highs(c - 1)
                highs(NC - 1)

            def model_norm(inst, ht0, ready):
                def highs(c):
                    for k in range(KT):
                        act.wait_ge(ht_ready, ht0 + KT * c + k + 1)
                        high(hh[:, k, cols(c)], htmp[(KT * c + k) % NH][:])
                norm(inst, lambda k, c: xT[:, k, cols(c)], ready, 1.0 / D, highs)

            def ada_rows(a, b):
                act.wait_ge(ada_used, a + 1 + 2)
                act.wait_ge(ada_back, a + 1)
                nc.scalar.copy(adar[:], bank[4 + b][:, 0:AW]).then_inc(ada_copied, 1)

            def updated(g):
                return lambda c: act.wait_ge(bank_free[c], g + 1)

            def setup():
                for k in range(KT):
                    act.wait_ge(xt_bank, 2 * k + 2)
                    nc.scalar.copy(xT[:, k, T // 2:T], bank[(2 * k + 1) % 6]).then_inc(xt_act, 1)
                act.wait_ge(vec_ready, 2)
                nc.scalar.activation(siluc[:].rearrange("p k n -> p n k"), cT, ACT.Silu).then_inc(siluc_ready, 1)
                for a in range(ADA_MIX):
                    ada_rows(a, a % 2)
                act.wait_ge(xt_dve, 9)
                model_norm(0, 0, lambda c: None)

            def mixer():
                act.wait_ge(x_saved, 16)
                with nc.scalar.Fori(0, HEADS // 2) as i:
                    for e in range(2):
                        h = i * 2 + e
                        def filled(u, c):
                            act.wait_ge(bank_ready[c], 14 * i + G_IN + 7 * e + u + 1 + READY0[c])
                        act.wait_ge(o_taken, h + 1)
                        for c in range(NC):
                            filled(SLOT_F, c)
                            nc.scalar.activation(hf[:, cols(c)], bank[c][:, 0:CW], ACT.Sigmoid)
                            nc.scalar.activation(hk[:, cols(c)], bank[c][:, 0:CW], ACT.Sigmoid, scale=-1.0).then_inc(bank_free[c], 1)
                        for c in range(NC):
                            filled(SLOT_Q, c)
                            nc.scalar.activation(hq[:, cols(c)], bank[c][:, 0:CW], ACT.Sigmoid).then_inc(qsig_ready, 1)
                        for c in range(NC):
                            filled(SLOT_V, c)
                            nc.scalar.copy(hv[:, cols(c)], bank[c][:, 0:CW]).then_inc(bank_free[c], 1)

                        def tokens(task, dst):
                            act.wait_ge(wk_ready, 8 * h + task + 1)
                            nc.scalar.copy(dst, bank[5].rearrange("p (b k) -> p b k", b=4)).then_inc(wk_free, 1)

                        for c in range(NC):
                            filled(SLOT_CG, c)
                            nc.scalar.copy(ug[:, 2 + c * CW:2 + (c + 1) * CW], bank[c][:, 0:CW]).then_inc(bank_free[c], 1)
                            if c < 2:
                                tokens(c, vtok[:, 4 * c:4 * c + 4, :])
                        tokens(2, ktok[:, 0:4, :])
                        tokens(3, ktok[:, 4:8, :])
                        for c in range(NC):
                            filled(SLOT_G, c)
                            nc.scalar.activation(one(xT[:, bass.ds(h + HEADS, 1), cols(c)]), bank[c][:, 0:CW],
                                                 ACT.Sigmoid).then_inc(gsig_ready, 1)
                            if c == 0:
                                act.wait_ge(s_new, h + 1)
                                act.dma_start(hgrn_sample[0].rearrange("n h k v -> k n h v")[:, :, bass.ds(h, 1), :]
                                              .rearrange("k n o v -> k n (o v)"), s0[:]).then_inc(so_saved, 16)
                        act.wait_ge(st_ready, h + 1)
                        act.dma_start(hgrn_prompt[0, 0, bass.ds(h, 1)].rearrange("o k v -> k (o v)"),
                                      st[:, NCH, :]).then_inc(st_saved, 16)
                        act.wait_ge(oacc_ready, h + 1)
                        def square(c):
                            nc.scalar.activation(sq[c % 2][:], oacc[:, cols(c)], ACT.Square).then_inc(hsq_ready, 1)
                        def root(c):
                            act.wait_ge(bc_ready[(15 + c) % 2], 9 * h + (15 + c) // 2 + 1)
                            act.wait_ge(hrs_ready, NC * h + c + 1)
                            nc.scalar.activation(rt[:], bank[6 + (15 + c) % 2][:, 0:CW], ACT.Sqrt, bias=EPS,
                                                 scale=1.0 / P).then_inc(hrt_ready, 1)
                            act.wait_ge(hrt_ready, NC * h + c + 1)
                            act.sem_inc(bc_free[(15 + c) % 2], 1)
                        square(0)
                        square(1)
                        root(0)
                        square(2)
                        root(1)
                        root(2)

            def out_proj():
                act.wait_ge(bank_ready[NC - 1], G_OUT + READY0[NC - 1])
                act.wait_ge(y_ready, HEADS)
                for c in range(NC):
                    for k in range(KT):
                        high(hh[:, k, cols(c)], xT[:, k, cols(c)])
                with nc.scalar.Fori(1, KT // 2) as i:
                    for u in range(4):
                        ada_rows(4 * i + ADA_MIX - 4 + u, u % 2)

            def ffn(l, g0, inst, ht0):
                model_norm(inst, ht0, updated(g0))
                g = g0
                for f0, n in FFN_CHUNKS:
                    act.wait_ge(bank_ready[NC - 1], g + READY0[NC - 1])
                    with_ada = l == 0 and f0 < ADA_LAYER // 2
                    with nc.scalar.Fori(0, n) as i:
                        m0 = i * 3 + 3 * (FT * l + f0)
                        for c in range(NC):
                            act.wait_ge(bank_ready[c], 2 * i + g + 1 + READY0[c])
                            act.wait_ge(act_ready, m0 + c + 1)
                            nc.scalar.activation(sil[c][:], bank[c][:, 0:CW], ACT.Silu).then_inc(bank_free[c], 1)
                            if c == 0 and with_ada:
                                ada_rows(2 * i + 2 * f0 + ADA_LAYER, 0)
                        if with_ada:
                            ada_rows(2 * i + 2 * f0 + 1 + ADA_LAYER, 1)
                        for c in range(NC):
                            act.wait_ge(act_ready, m0 + c + 1 + NC)
                            high(one(ahi[:, bass.ds(i, 1), cols(c)]), atmp[c][:], ahi_ready)
                    g += 2 * n + KT

            def swap_halves(dst, src, n, done):
                for j in range(n):
                    ins = nc.scalar.copy(dst[(j ^ 1) * HR:((j ^ 1) + 1) * HR], src[j * HR:(j + 1) * HR])
                ins.then_inc(done, 1)

            def latents():
                model_norm(2, 48, updated(G_LAT))
                for u in range(QT + CT):
                    for c in range(NC):
                        act.wait_ge(bank_ready[c], G_LAT + u + 1 + READY0[c])
                        nc.scalar.copy(craw[:, u, cols(c)], bank[c][:, 0:CW]).then_inc(bank_free[c], 1)
                for c in range(NC):
                    act.wait_ge(bank_ready[c], G_LAT + 5 + 1 + READY0[c])
                    swap_halves(sw[c][0:ROPE, :], bank[c][0:ROPE, 0:CW], 2, sw_ready)
                act.wait_ge(kr_ready, NC)
                nc.scalar.copy(kr[ROPE:P, :], kr[0:ROPE, :]).then_inc(kr2_ready, 1)

                def cq_highs(c):
                    for k in range(QT):
                        act.wait_ge(ht_ready, 72 + QT * c + k + 1)
                        high(hh[:, k, cols(c)], lt[(QT * c + k) % 2][:])

                def ckv_highs(c):
                    for k in range(CT):
                        act.wait_ge(ht_ready, 81 + CT * c + k + 1)
                        high(hh[:, QT + k, cols(c)], ckv32[:, k, cols(c)])
                norm(3, lambda k, c: craw[:, k, cols(c)], lambda c: act.wait_ge(bank_free[c], G_LAT + QT + CT + 1), 1.0 / (QT * P), cq_highs)
                norm(4, lambda k, c: craw[:, QT + k, cols(c)], lambda c: None, 1.0 / (CT * P), ckv_highs)

            def tokens_out():
                for i in range(TB + 1):
                    b, rows = i % 2, P if i < TB else NS
                    act.wait_ge(tk_ready, i + 1)
                    act.wait_ge(tk_saved[b], 32 * (i // 2) + 32)
                    nc.scalar.copy(ctok[b][0:rows, :], bank[3 + b][0:rows, 0:PW]).then_inc(tk_taken, 1)

            def decode():
                act.wait_ge(qs_ready, 1)
                swap_halves(qsw[:], bank[1][0:ROPE, 0:MH * NS].rearrange("p (h n) -> p h n", h=MH), 2, qs_sw)
                with nc.scalar.Fori(0, NS) as n:
                    def keys_out(m):
                        b = 2 * m % KB
                        act.wait_ge(kt_bank[b], n * (PAGES // KB) + m // 2 + 1)
                        act.wait_ge(sc_bank, n * UN + m + 1)
                        nc.scalar.copy(ktp[m % 2][:, :, 0:P], bank[KT_BANKS[b]][:, 0:3 * P].rearrange("p (k m) -> p k m", k=3)
                                       ).then_inc(kt_out[b], 1)
                    keys_out(0)
                    for m in range(UN):
                        if m + 1 < UN:
                            keys_out(m + 1)
                        if m % 2 == 0:
                            continue
                        q = m // 2
                        act.wait_ge(sc_bank, n * UN + m + 1 + 2)
                        act.wait_ge(sc_back, n * QN + q + 1)
                        w = P if q < QN - 1 else 2 * P
                        nc.scalar.copy(sct[q % 2][:, 0:w], bank[SC_BANKS[q % 2]][:, 0:w]).then_inc(sc_out, 1)
                    act.wait_ge(pse_ready, n + 1 + 1)
                    nc.scalar.activation(pex[:], pse[:], ACT.Exp, scale=MLA_SCALE).then_inc(pex_ready, 1)

            def pairs():
                with nc.scalar.Fori(0, PAIRS) as r:
                    g = r * PAIR_SLOTS + G_PAIR
                    def out_of(u, c, dst, src=None):
                        act.wait_ge(bank_ready[c], g + u + 1 + READY0[c])
                        nc.scalar.copy(dst, bank[c][:, 0:CW]).then_inc(bank_free[c], 1)
                    act.wait_ge(bank_free[NC - 1], g + 1)
                    for e in range(2):
                        for c in range(NC):
                            out_of(e, c, qn[:, e, cols(c)])
                    for c in range(NC):
                        act.wait_ge(bank_ready[c], g + 2 + 1 + READY0[c])
                        act.wait_ge(sw_used, r * NC + c + 1)
                        swap_halves(sw[c][:], bank[c][:, 0:CW], 4, sw_ready)
                    for e in range(2):
                        for c in range(NC):
                            out_of(3 + e, c, kn[:, e, cols(c)])
                    u0 = r * (2 * TB)

                    def probs(u):
                        w = (u // 2 + 1) * P
                        act.wait_ge(nb_ready, u0 + u + 1)
                        act.wait_ge(p_used, u0 + u + 1)
                        nc.scalar.activation(pp[u % 2][:, 0:w], sbank[u % 2][:, 0:w], ACT.Exp, bias=amx[u % 2][:, 1:2],
                                             scale=MLA_SCALE, accum_out=amx[u % 2][:, 2:3]).then_inc(p_ready, 1)

                    def output(u):
                        e, q = u % 2, u // 2
                        act.wait_ge(ao_ready, u0 + u + 1 + 2)
                        high(hh[:, O0 + e, q * P:(q + 1) * P], bank[e][:, 0:P], oh_ready)

                    probs(0)
                    for u in range(2 * TB):
                        if u + 1 < 2 * TB:
                            probs(u + 1)
                        if u // 2 >= 4:
                            act.wait_ge(pt_bank[1], r * TB + (u - 8) + 1)
                            act.wait_ge(ao_ready, u0 + u + 1)
                            w = u // 2 + 1 - 4
                            nc.scalar.copy(pt[u % 2][:, 4:4 + w, :], bank[7][:, 0:w * P].rearrange("p (b q) -> p b q", b=w)
                                           ).then_inc(pt_out[1], 1)
                        if u > 0:
                            output(u - 1)
                    output(2 * TB - 1)
                    for e in range(2):
                        high(hh[:, O0 + e, T:N], one(os32[:, bass.ds(2 * r + e, 1), :]), oh_ready)

            def final():
                model_norm_no_split()
                act.wait_ge(conv_bank, 1)
                nc.scalar.copy(crow[:], bank[0][0:72, 0:P]).then_inc(conv_out, 1)
                for i in range(TB + 1):
                    b, rows = i % 2, P if i < TB else NS
                    act.wait_ge(yt_bank[1], i + 1)
                    act.wait_ge(yt_saved[b], 16 * (i // 2) + 16)
                    nc.scalar.copy(ytok[b][0:rows, 512:D], bank[4 + 2 * b][0:rows, :]).then_inc(yt_out[b], 1)

            def model_norm_no_split():
                norm(6, lambda k, c: xT[:, k, cols(c)], updated(G_END), 1.0 / D, lambda c: None)

            act.sem_inc(bank_free[0], 1)
            act.sem_inc(bank_free[1], 1)
            act.sem_inc(bank_free[2], 1)
            act.sem_inc(wk_free, 1)
            act.sem_inc(sc_out, 2)
            act.sem_inc(ada_copied, 2)
            act.sem_inc(p_ready, 2)
            act.sem_inc(pt_out[1], 1)
            phases = [setup, mixer, out_proj, lambda: ffn(0, G_FFN0, 1, 24), latents, tokens_out, decode, pairs,
                      lambda: ffn(1, G_FFN1, 5, 87), final]
            for phase in phases:
                phase()

        @block.vector
        def _(dve):
            v = nc.vector
            order = InOrder(dve, dve_order)

            def inverse_root(ready, n, done):
                dve.wait_ge(ready, n)
                v.reciprocal(rs[:], rt[:]).then_inc(done, 1)

            def model_norm(inst, ht0, hi0, which):
                l, s = divmod(which, 2)
                a, shift = amp[:, which], mod[:, l, 24 * s:24 * s + KT]
                for c in range(NC):
                    inverse_root(rt_ready, NC * inst + c + 1, rs_ready)
                    dve.wait_ge(rs_ready, NC * inst + c + 1)
                    w = CW if c < NC - 1 else LASTP
                    for k in range(KT):
                        m = KT * c + k
                        h = htmp[m % NH]
                        if m >= NH:
                            dve.wait_ge(lo_ready, hi0 + m - NH + 1)
                        order(v.tensor_tensor(h[:], xT[:, k, cols(c)], rs[:], ALU.mult))
                        if c == NC - 1:
                            order(v.tensor_tensor(h[:, w:CW], h[:, w:CW], a[:, k, 1:1 + NS], ALU.mult))
                            order.put(v.tensor_tensor(h[:, w:CW], h[:, w:CW], shift[:, k, 1:1 + NS], ALU.add))
                        v.tensor_scalar(h[:, 0:w], h[:, 0:w], a[:, k, 0:1], shift[:, k, 0:1], ALU.mult, ALU.add
                                        ).then_inc(ht_ready, 1)

            def add_to_x(c, m, gate, src, turn, order=order):
                w = CW if c < NC - 1 else LASTP
                if c == NC - 1:
                    order(v.tensor_tensor(gtmp[:], src[:, w:CW], one(gate[:, bass.ds(m, 1), 1:1 + NS]), ALU.mult))
                xc = one(xT[:, bass.ds(m, 1), c * CW:c * CW + w])
                ins = v.scalar_tensor_tensor(xc, src[:, 0:w], one(gate[:, bass.ds(m, 1), 0:1]), xc, ALU.mult, ALU.add)
                if c == NC - 1:
                    order.put(ins)
                    xs = one(xT[:, bass.ds(m, 1), T:N])
                    ins = v.tensor_tensor(xs, xs, gtmp[:], ALU.add)
                    ins.then_inc(bank_free[c], 1)
                    dve.wait_ge(bank_free[c], turn + 1)
                else:
                    ins.then_inc(bank_free[c], 1)

            def modulation(group, l, first, end, norms):
                dve.wait_ge(ada_bank, group + 1)
                order(v.tensor_tensor(mod[:, l, first:end], bank[6][:, first * 9:end * 9].rearrange("p (i n) -> p i n", n=9),
                                      b_adaT[:, l, first:end].unsqueeze(2).to_broadcast([P, end - first, 9]), ALU.add))
                for s in norms:
                    order(v.scalar_tensor_tensor(amp[:, 2 * l + s], mod[:, l, 24 * s + KT:24 * s + 2 * KT], 1.0,
                                                 gT[:, s, l, :].unsqueeze(2).to_broadcast([P, KT, 9]), ALU.add, ALU.mult))
                dve.sem_inc(mod_ready, 1)

            def setup():
                for n, dst, src in ((0, vec0[:], bank[6][:, 0:P]), (1, vec1[:], bank[6][:, P:P + 98]),
                                    (2, cconv[:], bank[6][:, 256:320].rearrange("p (n w j) -> p n w j", n=NS, w=2))):
                    dve.wait_ge(vec_bank, n + 1)
                    v.tensor_copy(dst, src).then_inc(vec_ready, 1)
                for k in range(KT):
                    dve.wait_ge(xt_bank, 2 * k + 1)
                    v.tensor_copy(xT[:, k, 0:T // 2], bank[(2 * k) % 6]).then_inc(xt_dve, 1)
                dve.wait_ge(xt_bank, 2 * KT + 1)
                v.tensor_copy(xT[:, :, T:N], bank[7][:, 0:KT * NS].rearrange("p (k n) -> p k n", k=KT)).then_inc(xt_dve, 1)
                dve.wait_ge(ident_ready, 1)
                order(v.tensor_copy(sel[:], ident[:, 0:1 + NS]))
                for g in range(1, CG):
                    ins = v.tensor_tensor(sel[:], sel[:], ident[:, g * GC:g * GC + 1 + NS], ALU.add)
                    if g == CG - 1:
                        ins.then_inc(sel_ready, 1)
                    else:
                        order(ins)
                modulation(0, 0, 0, 2 * KT, (0,))
                model_norm(0, 0, HI_MIX, 0)
                modulation(1, 0, 2 * KT, 3 * KT, ())

            def mixer():
                dve.wait_ge(x_saved, 16)
                order.put(v.memset(ug[:, 0:2], 0.0))
                order.put(v.tensor_copy(cout[:, 1:1 + NS, 0, :], cconv[:, :, 1, :]))
                with nc.vector.Fori(0, HEADS // 2) as i:
                    order.enter(i, 2 * ORDER_HEAD)
                    for e in range(2):
                        head(i, e)
                    order.leave(HEADS // 2)

            def blocks(t, first=0, n=NBL):
                return t[:, first * BL:(first + n) * BL].rearrange("p (b t) -> p b t", t=BL)

            def head(i, e):
                h = i * 2 + e
                n0 = order.n
                def filled(u, c):
                    dve.wait_ge(bank_ready[c], 14 * i + G_IN + 7 * e + u + 1 + READY0[c])
                def evacuated(u, c):
                    dve.wait_ge(bank_free[c], 14 * i + G_IN + 7 * e + u + 1 + 1)
                yc, yo = xT[:, bass.ds(h, 1), :], xT[:, bass.ds(h + HEADS, 1), :]

                order.put(v.memset(ki[0][:], 0.0))
                order(v.memset(ki[1][:], 0.0))
                for c in range(NC):
                    evacuated(SLOT_F, c)
                fv, kv, qv, vvw = (blocks(t) for t in (hf, hk, hq, hv))
                pf, kb = blocks(qb), blocks(k1)
                order(v.tensor_copy(pf[:, :, 0], fv[:, :, 0]))
                order(v.memset(kb[:, :, BL - 1], 1.0))
                for t in range(1, BL):
                    order.put(v.tensor_tensor(pf[:, :, t], pf[:, :, t - 1], fv[:, :, t], ALU.mult))
                    order(v.tensor_tensor(kb[:, :, BL - 1 - t], kb[:, :, BL - t], fv[:, :, BL - t], ALU.mult))
                order(v.tensor_copy(fb[:], pf[:, :, BL - 1]))
                fc, cc = fb[:].rearrange("p (c b) -> p c b", b=CB), cp[:].rearrange("p (c b) -> p c b", b=CB)
                order(v.memset(cc[:, :, 0], 1.0))
                for t in range(1, CB):
                    order(v.tensor_tensor(cc[:, :, t], cc[:, :, t - 1], fc[:, :, t - 1], ALU.mult))
                order(v.tensor_tensor(ftot[:], cc[:, :, CB - 1], fc[:, :, CB - 1], ALU.mult))
                order(v.tensor_tensor(k1[:], k1[:], hk[:, 0:T], ALU.mult))
                for c in range(NC):
                    dve.wait_ge(qsig_ready, NC * h + c + 1)
                    v.scalar_tensor_tensor(hq[:, cols(c)], bank[c][:, 0:CW], P ** -0.5, hq[:, cols(c)], ALU.mult, ALU.mult
                                           ).then_inc(bank_free[c], 1)
                for c in range(NC):
                    evacuated(SLOT_Q, c)
                order(v.tensor_tensor(qb[:], qb[:], hq[:, 0:T], ALU.mult))

                kiv = [t[:].rearrange("p (c s) -> p c s", c=NCH) for t in ki]
                k1v = k1[:].rearrange("p (c s) -> p c s", c=NCH)

                def keys(b):
                    if b > 2:
                        dve.wait_ge(ki_used, 7 * h + b - 2)
                    if b > 1:
                        w = (b - 1) * BL
                        order.put(v.tensor_tensor(kiv[b % 2][:, :, 0:w], kiv[(b - 1) % 2][:, :, 0:w],
                                              fc[:, :, b - 1].unsqueeze(2).to_broadcast([P, NCH, w]), ALU.mult))
                    v.tensor_copy(kiv[b % 2][:, :, (b - 1) * BL:b * BL], k1v[:, :, (b - 1) * BL:b * BL]).then_inc(ki_ready, 1)
                    dve.wait_ge(ki_ready, 8 * h + b)

                def product(n):
                    d, first, nb = PIECES[n]
                    if first == 0:
                        if d == 0:
                            order(v.tensor_copy(mq[:], hq[:, 0:T]))
                        else:
                            dve.wait_ge(e_ready, 12 * h + n)
                            m = blocks(mq)
                            order(v.tensor_tensor(m[:, :, d:BL], m[:, :, d:BL], fv[:, :, 1:BL - d + 1], ALU.mult))
                    w = BL - d
                    v.tensor_tensor(ed[n % 2][:, 0:nb * w].rearrange("p (b t) -> p b t", t=w), blocks(mq, first, nb)[:, :, d:BL],
                                    blocks(hk, first, nb)[:, :, 0:w], ALU.mult).then_inc(e_ready, 1)

                def weigh(n):
                    d, first, nb = PIECES[n]
                    w = BL - d
                    dve.wait_ge(bc_ready[n % 2], 9 * h + n // 2 + 1)
                    src = bank[6 + n % 2][:, 0:nb * w].rearrange("p (b t) -> p b t", t=w)
                    o = blocks(oacc, first, nb)[:, :, d:BL]
                    val = blocks(hv, first, nb)[:, :, 0:w]
                    if d == 0:
                        v.tensor_tensor(o, src, val, ALU.mult).then_inc(bc_free[n % 2], 1)
                        dve.wait_ge(bc_free[n % 2], 9 * h + n // 2 + 2)
                    else:
                        t = dtmp[:, 0:nb * w].rearrange("p (b t) -> p b t", t=w)
                        v.tensor_tensor(t, src, val, ALU.mult).then_inc(bc_free[n % 2], 1)
                        dve.wait_ge(bc_free[n % 2], 9 * h + n // 2 + 2)
                        order(v.tensor_tensor(o, o, t, ALU.add))

                def conv_input(c):
                    filled(SLOT_XV, c)
                    u = ug[:, 2 + c * CW:2 + (c + 1) * CW]
                    v.tensor_tensor(u, bank[c][:, 0:CW], u, ALU.mult).then_inc(bank_free[c], 1)

                def gated_conv(c):
                    filled(SLOT_BG, c)
                    y = one(yc[:, :, cols(c)])
                    v.tensor_tensor(y, bank[c][:, 0:CW], y, ALU.mult).then_inc(bank_free[c], 1)

                def out_gate(c):
                    dve.wait_ge(gsig_ready, NC * h + c + 1)
                    y = one(yo[:, :, cols(c)])
                    v.tensor_tensor(y, bank[c][:, 0:CW], y, ALU.mult).then_inc(bank_free[c], 1)

                def states(n):
                    dve.wait_ge(wk_ready, 8 * h + 4 + n + 1)
                    for q in range(4):
                        c = 4 * n + q
                        src = bank[5][:, q * P:(q + 1) * P]
                        if c == NCH - 1:
                            dve.wait_ge(st_saved, 16 * h + 16)
                        if c == 0:
                            ins = v.tensor_copy(st[:, 1, :], src)
                        else:
                            ins = v.scalar_tensor_tensor(st[:, c + 1, :], st[:, c, :], ftot[:, c:c + 1], src, ALU.mult, ALU.add)
                        if q == 3:
                            ins.then_inc(wk_free, 1)
                            dve.wait_ge(wk_free, 8 * h + 4 + n + 2)
                        else:
                            order(ins)

                def sample_states(n):
                    dve.wait_ge(bc_ready[n], 9 * h + 6 + 1)
                    t = k1[:, n * 512:(n + 1) * 512].rearrange("p (n v) -> p n v", n=4)
                    v.tensor_tensor(t, bank[6 + n].rearrange("p (n v) -> p n v", n=4),
                                    hk[:, T + 4 * n:T + 4 * n + 4].unsqueeze(2).to_broadcast([P, 4, P]), ALU.mult
                                    ).then_inc(bc_free[n], 1)
                    dve.wait_ge(bc_free[n], 9 * h + 6 + 2)
                    s = s0[:, 4 * n:4 * n + 4, :]
                    order(v.tensor_tensor(s, s, t, ALU.add))

                keys(1)
                keys(2)
                product(0)
                product(1)
                for c in range(NC):
                    evacuated(SLOT_V, c)
                for n in range(0, 12, 2):
                    keys(n // 2 + 3)
                    if n >= 6:
                        conv_input((n - 6) // 2)
                    weigh(n)
                    weigh(n + 1)
                    if n + 2 < 12:
                        product(n + 2)
                        product(n + 3)
                dve.wait_ge(e_ready, 12 * h + 12)
                order(v.memset(mq[:], 0.0))
                dve.wait_ge(a_ready, h + 1)
                for half in range(2):
                    rows = slice(CH * half, CH * half + CH)
                    v.tensor_copy(am[rows, :, CH * half + BL:CH * half + CH],
                                  w34[rows, 0:512].rearrange("p (c t) -> p c t", t=CH)[:, :, BL:CH]).then_inc(a_taken, 1)
                v.tensor_tensor(blocks(qb), blocks(qb), cp[:].unsqueeze(2).to_broadcast([P, NBL, BL]), ALU.mult).then_inc(qe_ready, 1)
                dg = ki[1][:].rearrange("p (n v) -> p n v", n=NS)
                v.tensor_tensor(dg, ident[:].unsqueeze(1).to_broadcast([P, NS, P]),
                                hv[:, T:N].unsqueeze(2).to_broadcast([P, NS, P]), ALU.mult).then_inc(dv_ready, 1)
                for c in range(NC):
                    evacuated(SLOT_XV, c)
                wc = [convT[:, w, bass.ds(h, 1)] for w in range(3)]
                y = one(yc[:, :, 0:T])
                order(v.tensor_scalar(y, ug[:, 2:2 + T], wc[2], None, ALU.mult))
                order(v.scalar_tensor_tensor(y, ug[:, 1:1 + T], wc[1], y, ALU.mult, ALU.add))
                order(v.scalar_tensor_tensor(y, ug[:, 0:T], wc[0], y, ALU.mult, ALU.add))
                y = one(yc[:, :, T:N])
                order(v.tensor_scalar(y, ug[:, 2 + T:2 + N], wc[2], None, ALU.mult))
                for w in range(2):
                    order(v.scalar_tensor_tensor(y, cconv[:, :, w, bass.ds(h, 1)].rearrange("p n o -> p (n o)"), wc[w], y,
                                                 ALU.mult, ALU.add))
                order.put(v.tensor_copy(cout[:, 0, :, bass.ds(h, 1)], ug[:, T:2 + T].unsqueeze(2)))
                order.put(v.tensor_copy(cout[:, 1:1 + NS, 1, bass.ds(h, 1)], ug[:, 2 + T:2 + N].unsqueeze(2)))
                gated_conv(0)
                dve.wait_ge(s0_loaded, 16 * h + 16)
                order(v.tensor_tensor(s0[:], s0[:], hf[:, T:N].unsqueeze(2).to_broadcast([P, NS, P]), ALU.mult))
                sample_states(0)
                sample_states(1)
                dve.sem_inc(s_new, 1)
                gated_conv(1)
                states(0)
                gated_conv(2)
                states(1)
                out_gate(0)
                states(2)
                dve.wait_ge(bc_ready[0], 9 * h + 7 + 1)
                v.tensor_copy(oacc[:, T:N], bank[6][:, 0:NS]).then_inc(bc_free[0], 1)
                out_gate(1)
                states(3)
                dve.sem_inc(st_ready, 1)
                out_gate(2)
                dve.wait_ge(o_ready, h + 1)
                dve.wait_ge(bc_free[0], 9 * h + 7 + 2)
                order.put(v.tensor_tensor(oacc[:, 0:512], w34[:, 0:512], oacc[:, 0:512], ALU.add))
                v.tensor_tensor(oacc[:, 512:T], w34[:, 512:T], oacc[:, 512:T], ALU.add).then_inc(o_taken, 1)
                dve.wait_ge(o_taken, h + 2)
                dve.sem_inc(oacc_ready, 1)
                for c in range(NC):
                    inverse_root(hrt_ready, NC * h + c + 1, hrs_ready)
                    dve.wait_ge(hrs_ready, NC * h + c + 2)
                    evacuated(SLOT_G, c)
                    order(v.scalar_tensor_tensor(oacc[:, cols(c)], oacc[:, cols(c)], gnT, rs[:], ALU.mult, ALU.mult))
                    y = one(yo[:, :, cols(c)])
                    ins = v.tensor_tensor(y, y, oacc[:, cols(c)], ALU.mult)
                    if c == NC - 1:
                        ins.then_inc(y_ready, 1)
                    else:
                        order.put(ins)
                assert order.n - n0 == ORDER_HEAD, order.n - n0

            def out_proj():
                dve.wait_ge(x_back, 16)
                dve.wait_ge(st_saved, 16 * HEADS + 16)
                dve.wait_ge(so_saved, 16 * HEADS + 16)
                residual_slots(G_OUT, 2 * KT, 0)

            def residual_slots(g, gate_at, l):
                with nc.vector.Fori(0, KT // 2) as i:
                    order.enter(i, 4)
                    for b in range(2):
                        for c in range(NC):
                            s = 2 * i + b + g
                            dve.wait_ge(bank_ready[c], s + 1 + READY0[c])
                            add_to_x(c, 2 * i + b, mod[:, l, gate_at:gate_at + KT, :], bank[c], s + 1)
                    order.leave(KT // 2)

            def ffn(l, g0, inst, ht0, hi0):
                if l == 0:
                    modulation(2, 0, 3 * KT, 6 * KT, (1,))
                model_norm(inst, ht0, hi0, 2 * l + 1)
                g = g0
                for f0, n in FFN_CHUNKS:
                    with nc.vector.Fori(0, n) as i:
                        m0 = i * 3 + 3 * (FT * l + f0)
                        for c in range(NC):
                            dve.wait_ge(bank_free[c], 2 * i + g + 1 + 1)
                            dve.wait_ge(bank_ready[c], 2 * i + g + 2 + READY0[c])
                            dve.wait_ge(alo_ready, m0 + c + 1)
                            v.tensor_tensor(atmp[c][:], sil[c][:], bank[c][:, 0:CW], ALU.mult).then_inc(act_ready, 1)
                            dve.wait_ge(act_ready, m0 + c + 1 + NC)
                            dve.sem_inc(bank_free[c], 1)
                    g += 2 * n
                    residual_slots(g, 5 * KT, l)
                    g += KT

            def rope(dst, c, src, rows, done, turn):
                s = sw[c][0:rows, :]
                order(v.tensor_tensor(s, s, rsn[0:rows, cols(c)], ALU.mult))
                v.tensor_tensor(dst, src, rc[0:rows, cols(c)], ALU.mult).then_inc(bank_free[c], 1)
                dve.wait_ge(bank_free[c], turn + 1)
                v.tensor_tensor(dst, dst, s, ALU.add).then_inc(done, 1)

            def latents():
                modulation(3, 1, 0, 6 * KT, (0, 1))
                model_norm(2, 48, HI_LAT, 2)
                dve.wait_ge(rope_loaded, 32)
                for c in range(NC):
                    dve.wait_ge(sw_ready, c + 1)
                    rope(kr[0:ROPE, cols(c)], c, bank[c][0:ROPE, 0:CW], ROPE, kr_ready, G_LAT + 6)
                for inst, nk, k0, g, ht0, hi0 in ((3, QT, 0, qnT, 72, HI_CQ), (4, CT, QT, kvnT, 81, HI_CKV)):
                    for c in range(NC):
                        dve.wait_ge(ht_ready, ht0 + nk * c)
                        inverse_root(rt_ready, NC * inst + c + 1, rs_ready)
                        dve.wait_ge(rs_ready, NC * inst + c + 1)
                        for k in range(nk):
                            m = nk * c + k
                            if inst == 3:
                                dst = lt[m % 2][:]
                                if m >= 2:
                                    dve.wait_ge(lo_ready, hi0 + m - 1)
                            else:
                                dst = ckv32[:, k, cols(c)]
                            ins = v.scalar_tensor_tensor(dst, craw[:, k0 + k, cols(c)], g[:, k:k + 1], rs[:], ALU.mult, ALU.mult)
                            ins.then_inc(ht_ready, 1)
                            if inst == 3 and c == NC - 1:
                                dve.wait_ge(ht_ready, ht0 + m + 1)
                                order.put(v.tensor_copy(cqs[:, k, :], dst[:, LASTP:CW]))

            def tokens_out():
                order.put(v.memset(ktn[:], 0.0))
                order(v.memset(knew[:], 0.0))
                dve.wait_ge(ht_ready, 87)
                dve.wait_ge(kr_ready, NC)
                order.put(v.tensor_copy(ktn[:, 0:CT, 0:NS], ckv32[:, :, T:N]))
                order.put(v.tensor_copy(ktn[0:ROPE, CT, 0:NS], kr[0:ROPE, T:N]))
                dve.wait_ge(tk_taken, TB + 1)
                v.tensor_copy(knew[0:NS, :], ctok[0][0:NS, 0:CT * P]).then_inc(knew_ready, 1)

            def decode():
                order.wait()
                order(v.memset(qall[:], 0.0))
                for b in (6,) + SC_BANKS:
                    order(v.memset(bank[b][:, 0:2 * P], 0.0))
                dve.wait_ge(qs_ready, 1)
                order.put(v.tensor_copy(qns[:], bank[0][:, 0:MH * NS].rearrange("p (h n) -> p h n", h=MH)))
                dve.wait_ge(qs_sw, 1)
                q = qall[0:ROPE, CT].rearrange("p n h -> p h n")
                order(v.tensor_scalar(qsw[:], qsw[:], rsn[0:ROPE, T:T + 1], None, ALU.mult))
                v.scalar_tensor_tensor(q, bank[1][0:ROPE, 0:MH * NS].rearrange("p (h n) -> p h n", h=MH), rc[0:ROPE, T:T + 1],
                                       qsw[:], ALU.mult, ALU.add).then_inc(qs_taken, 1)
                for h in range(MH):
                    dve.wait_ge(wt_ready, h + 1)
                    if h > 0:
                        dve.wait_ge(ql_ready, h)
                    v.tensor_copy(wukt[:], bank[3 + h % 2][:, 0:CT * P]).then_inc(wt_taken, 1)
                dve.wait_ge(ql_ready, MH)
                for ct in range(CT):
                    ins = v.tensor_copy(qall[:, ct].rearrange("p n h -> p h n"),
                                        bank[5 + ct][:, 0:MH * NS].rearrange("p (h n) -> p h n", h=MH))
                    ins.then_inc(ql_taken, 1)
                with nc.vector.Fori(0, NS) as n:
                    order.enter(n, ORDER_SEQ)
                    dve.wait_ge(ql_taken, CT)
                    dve.wait_ge(sc_bank, n * UN + 2)
                    v.tensor_copy(qcur[:], qall[:, :, bass.ds(n, 1), :].rearrange("p k o h -> p k (o h)")).then_inc(q_ready, 1)
                    for m in range(UN):
                        b = (2 * m + 1) % KB
                        dve.wait_ge(kt_bank[b], n * (PAGES // KB) + m // 2 + 1)
                        dve.wait_ge(sc_bank, n * UN + m + 1)
                        v.tensor_copy(ktp[m % 2][:, :, P:2 * P], bank[KT_BANKS[b]][:, 0:3 * P].rearrange("p (k m) -> p k m", k=3)
                                      ).then_inc(kt_out[b], 1)
                    dve.wait_ge(ds_ready, n + 1)
                    sc = bank[5][:, 0:(PAGES + 1) * MH].rearrange("p (j h) -> p j h", h=MH)
                    order(v.tensor_scalar(sc[:, PAGES, :], sc[:, PAGES, :], masks[:, bass.ds(n, 1)], None, ALU.add))
                    v.tensor_reduce(mx[:], bank[5][:, 0:(PAGES + 1) * MH].rearrange("p (j h) -> p h j", h=MH), axis=AX.X,
                                    op=ALU.max).then_inc(mx_ready, 1)
                    dve.wait_ge(mxa_ready, n + 1)
                    v.tensor_tensor(pse[:], sc, mxa[:].unsqueeze(1).to_broadcast([P, PAGES + 1, MH]), ALU.subtract
                                    ).then_inc(pse_ready, 1)
                    dve.wait_ge(pex_ready, n + 1)
                    v.tensor_reduce(den[:], pex[:].rearrange("p j h -> p h j"), axis=AX.X, op=ALU.add).then_inc(den_ready, 1)
                    dve.wait_ge(den_sum, n + 1)
                    order(v.reciprocal(rden[:], bank[6][:, CT * P:CT * P + MH]))
                    v.tensor_copy(ctx8[:], bank[6][:, 0:CT * P]).then_inc(c8_ready, 1)
                    dve.wait_ge(ct_bank, n + 1)
                    v.tensor_tensor(ctxs[:, :, :, bass.ds(n, 1)].rearrange("p k h o -> p k (h o)"),
                                    bank[6][:, CT * P + MH:CT * P + 3 * MH].rearrange("p (k h) -> p k h", k=CT),
                                    rden[:].unsqueeze(1).to_broadcast([P, CT, MH]), ALU.mult).then_inc(ctx_taken, 1)
                    order.leave(NS)
                dve.wait_ge(os_ready, 1)
                v.tensor_copy(os32[:], bank[1][:, 0:MH * NS].rearrange("p (h n) -> p h n", h=MH)).then_inc(os_taken, 1)

            def pairs():
                with nc.vector.Fori(0, PAIRS) as r:
                    order.enter(r, ORDER_PAIR)
                    g = r * PAIR_SLOTS + G_PAIR
                    for c in range(NC):
                        dve.wait_ge(sw_ready, r * NC + NC + c + 1)
                        rope(qr[:, cols(c)], c, bank[c][:, 0:CW], P, sw_used, g + 3)
                    for c in range(NC):
                        dve.wait_ge(bank_ready[c], g + 5 + 1 + READY0[c])
                        v.tensor_copy(vv[:, 2 * c:2 * c + 2, :], bank[c].rearrange("p (b m) -> p b m", b=2)).then_inc(bank_free[c], 1)
                    dve.wait_ge(vx_ready, r + 1)
                    v.tensor_copy(vv[:, 6:8, :], bank[7].rearrange("p (b m) -> p b m", b=2)).then_inc(vx_taken, 1)
                    u0 = r * (2 * TB)

                    def maxima(u):
                        q, s = u // 2, sbank[u % 2]
                        dve.wait_ge(sc_ready, u0 + u + 1)
                        diag = s[:, q * P:(q + 1) * P]
                        order(v.tensor_tensor(diag, diag, causal[:], ALU.add))
                        order(v.reduce_max(amx[u % 2][:, 0:1], s[:, 0:(q + 1) * P], axis=AX.X))
                        v.tensor_scalar(amx[u % 2][:, 1:2], amx[u % 2][:, 0:1], -MLA_SCALE, None, ALU.mult).then_inc(nb_ready, 1)

                    def low_output(u):
                        e, q = u % 2, u // 2
                        dve.wait_ge(oh_ready, r * (2 * TB + 2) + u + 1)
                        v.tensor_tensor(hl[:, O0 + e, q * P:(q + 1) * P], bank[e][:, 0:P],
                                        hh[:, O0 + e, q * P:(q + 1) * P].bitcast(F), ALU.subtract).then_inc(ol_ready, 1)

                    maxima(0)
                    for u in range(2 * TB):
                        q = u // 2
                        dve.wait_ge(p_ready, u0 + u + 1 + 2)
                        order(v.reciprocal(amx[u % 2][:, 3:4], amx[u % 2][:, 2:3]))
                        p = pp[u % 2][:, 0:(q + 1) * P]
                        v.tensor_scalar(p, p, amx[u % 2][:, 3:4], None, ALU.mult).then_inc(pn_ready, 1)
                        if u + 1 < 2 * TB:
                            maxima(u + 1)
                        dve.wait_ge(pt_bank[0], u0 + u + 1)
                        dve.wait_ge(ao_ready, u0 + u + 1)
                        w = min(q + 1, 4)
                        v.tensor_copy(pt[u % 2][:, 0:w, :], bank[2][:, 0:w * P].rearrange("p (b q) -> p b q", b=w)
                                      ).then_inc(pt_out[0], 1)
                        if u > 0:
                            low_output(u - 1)
                    low_output(2 * TB - 1)
                    for e in range(2):
                        dve.wait_ge(oh_ready, r * (2 * TB + 2) + 2 * TB + e + 1)
                        v.tensor_tensor(hl[:, O0 + e, T:N], one(os32[:, bass.ds(2 * r + e, 1), :]),
                                        hh[:, O0 + e, T:N].bitcast(F), ALU.subtract).then_inc(ol_ready, 1)
                    with nc.vector.Fori(0, KT // 2) as i:
                        inner = InOrder(dve, x_order)
                        inner.base = (r * (KT // 2) + i) * 4
                        for b in range(2):
                            for c in range(NC):
                                s = g + 2 * i + 6 + b
                                dve.wait_ge(bank_ready[c], s + 1 + READY0[c])
                                add_to_x(c, 2 * i + b, mod[:, 1, 2 * KT:3 * KT, :], bank[c], s + 1, inner)
                    order.leave(PAIRS)

            def final():
                for c in range(NC):
                    if c > 0:
                        dve.wait_ge(f_ready, KT * c)
                    inverse_root(rt_ready, NC * 6 + c + 1, rs_ready)
                    dve.wait_ge(rs_ready, NC * 6 + c + 1)
                    for k in range(KT):
                        x = xT[:, k, cols(c)]
                        v.scalar_tensor_tensor(x, x, finT[:, k:k + 1], rs[:], ALU.mult, ALU.mult).then_inc(f_ready, 1)
                for i in range(TB + 1):
                    b, rows = i % 2, P if i < TB else NS
                    dve.wait_ge(yt_bank[0], i + 1)
                    dve.wait_ge(yt_saved[b], 16 * (i // 2) + 16)
                    v.tensor_copy(ytok[b][0:rows, 0:512], bank[3 + 2 * b][0:rows, :]).then_inc(yt_out[b], 1)

            dve.sem_inc(act_ready, NC)
            dve.sem_inc(o_taken, 1)
            dve.sem_inc(hrs_ready, 1)
            dve.sem_inc(pse_ready, 1)
            dve.sem_inc(ctx_taken, 1)
            dve.sem_inc(sw_used, NC)
            dve.sem_inc(ol_ready, 2)
            for b in range(2):
                dve.sem_inc(bc_free[b], 1)
            dve.sem_inc(pt_out[0], 1)
            phases = [setup, mixer, out_proj, lambda: ffn(0, G_FFN0, 1, 24, HI_FFN0), latents, tokens_out, decode, pairs,
                      lambda: ffn(1, G_FFN1, 5, 87, HI_FFN1), final]
            for phase in phases:
                phase()

        @block.tensor
        def _(pe):
            mm = nc.tensor.matmul

            def three(out, wh_, wl_, xh_, xl_, start, stop):
                mm(out, wh_, xh_, start=start, stop=False)
                mm(out, wh_, xl_, start=False, stop=False)
                return mm(out, wl_, xh_, start=False, stop=stop)

            def slot(g, b, nk, hi, lo, ready=None, after=None, rows=P):
                pe.wait_ge(w_split, g + 1 + 2)
                for c in range(NC):
                    if ready:
                        ready(c)
                    pe.wait_ge(bank_free[c], g + 1)
                    for k in range(nk):
                        last = three(bank[c][0:rows, 0:CW], whi[b][:, k, 0:rows], wlo[b][:, k, 0:rows], hi[:, k, cols(c)],
                                     lo[:, k, cols(c)], k == 0, k == nk - 1)
                    last.then_inc(bank_ready[c], 1)
                    if after:
                        after(c)

            def sums(inst):
                nk = NORMS[inst]
                for c in range(NC):
                    if NC * inst + c > 0:
                        pe.wait_ge(rt_ready, NC * inst + c)
                    for k in range(nk):
                        m = SQ_BASE[inst] + nk * c + k
                        pe.wait_ge(sq_ready, m + 1)
                        mm(bank[7][:, 0:CW], ones[:], sq[m % 2][:], start=k == 0, stop=k == nk - 1).then_inc(sq_used, 1)
                    pe.wait_ge(sq_used, SQ_BASE[inst] + nk * (c + 1) + 2)
                    pe.sem_inc(ss_ready, 1)

            def lows_ready(hi0, nk):
                return lambda c: pe.wait_ge(lo_ready, hi0 + nk * (c + 1))

            def ada(a, i, b, l=0):
                pe.wait_ge(ada_loaded[b], 16 * i + 16 * (ADA_LAYER // 2) * l + 16)
                pe.wait_ge(ada_copied, a + ADA_LAYER * l + 1)
                for k in range(KT):
                    rows = slice(k % CG * GC, k % CG * GC + 1 + NS)
                    ins = mm(bank[4 + b][rows, 0:AW], siluc[:, k, :], adaw[b][:, k, :], start=k < CG, stop=k >= KT - CG)
                    if k >= KT - CG:
                        ins.then_inc(ada_part, 1)
                pe.wait_ge(ada_part, CG * (a + ADA_LAYER * l + 1))
                pe.sem_inc(ada_used, 1)

            def ada_turned(a, i, b, l=0):
                pe.wait_ge(ada_copied, a + ADA_LAYER * l + 1 + 2)
                pe.sem_inc(pe_turn, 1)
                for q in range(AW // P):
                    ins = mm(bank[6][:, bass.ds(i * 36 + (2 * b + q) * 9, 9)], adar[:, q * P:(q + 1) * P], sel[:],
                             start=True, stop=True)
                ins.then_inc(ada_back, 1)

            def ada_done(n):
                pe.wait_ge(ada_back, n + 1)
                pe.sem_inc(ada_bank, 1)

            def ada_units(first, end):
                for a in range(first, end):
                    ada(a, a // 2, a % 2)
                    if a > first:
                        ada_turned(a - 1, (a - 1) // 2, (a - 1) % 2)
                ada_turned(end - 1, (end - 1) // 2, (end - 1) % 2)
                ada_done(end)

            def setup():
                pe.wait_ge(ident_ready, 1)
                pe.wait_ge(vecs_loaded, 16 * 11)
                for dst, src, n in ((bank[6][:, 0:P], rows0, P), (bank[6][:, P:P + 98], rows1, 98), (bank[6][:, 256:320], rows2, 64)):
                    ins = nc.tensor.transpose(dst, src[:], ident[0:n, 0:n])
                ins.then_inc(vec_bank, 3)
                pe.wait_ge(x_loaded, 16 * (TB + 1))
                for k in range(KT):
                    for half in range(2):
                        n = 2 * k + half
                        if n >= 6:
                            pe.wait_ge(xt_act if half else xt_dve, (n - 6) // 2 + 1)
                        for q in range(4):
                            ins = nc.tensor.transpose(bank[n % 6][:, q * P:(q + 1) * P], xtok[:, 4 * half + q, k * P:(k + 1) * P], ident[:])
                        ins.then_inc(xt_bank, 1)
                for k in range(KT):
                    ins = nc.tensor.transpose(bank[7][:, k * NS:(k + 1) * NS], xstok[:, k * P:(k + 1) * P], ident[0:NS, 0:NS])
                ins.then_inc(xt_bank, 1)
                pe.wait_ge(siluc_ready, 1)
                pe.wait_ge(vec_ready, 3)
                pe.wait_ge(xt_dve, KT + 1)
                pe.wait_ge(xt_act, KT)
                pe.wait_ge(sel_ready, 1)
                ada_units(0, ADA_SHIFT_SCALE)
                pe.wait_ge(mod_ready, 1)
                ada_units(ADA_SHIFT_SCALE, ADA_MIX)
                sums(0)

            def mixer():
                with nc.tensor.Fori(0, HEADS // 2) as i:
                    for e in range(2):
                        head(i, e)

            def head(i, e):
                h = i * 2 + e

                def attend(b):
                    pe.wait_ge(ki_ready, 8 * h + b)
                    if b == 1:
                        pe.wait_ge(o_taken, h + 1)
                    for c in range(NCH):
                        ins = mm(w34[CH * (c % 2):CH * (c % 2) + CH, (c // 2) * CH + b * BL:(c // 2) * CH + (b + 1) * BL],
                                 ki[b % 2][:, c * CH:(c + 1) * CH], qb[:, c * CH + b * BL:c * CH + (b + 1) * BL],
                                 start=True, stop=True)
                    ins.then_inc(ki_used, 1)
                    if b == CB - 1:
                        pe.wait_ge(ki_used, 7 * h + 7)
                        pe.sem_inc(a_ready, 1)

                def transposes(task, src):
                    pe.wait_ge(wk_free, 8 * h + task + 1)
                    if task == 0:
                        for c in range(NC):
                            pe.wait_ge(bank_free[c], 14 * i + G_IN + 7 * e + SLOT_V + 1 + 1)
                    if task == 2:
                        pe.wait_ge(ki_ready, 8 * h + 8)
                    for q in range(4):
                        t = (4 * (task % 2) + q) * P
                        ins = nc.tensor.transpose(bank[5][:, q * P:(q + 1) * P], src[:, t:t + P], ident[:])
                    ins.then_inc(wk_ready, 1)

                def broadcast(n):
                    d, _, nb = PIECES[n]
                    w = nb * (BL - d)
                    pe.wait_ge(bc_free[n % 2], 9 * h + n // 2 + 1)
                    pe.wait_ge(e_ready, 12 * h + n + 1)
                    mm(bank[6 + n % 2][:, 0:w], ones[:], ed[n % 2][:, 0:w], start=True, stop=True).then_inc(bc_ready[n % 2], 1)

                def sample_values(n):
                    pe.wait_ge(bc_free[n], 9 * h + 6 + 1)
                    pe.wait_ge(dv_ready, h + 1)
                    mm(bank[6 + n][:], ones[:], ki[1][:, n * 512:(n + 1) * 512], start=True, stop=True).then_inc(bc_ready[n], 1)

                def outer(n):
                    pe.wait_ge(wk_free, 8 * h + 4 + n + 1)
                    for q in (0, 2, 1, 3):
                        c = 4 * n + q
                        rows = slice(CH * (c % 2), CH * (c % 2) + CH)
                        if q == 1:
                            ins.then_inc(wk_half, 1)
                            pe.wait_ge(wk_half, 4 * h + n + 1)
                        ins = mm(bank[5][:, q * P:(q + 1) * P], ktok[rows, c // 2, :], vtok[rows, c // 2, :], start=True, stop=True)
                    ins.then_inc(wk_ready, 1)

                def sample_outputs():
                    pe.wait_ge(bc_free[0], 9 * h + 7 + 1)
                    pe.wait_ge(s_new, h + 1)
                    for n in range(NS):
                        ins = mm(bank[6][:, n:n + 1], s0[:, n, :], hq[:, T + n:T + n + 1], start=True, stop=True)
                    ins.then_inc(bc_ready[0], 1)

                def outputs():
                    pe.wait_ge(a_taken, 2 * h + 2)
                    pe.wait_ge(qe_ready, h + 1)
                    pe.wait_ge(st_ready, h + 1)
                    for c in range(NCH):
                        if c % 2 == 0:
                            mm(w34[:, c * CH:(c + 2) * CH], vtok[:, c // 2, :], am[:, c // 2, :], start=True, stop=False)
                        if c > 0:
                            ins = mm(w34[:, c * CH:(c + 1) * CH], st[:, c, :], qb[:, c * CH:(c + 1) * CH],
                                     start=False, stop=c % 2 == 1)
                    ins.then_inc(o_ready, 1)

                def head_sums(c):
                    b, n = (15 + c) % 2, 9 * h + (15 + c) // 2
                    pe.wait_ge(bc_free[b], n + 1)
                    pe.wait_ge(hsq_ready, NC * h + c + 1)
                    mm(bank[6 + b][:, 0:CW], ones[:], sq[c % 2][:], start=True, stop=True).then_inc(bc_ready[b], 1)

                steps = {(SLOT_V, 1): [lambda: attend(1)], (SLOT_V, 2): [lambda: attend(2)],
                         (SLOT_CG, 0): [lambda: attend(3), lambda: transposes(0, hv), lambda: broadcast(0), lambda: broadcast(1)],
                         (SLOT_CG, 1): [lambda: attend(4), lambda: transposes(1, hv), lambda: broadcast(2), lambda: broadcast(3)],
                         (SLOT_CG, 2): [lambda: attend(5), lambda: broadcast(4), lambda: broadcast(5)],
                         (SLOT_XV, 0): [lambda: attend(6), lambda: broadcast(6), lambda: broadcast(7)],
                         (SLOT_XV, 1): [lambda: attend(7), lambda: broadcast(8), lambda: broadcast(9)],
                         (SLOT_XV, 2): [lambda: broadcast(10), lambda: broadcast(11)],
                         (SLOT_BG, 0): [lambda: transposes(2, ki[0]), lambda: sample_values(0), lambda: sample_values(1)],
                         (SLOT_BG, 1): [lambda: transposes(3, ki[0]), lambda: outer(0)],
                         (SLOT_BG, 2): [lambda: outer(1)],
                         (SLOT_G, 0): [lambda: outer(2), sample_outputs],
                         (SLOT_G, 1): [lambda: outer(3)],
                         (SLOT_G, 2): [outputs, lambda: head_sums(0), lambda: head_sums(1), lambda: head_sums(2)]}
                for u in range(7):
                    def after(c):
                        for step in steps.get((u, c), ()):
                            step()
                    slot(14 * i + G_IN + 7 * e + u, (7 * e + u) % 2, KT, hh, hl, lows_ready(HI_MIX, KT), after)

            def out_proj():
                for b in range(2):
                    slot(G_OUT + b, b, KT, hh, hl, lows_ready(HI_OUT, KT))
                with nc.tensor.Fori(1, KT // 2) as i:
                    for b in range(2):
                        j = 2 * i + (ADA_MIX - 4) // 2 + b
                        def after(c):
                            if c > 0:
                                ada_turned(2 * j + c - 1, j, c - 1)
                            if c < 2:
                                ada(2 * j + c, j, c)
                        slot(2 * i + G_OUT + b, b, KT, hh, hl, lows_ready(HI_OUT, KT), after)
                ada_done(ADA_LAYER)

            def slots(g, n, nk, hi, lo, ready=None, after=None):
                with nc.tensor.Fori(0, n // 2) as i:
                    for b in range(2):
                        slot(2 * i + g + b, b, nk, hi, lo, ready, (lambda c: after(i, b, c)) if after else None)

            def ffn(l, g0, hi0, inst):
                sums(inst)
                g = g0
                for f0, n in FFN_CHUNKS:
                    def with_ada(i, b, c):
                        if c == 0:
                            ada(2 * i + 2 * f0 + b, i + f0, b, 1)
                        if c == 2:
                            ada_turned(2 * i + 2 * f0 + b, i + f0, b, 1)
                    slots(g, 2 * n, KT, hh, hl, lows_ready(hi0, KT), with_ada if l == 0 and f0 < ADA_LAYER // 2 else None)
                    g += 2 * n
                    slots(g, KT, n, ahi, alo, lambda c: pe.wait_ge(alo_ready, NC * (FT * l + f0 + n - 1) + c + 1 + NC))
                    g += KT

            def latents():
                ada_done(2 * ADA_LAYER)
                sums(2)
                for u in range(6):
                    slot(G_LAT + u, u % 2, KT, hh, hl, lows_ready(HI_LAT, KT), rows=P if u < 5 else ROPE)
                sums(3)
                sums(4)

            def tokens_out():
                pe.wait_ge(ht_ready, 87)
                pe.wait_ge(kr_ready, NC)
                for i in range(TB + 1):
                    b = i % 2
                    ts, rows = (slice(i * P, (i + 1) * P), P) if i < TB else (slice(T, N), NS)
                    if i >= 2:
                        pe.wait_ge(tk_taken, i - 1)
                    for ct in range(CT):
                        nc.tensor.transpose(bank[3 + b][0:rows, ct * P:(ct + 1) * P], ckv32[:, ct, ts], ident[:])
                    nc.tensor.transpose(bank[3 + b][0:rows, CT * P:PW], kr[0:ROPE, ts], ident[0:ROPE, 0:ROPE]).then_inc(tk_ready, 1)

            def decode():
                pe.wait_ge(wuq_loaded, 16)
                for c in range(NC):
                    pe.wait_ge(bank_free[c], G_PAIR + 1)
                for h in range(MH):
                    for part, w in ((0, P), (1, ROPE)):
                        for k in range(QT):
                            at = h * (P + ROPE) + part * P
                            ins = mm(bank[part][0:w, h * NS:(h + 1) * NS], wuqw[:, k, at:at + w], cqs[:, k, :],
                                     start=k == 0, stop=k == QT - 1)
                ins.then_inc(qs_ready, 1)
                pe.wait_ge(wuk_loaded, 16)
                pe.wait_ge(tk_taken, TB + 1)
                pe.wait_ge(qs_taken, 1)

                def latent_query(h):
                    pe.wait_ge(wt_taken, h + 1)
                    for ct in range(CT):
                        ins = mm(bank[5 + ct][:, h * NS:(h + 1) * NS], wukt[:, ct * P:(ct + 1) * P], qns[:, h, :], start=True, stop=True)
                    ins.then_inc(ql_ready, 1)
                for h in range(MH):
                    for ct in range(CT):
                        ins = nc.tensor.transpose(bank[3 + h % 2][:, ct * P:(ct + 1) * P], wukw[:, ct, h * P:(h + 1) * P], ident[:])
                    ins.then_inc(wt_ready, 1)
                    latent_query(h)
                pe.wait_ge(ql_taken, CT)
                pe.wait_ge(knew_ready, 1)
                with nc.tensor.Fori(0, NS) as n:
                    def turned(j):
                        b = j % KB
                        if j % PG == 0:
                            by_sp, by_pool = 16 * (PG + len(SP_ROPE)), 16 * (PG - len(SP_ROPE))
                            pe.wait_ge(page_loaded[j // PG], by_sp * n + by_sp)
                            pe.wait_ge(prope_loaded[j // PG], by_pool * n + by_pool)
                        pe.wait_ge(kt_out[b], n * (PAGES // KB) + j // KB + 1)
                        for ct in range(CT):
                            nc.tensor.transpose(bank[KT_BANKS[b]][:, ct * P:(ct + 1) * P], pages[:, j, ct * P:(ct + 1) * P], ident[:])
                        nc.tensor.transpose(bank[KT_BANKS[b]][0:ROPE, CT * P:3 * P], pages[:, j, CT * P:PW], ident[:]).then_inc(kt_bank[b], 1)

                    def scored(m):
                        q = m // 2
                        pe.wait_ge(sc_out, n * QN + q + 1)
                        for e in range(2):
                            pe.wait_ge(kt_out[(2 * m + e) % KB], n * (PAGES // KB) + m // 2 + 1 + 1)
                        out = bank[SC_BANKS[q % 2]]
                        parts = [(2 * m + e) % CG * GC for e in range(2)]
                        for ct in range(CT + 1):
                            k = P if ct < CT else ROPE
                            for e in range(2):
                                ins = mm(out[parts[e]:parts[e] + MH, 0:P], qcur[0:k, ct, :], ktp[m % 2][0:k, ct, e * P:(e + 1) * P],
                                         start=ct == 0, stop=ct == CT)
                                if ct == CT:
                                    ins.then_inc(sc_part, 1)
                        pe.wait_ge(sc_part, 2 * UN * n + 2 * m + 2)
                        if m == UN - 1:
                            for ct in range(CT + 1):
                                k = P if ct < CT else ROPE
                                ins = mm(out[0:MH, P:2 * P], qcur[0:k, ct, :], ktn[0:k, ct, :], start=ct == 0, stop=ct == CT)
                            ins.then_inc(sc_bank, 1)
                        else:
                            pe.sem_inc(sc_bank, 1)

                    def back(q):
                        pe.wait_ge(sc_out, n * QN + q + 1 + 2)
                        pick = ident[:].rearrange("p (g r) -> p g r", g=CG)
                        ins = mm(bank[5][:, q * CG * MH:(q + 1) * CG * MH], sct[q % 2][:, 0:P], pick[:, :, 0:MH], start=True, stop=True)
                        if q == QN - 1:
                            ins = mm(bank[5][:, PAGES * MH:(PAGES + 1) * MH], sct[q % 2][:, P:2 * P], ident[:, 0:MH], start=True, stop=True)
                        ins.then_inc(sc_back, 1)

                    turned(0)
                    turned(1)
                    pe.wait_ge(q_ready, n + 1)
                    for m in range(UN):
                        if m + 1 < UN:
                            turned(2 * m + 2)
                            turned(2 * m + 3)
                        scored(m)
                        if m == 2:
                            pe.wait_ge(pse_ready, n + 1)
                        if m > 0 and m % 2 == 0:
                            back(m // 2 - 1)
                    back(QN - 1)
                    pe.wait_ge(sc_back, n * QN + QN + 2)
                    pe.sem_inc(ds_ready, 1)
                    pe.wait_ge(pex_ready, n + 1)
                    pe.wait_ge(ctx_taken, n + 1)
                    for j in range(PAGES + 1):
                        keys = pages[:, j, 0:CT * P] if j < PAGES else knew[:]
                        part = j % CG * GC
                        ins = mm(bank[6][part:part + MH, 0:CT * P], pex[:, j, :], keys, start=j < CG, stop=j > PAGES - CG)
                        if j % PG >= PG - CG or j == PAGES:
                            ins.then_inc(ctx_part, 1)
                        if j % PG == PG - 1:
                            pe.wait_ge(ctx_part, (CG * (PAGES // PG) + 1) * n + CG * (j // PG + 1))
                            pe.sem_inc(page_used, 1)
                    pe.wait_ge(ctx_part, (CG * (PAGES // PG) + 1) * n + CG * (PAGES // PG) + 1)
                    pe.wait_ge(den_ready, n + 1)
                    mm(bank[6][:, CT * P:CT * P + MH], ones[:], den[:], start=True, stop=True).then_inc(den_sum, 1)
                    pe.wait_ge(c8_ready, n + 1)
                    for ct in range(CT):
                        at = CT * P + MH + ct * MH
                        ins = mm(bank[6][:, at:at + MH], ctx8[:, ct * P:(ct + 1) * P], sel[:, 0:MH], start=True, stop=True)
                    ins.then_inc(ct_bank, 1)
                pe.wait_ge(wuv_loaded, 16)
                pe.wait_ge(ctx_taken, NS + 1)
                for h in range(MH):
                    for ct in range(CT):
                        ins = mm(bank[1][:, h * NS:(h + 1) * NS], wuvw[:, ct, h * P:(h + 1) * P], ctxs[:, ct, h, :],
                                 start=ct == 0, stop=ct == CT - 1)
                ins.then_inc(os_ready, 1)

            def pairs():
                pe.wait_ge(os_taken, 1)
                pe.wait_ge(kr2_ready, 1)
                with nc.tensor.Fori(0, PAIRS) as r:
                    g = r * PAIR_SLOTS + G_PAIR
                    for u in range(3):
                        slot(g + u, u % 2, QT, hh, hl)
                    for e in range(2):
                        slot(g + 3 + e, (3 + e) % 2, CT, hh[:, QT:QT + CT, :], hl[:, QT:QT + CT, :])
                    pe.wait_ge(w_split, g + 5 + 1 + 2)
                    wv_h, wv_l = (w[1][:, 0:2 * CT, :].rearrange("p (k e) m -> p k (e m)", k=CT) for w in (whi, wlo))
                    for c in range(NC + 1):
                        if c < NC:
                            pe.wait_ge(bank_free[c], g + 5 + 1)
                            out = bank[c]
                        else:
                            pe.wait_ge(pt_out[1], r * TB + 1)
                            out = bank[7]
                        for q in range(2):
                            keys = slice((2 * c + q) * P, (2 * c + q + 1) * P)
                            for k in range(CT):
                                ins = three(out[:, q * 2 * P:(q + 1) * 2 * P], hh[:, QT + k, keys], hl[:, QT + k, keys],
                                            wv_h[:, k, :], wv_l[:, k, :], k == 0, k == CT - 1)
                        if c == NC:
                            ins.then_inc(vx_ready, 1)
                        elif c < NC - 1:
                            ins.then_inc(bank_ready[c], 1)
                    pe.wait_ge(vx_ready, r + 1)
                    pe.sem_inc(bank_ready[NC - 1], 1)
                    for c in range(NC):
                        pe.wait_ge(bank_free[c], g + 6 + 1)
                    pe.wait_ge(vx_taken, r + 1)
                    u0 = r * (2 * TB)

                    def scores(u):
                        e, q = u % 2, u // 2
                        pe.wait_ge(p_ready, u0 + u + 1)
                        for at in range(0, (q + 1) * P, 512):
                            keys = slice(at, min(at + 512, (q + 1) * P))
                            mm(sbank[e][:, keys], qn[:, e, q * P:(q + 1) * P], kn[:, e, keys], start=True, stop=False)
                            ins = mm(sbank[e][:, keys], qr[e * ROPE:(e + 1) * ROPE, q * P:(q + 1) * P],
                                     kr[e * ROPE:(e + 1) * ROPE, keys], start=False, stop=True)
                        ins.then_inc(sc_ready, 1)

                    def turned(u):
                        q = u // 2
                        pe.wait_ge(pn_ready, u0 + u + 1)
                        for part, bk in ((0, 2), (1, 7)):
                            if q < 4 * part:
                                continue
                            if part == 0:
                                pe.wait_ge(pt_out[0], u0 + u + 1)
                            else:
                                pe.wait_ge(pt_out[1], r * TB + (u - 8) + 1)
                            for k in range(4 * part, min(q + 1, 4 * part + 4)):
                                at = (k - 4 * part) * P
                                ins = nc.tensor.transpose(bank[bk][:, at:at + P], pp[u % 2][:, k * P:(k + 1) * P], ident[:])
                            ins.then_inc(pt_bank[part], 1)
                        pe.wait_ge(pt_bank[part if q >= 4 else 0], (r * TB + (u - 8) + 1) if q >= 4 else u0 + u + 1)
                        pe.sem_inc(p_used, 1)

                    def weighed(u):
                        e, q = u % 2, u // 2
                        pe.wait_ge(pt_out[0], u0 + u + 1 + 1)
                        if q >= 4:
                            pe.wait_ge(pt_out[1], r * TB + (u - 8) + 1 + 1)
                        pe.wait_ge(ol_ready, r * (2 * TB + 2) + u + 1)
                        for k in range(q + 1):
                            ins = mm(bank[e][:, 0:P], vv[:, k, e * P:(e + 1) * P], pt[e][:, k, :], start=k == 0, stop=k == q)
                        ins.then_inc(ao_ready, 1)

                    scores(0)
                    for u in range(2 * TB):
                        if u + 1 < 2 * TB:
                            scores(u + 1)
                        turned(u)
                        if u > 0:
                            weighed(u - 1)
                    weighed(2 * TB - 1)
                    with nc.tensor.Fori(0, KT // 2) as i:
                        for b in range(2):
                            slot(g + 2 * i + 6 + b, b, 2, hh[:, O0:O0 + 2, :], hl[:, O0:O0 + 2, :],
                                 lambda c: pe.wait_ge(ol_ready, r * (2 * TB + 2) + 2 * TB + 2 + 2))

            def final():
                sums(6)
                for c in range(NC):
                    pe.wait_ge(bank_free[c], G_END + 1)
                nc.tensor.transpose(bank[0][0:72, 0:P], cout[:].rearrange("p s w j -> p (s w j)"), ident[:]).then_inc(conv_bank, 1)
                pe.wait_ge(f_ready, NC * KT)
                for i in range(TB + 1):
                    b = i % 2
                    ts, rows = (slice(i * P, (i + 1) * P), P) if i < TB else (slice(T, N), NS)
                    if i >= 2:
                        pe.wait_ge(yt_out[b], 2 * (i // 2))
                    for half in range(2):
                        for q in range(4):
                            ins = nc.tensor.transpose(bank[3 + 2 * b + half][0:rows, q * P:(q + 1) * P], xT[:, 4 * half + q, ts], ident[:])
                        ins.then_inc(yt_bank[half], 1)

            pe.sem_inc(ada_used, 2)
            pe.sem_inc(ada_back, 1)
            pe.sem_inc(sq_used, 2)
            pe.sem_inc(bank_ready[NC - 1], READY0[NC - 1])
            pe.sem_inc(page_used, PAGES // PG)
            pe.sem_inc(sc_bank, 2)
            pe.sem_inc(sc_back, 2)
            pe.sem_inc(p_used, 2)
            pe.sem_inc(ao_ready, 2)
            for b in range(KB):
                pe.sem_inc(kt_out[b], 1)
            phases = [setup, mixer, out_proj, lambda: ffn(0, G_FFN0, HI_FFN0, 1), latents, tokens_out, decode, pairs,
                      lambda: ffn(1, G_FFN1, HI_FFN1, 5), final]
            for phase in phases:
                phase()


_INS = ['x_prompt', 'x_sample', 'c_prompt', 'c_sample', 'cache_conv', 'state_hgrn', 'cache_ckv', 'cache_krope',
        'page_table', 'w_ada', 'b_ada', 'norm_mix', 'norm_ffn', 'w_in_even', 'conv_w', 'hg_gnorm', 'w_out_even',
        'w_dqkv', 'q_norm', 'w_uq', 'kv_norm', 'w_uk', 'w_uv', 'w_o', 'w_gu', 'w_down', 'norm_final']
_OUTS = [(1, T, D), (NS, 1, D), (1, 1, 2, 512), (1, 1, HEADS, P, P), (1, 1, T, CT * P), (1, 1, T, ROPE),
         (1, NS, 2, 512), (1, NS, HEADS, P, P), (1, NS, 1, CT * P), (1, NS, 1, ROPE)]


def rope_tables():
    past = PAGES * P
    pos = np.concatenate([np.arange(T), np.full(NS, past)]).astype(np.float32)
    inv = (10000.0 ** (-np.arange(HR) / HR)).astype(np.float32)
    ang = (inv[:, None] * pos[None, :]).astype(np.float32)
    cos, sin = np.cos(ang), np.sin(ang)
    return (np.ascontiguousarray(np.tile(cos, (4, 1)), np.float32),
            np.ascontiguousarray(np.concatenate([-sin, sin, -sin, sin]), np.float32))


def kernel(**inputs):
    import concourse.bacc as _bacc
    from concourse.bass_utils import run_bass_kernel_spmd as _run

    nc = _bacc.Bacc("TRN2", target_bir_lowering=False, num_devices=1)
    arrays, args = {}, []
    given = {name: np.ascontiguousarray(inputs[name]) for name in _INS}
    given["rope_cos"], given["rope_sin"] = rope_tables()
    for name, a in given.items():
        arrays[f"in_{name}"] = a
        args.append(nc.dram_tensor(f"in_{name}", a.shape, mybir.dt.from_np(a.dtype), kind="ExternalInput").ap())
    for i, shape in enumerate(_OUTS):
        args.append(nc.dram_tensor(f"out_{i}", shape, F, kind="ExternalOutput").ap())
    trunk(nc, *args)
    r = _run(nc, [arrays], core_ids=[0])
    return tuple(r.results[0][f"out_{i}"] for i in range(len(_OUTS)))
```
